# Optimizing a Trainium2 kernel written in Bass

```python
import jax, jax.numpy as jnp
from jax import lax
import numpy as np

D_MODEL = 2048
BATCH = 1
SEQ = 256
DEPTH = 2

N_EVEN = (DEPTH + 1) // 2
N_ODD = DEPTH // 2

A_HEAD_DIM = 64
A_HEADS = D_MODEL // 128
A_KV_HEADS = A_HEADS // 8
A_WIDTH = A_HEADS * A_HEAD_DIM
A_KV_WIDTH = A_KV_HEADS * A_HEAD_DIM
WINDOW = 128
A_BLOCK = 128
ROPE_THETA = 10000.0

B_HEAD_DIM = 128
B_HEADS = (D_MODEL // 2) // B_HEAD_DIM
B_WIDTH = B_HEADS * B_HEAD_DIM
B_CHUNK = 16
LB_FLOOR = 1e-30

C_HEAD_DIM = 128
C_HEADS = D_MODEL // C_HEAD_DIM
C_WIDTH = C_HEADS * C_HEAD_DIM
C_BLOCK = 128

EVEN_SPLITS = [A_WIDTH, A_KV_WIDTH, A_KV_WIDTH, A_WIDTH, B_WIDTH, B_WIDTH, B_WIDTH, B_WIDTH]
EVEN_IN = sum(EVEN_SPLITS)
EVEN_MIX = A_WIDTH + B_WIDTH
ODD_IN = 4 * C_WIDTH
EPS = 1e-6


def rmsnorm(x, w):
    xf = x.astype(jnp.float32)
    return xf * lax.rsqrt(jnp.mean(xf * xf, axis=-1, keepdims=True) + EPS) * w.astype(jnp.float32)

def rope(x, pos):
    half = x.shape[-1] // 2
    inv_freq = 1.0 / (ROPE_THETA ** (jnp.arange(half, dtype=jnp.float32) / half))
    ang = pos[:, None] * inv_freq[None, :]
    cos = jnp.cos(ang)[None, :, None, :]
    sin = jnp.sin(ang)[None, :, None, :]
    x1, x2 = x[..., :half], x[..., half:]
    return jnp.concatenate([x1 * cos - x2 * sin, x2 * cos + x1 * sin], axis=-1)

def sliding_window_attention(q, k, v, sinks):
    b_, s_ = q.shape[:2]
    nb = s_ // A_BLOCK
    g = A_HEADS // A_KV_HEADS
    qb = q.reshape(b_, nb, A_BLOCK, A_KV_HEADS, g, A_HEAD_DIM)

    def band(t):
        t = t.reshape(b_, nb, A_BLOCK, A_KV_HEADS, A_HEAD_DIM)
        prev = jnp.concatenate([jnp.zeros_like(t[:, :1]), t[:, :-1]], axis=1)
        return jnp.concatenate([prev, t], axis=2)

    kb, vb = band(k), band(v)
    scores = jnp.einsum('bnqhgd,bnkhd->bnhgqk', qb, kb) * (A_HEAD_DIM ** -0.5)
    qpos = jnp.arange(nb)[:, None] * A_BLOCK + jnp.arange(A_BLOCK)[None, :]
    kpos = jnp.arange(nb)[:, None] * A_BLOCK - A_BLOCK + jnp.arange(2 * A_BLOCK)[None, :]
    diff = qpos[:, :, None] - kpos[:, None, :]
    valid = (diff >= 0) & (diff < WINDOW) & (kpos[:, None, :] >= 0)
    scores = jnp.where(valid[None, :, None, None], scores, -1e30)
    sink = jnp.broadcast_to(sinks.astype(jnp.float32).reshape(1, 1, A_KV_HEADS, g, 1, 1),
                            scores.shape[:-1] + (1,))
    probs = jax.nn.softmax(jnp.concatenate([scores, sink], axis=-1), axis=-1)[..., :-1]
    out = jnp.einsum('bnhgqk,bnkhd->bnqhgd', probs, vb)
    return out.reshape(b_, s_, A_WIDTH)

def hgrn2_chunkwise(q, logf, k, v):
    b_, s_, h_, kd = q.shape
    vd = v.shape[-1]
    nc = s_ // B_CHUNK

    def chunks(t):
        return t.reshape(b_, nc, B_CHUNK, h_, t.shape[-1]).transpose(0, 3, 1, 2, 4)

    qc, lc, kc, vc = chunks(q), chunks(logf), chunks(k), chunks(v)
    bcum = jnp.cumsum(lc, axis=3)
    causal = jnp.tril(jnp.ones((B_CHUNK, B_CHUNK), dtype=bool))
    pair = jnp.exp(jnp.minimum(bcum[:, :, :, :, None, :] - bcum[:, :, :, None, :, :], 0.0))
    att = jnp.einsum('bhnik,bhnjk,bhnijk->bhnij', qc, kc, pair)
    att = jnp.where(causal, att, 0.0)
    o_intra = jnp.einsum('bhnij,bhnjv->bhniv', att, vc)

    blast = bcum[:, :, :, -1:]
    u = jnp.einsum('bhnjk,bhnjv->bhnkv', kc * jnp.exp(blast - bcum), vc)
    decay = jnp.exp(blast[:, :, :, 0])

    def step(state, inp):
        d, inc = inp
        return d[..., None] * state + inc, state

    s0 = jnp.zeros((b_, h_, kd, vd), jnp.float32)
    _, s_prev = lax.scan(step, s0, (decay.transpose(2, 0, 1, 3), u.transpose(2, 0, 1, 3, 4)))
    s_prev = s_prev.transpose(1, 2, 0, 3, 4)
    o_inter = jnp.einsum('bhnik,bhnkv->bhniv', qc * jnp.exp(bcum), s_prev)
    o = o_intra + o_inter
    return o.transpose(0, 2, 3, 1, 4).reshape(b_, s_, h_, vd)

def stick_breaking_attention(q, k, v):
    b_, h_, s_, d_ = q.shape
    nb = s_ // C_BLOCK
    qb = q.reshape(b_, h_, nb, C_BLOCK, d_).transpose(2, 0, 1, 3, 4)
    kpos = jnp.arange(s_)
    scale = d_ ** -0.5

    def block(args):
        c, qblk = args
        qpos = c * C_BLOCK + jnp.arange(C_BLOCK)
        z = jnp.einsum('bhqd,bhkd->bhqk', qblk, k) * scale
        before = kpos[None, :] < qpos[:, None]
        log1m = jnp.where(before, jax.nn.log_sigmoid(-z), 0.0)
        rc = lax.cumsum(log1m, axis=3, reverse=True)
        rc_excl = jnp.concatenate([rc[..., 1:], jnp.zeros_like(rc[..., :1])], axis=-1)
        w = jnp.where(before, jnp.exp(jax.nn.log_sigmoid(z) + rc_excl), 0.0)
        return jnp.einsum('bhqk,bhkd->bhqd', w, v)

    o = lax.map(block, (jnp.arange(nb), qb))
    return o.transpose(1, 0, 3, 2, 4).reshape(b_, s_, h_ * d_)

def even_layer(x, pos, ln, w_in, qn, kn, sinks, lb, gn, w_out):
    b_, s_, _ = x.shape
    h = rmsnorm(x, ln).astype(x.dtype)
    proj = h @ w_in
    idx = list(np.cumsum(EVEN_SPLITS)[:-1])
    aq, ak, av, ag, bq, bf, bi, bg = jnp.split(proj, idx, axis=-1)

    aq = rope(rmsnorm(aq.reshape(b_, s_, A_HEADS, A_HEAD_DIM), qn), pos)
    ak = rope(rmsnorm(ak.reshape(b_, s_, A_KV_HEADS, A_HEAD_DIM), kn), pos)
    av = av.reshape(b_, s_, A_KV_HEADS, A_HEAD_DIM).astype(jnp.float32)
    ya = sliding_window_attention(aq, ak, av, sinks) * jax.nn.silu(ag.astype(jnp.float32))

    lbf = lb.astype(jnp.float32)
    logf = jnp.logaddexp(jnp.log(jnp.maximum(lbf, LB_FLOOR)),
                         jnp.log1p(-lbf) + jax.nn.log_sigmoid(bf.astype(jnp.float32)))
    kin = -jnp.expm1(logf)
    shp = (b_, s_, B_HEADS, B_HEAD_DIM)
    ob = hgrn2_chunkwise(jax.nn.silu(bq.astype(jnp.float32)).reshape(shp), logf.reshape(shp),
                         kin.reshape(shp), bi.astype(jnp.float32).reshape(shp))
    yb = rmsnorm(ob, gn) * jax.nn.silu(bg.astype(jnp.float32)).reshape(shp)
    yb = yb.reshape(b_, s_, B_WIDTH)

    y = jnp.concatenate([ya, yb], axis=-1).astype(x.dtype) @ w_out
    return x + y

def odd_layer(x, ln, w_in, w_out):
    b_, s_, _ = x.shape
    h = rmsnorm(x, ln).astype(x.dtype)
    cq, ck, cv, cg = jnp.split(h @ w_in, 4, axis=-1)

    def heads(t):
        return t.reshape(b_, s_, C_HEADS, C_HEAD_DIM).transpose(0, 2, 1, 3).astype(jnp.float32)

    oc = stick_breaking_attention(heads(cq), heads(ck), heads(cv))
    y = (oc * jax.nn.silu(cg.astype(jnp.float32))).astype(x.dtype) @ w_out
    return x + y

def first_inputs(seed: int = 0) -> dict:
    key = jax.random.key(seed)
    ks = jax.random.split(key, 12)
    f32 = jnp.float32
    return {
        "x": jax.random.normal(ks[0], (BATCH, SEQ, D_MODEL), f32),
        "ln_even": 1.0 + 0.02 * jax.random.normal(ks[1], (N_EVEN, D_MODEL), f32),
        "w_in_even": jax.random.normal(ks[2], (N_EVEN, D_MODEL, EVEN_IN), f32) * D_MODEL ** -0.5,
        "q_norm_a": 1.0 + 0.02 * jax.random.normal(ks[3], (N_EVEN, A_HEAD_DIM), f32),
        "k_norm_a": 1.0 + 0.02 * jax.random.normal(ks[4], (N_EVEN, A_HEAD_DIM), f32),
        "sinks_a": jax.random.normal(ks[5], (N_EVEN, A_HEADS), f32),
        "lower_bounds": 0.5 * jax.random.normal(ks[6], (N_EVEN, B_WIDTH), f32),
        "g_norm_b": 1.0 + 0.02 * jax.random.normal(ks[7], (N_EVEN, B_HEAD_DIM), f32),
        "w_out_even": jax.random.normal(ks[8], (N_EVEN, EVEN_MIX, D_MODEL), f32) * EVEN_MIX ** -0.5,
        "ln_odd": 1.0 + 0.02 * jax.random.normal(ks[9], (N_ODD, D_MODEL), f32),
        "w_in_odd": jax.random.normal(ks[10], (N_ODD, D_MODEL, ODD_IN), f32) * D_MODEL ** -0.5,
        "w_out_odd": jax.random.normal(ks[11], (N_ODD, C_WIDTH, D_MODEL), f32) * C_WIDTH ** -0.5,
    }

def first_block(x, ln_even, w_in_even, q_norm_a, k_norm_a, sinks_a, lower_bounds, g_norm_b,
              w_out_even, ln_odd, w_in_odd, w_out_odd):
    pos = jnp.arange(x.shape[1], dtype=jnp.float32)
    lbs = jax.nn.softmax(lower_bounds.astype(jnp.float32), axis=0)
    lbs = jnp.cumsum(lbs, axis=0) - lbs[0]
    for layer in range(DEPTH):
        if layer % 2 == 0:
            e = layer // 2
            x = even_layer(x, pos, ln_even[e], w_in_even[e], q_norm_a[e], k_norm_a[e], sinks_a[e],
                           lbs[e], g_norm_b[e], w_out_even[e])
        else:
            o = layer // 2
            x = odd_layer(x, ln_odd[o], w_in_odd[o], w_out_odd[o])
    return x


DEPTH_2 = 1

CHUNK = 64
MIX_WIDTH = D_MODEL

SSD_HEAD_DIM = 64
SSD_INNER = MIX_WIDTH // 2
SSD_HEADS = SSD_INNER // SSD_HEAD_DIM
SSD_GROUPS = 2
SSD_STATE = 128
SSD_CONV = 4
SSD_CONV_DIM = SSD_INNER + 2 * SSD_GROUPS * SSD_STATE

FOX_HEAD_DIM = 64
FOX_INNER = MIX_WIDTH - SSD_INNER
FOX_HEADS = FOX_INNER // FOX_HEAD_DIM
Q_BLOCK = 128

PEER_HEADS = 8
PEER_N_KEYS = 128
PEER_N_EXPERTS = PEER_N_KEYS * PEER_N_KEYS
PEER_KEY_DIM = 256
PEER_TOPK = 16
PEER_TOKEN_BLOCK = 128

IN_SPLITS = (SSD_INNER, SSD_CONV_DIM, SSD_HEADS, FOX_INNER, FOX_INNER, FOX_INNER, FOX_HEADS)
IN_PROJ_DIM = sum(IN_SPLITS)


def rmsnorm_2(x, w):
    xf = x.astype(jnp.float32)
    xf = xf * lax.rsqrt(jnp.mean(xf * xf, axis=-1, keepdims=True) + EPS)
    return (xf * w.astype(jnp.float32)).astype(x.dtype)

def ssd_chunked(xs, dt, A, Bm, Cm):
    b, l = xs.shape[:2]
    nc = l // CHUNK
    R = SSD_HEADS // SSD_GROUPS
    x = xs.astype(jnp.float32).reshape(b, nc, CHUNK, SSD_GROUPS, R, SSD_HEAD_DIM)
    dtc = dt.reshape(b, nc, CHUNK, SSD_GROUPS, R)
    Bc = Bm.astype(jnp.float32).reshape(b, nc, CHUNK, SSD_GROUPS, SSD_STATE)
    Cc = Cm.astype(jnp.float32).reshape(b, nc, CHUNK, SSD_GROUPS, SSD_STATE)
    a = dtc * A.reshape(SSD_GROUPS, R)
    a_cum = jnp.cumsum(a, axis=2)
    xdt = x * dtc[..., None]
    seg = a_cum[:, :, :, None] - a_cum[:, :, None]
    tri = jnp.tril(jnp.ones((CHUNK, CHUNK), dtype=bool))[None, None, :, :, None, None]
    L = jnp.exp(jnp.where(tri, seg, -jnp.inf))
    cb = jnp.einsum('bctgn,bcsgn->bctsg', Cc, Bc)
    y_diag = jnp.einsum('bctsg,bctsgr,bcsgrp->bctgrp', cb, L, xdt)
    decay_states = jnp.exp(a_cum[:, :, -1:] - a_cum)
    states = jnp.einsum('bcsgn,bcsgr,bcsgrp->bcgrpn', Bc, decay_states, xdt)
    chunk_decay = jnp.exp(a_cum[:, :, -1])

    def step(h, inp):
        s_c, d_c = inp
        return h * d_c[..., None, None] + s_c, h

    h0 = jnp.zeros((b, SSD_GROUPS, R, SSD_HEAD_DIM, SSD_STATE), jnp.float32)
    _, prev = lax.scan(step, h0, (jnp.moveaxis(states, 1, 0), jnp.moveaxis(chunk_decay, 1, 0)))
    prev = jnp.moveaxis(prev, 0, 1)
    y_off = jnp.einsum('bctgn,bcgrpn,bctgr->bctgrp', Cc, prev, jnp.exp(a_cum))
    return (y_diag + y_off).reshape(b, l, SSD_HEADS, SSD_HEAD_DIM)

def ssd_group(z, xbc, dt_raw, conv_w, conv_b, dt_bias, a_log, d_skip, ssd_norm_w):
    b, l = z.shape[:2]
    xbc = lax.conv_general_dilated(
        xbc, conv_w[:, None, :], window_strides=(1,), padding=[(SSD_CONV - 1, 0)],
        dimension_numbers=('NWC', 'WIO', 'NWC'), feature_group_count=SSD_CONV_DIM) + conv_b
    xbc = jax.nn.silu(xbc)
    xs, Bm, Cm = jnp.split(xbc, [SSD_INNER, SSD_INNER + SSD_GROUPS * SSD_STATE], axis=-1)
    xs = xs.reshape(b, l, SSD_HEADS, SSD_HEAD_DIM)
    Bm = Bm.reshape(b, l, SSD_GROUPS, SSD_STATE)
    Cm = Cm.reshape(b, l, SSD_GROUPS, SSD_STATE)
    dt = jax.nn.softplus(dt_raw.astype(jnp.float32) + dt_bias.astype(jnp.float32))
    A = -jnp.exp(a_log.astype(jnp.float32))
    y = ssd_chunked(xs, dt, A, Bm, Cm)
    y = y + d_skip.astype(jnp.float32)[:, None] * xs.astype(jnp.float32)
    y = y.reshape(b, l, SSD_INNER) * jax.nn.silu(z.astype(jnp.float32))
    y = y.reshape(b, l, SSD_GROUPS, SSD_INNER // SSD_GROUPS)
    y = y * lax.rsqrt(jnp.mean(y * y, axis=-1, keepdims=True) + EPS)
    y = y.reshape(b, l, SSD_INNER) * ssd_norm_w.astype(jnp.float32)
    return y.astype(z.dtype)

def fox_group(q, k, v, f_raw, fox_f_bias):
    b, l = q.shape[:2]
    q = q.reshape(b, l, FOX_HEADS, FOX_HEAD_DIM) * (FOX_HEAD_DIM ** -0.5)
    k = k.reshape(b, l, FOX_HEADS, FOX_HEAD_DIM)
    v = v.reshape(b, l, FOX_HEADS, FOX_HEAD_DIM)
    log_f = jax.nn.log_sigmoid(f_raw.astype(jnp.float32) + fox_f_bias.astype(jnp.float32))
    cum = jnp.transpose(jnp.cumsum(log_f, axis=1), (0, 2, 1))
    outs = []
    for i in range(l // Q_BLOCK):
        qs, qe = i * Q_BLOCK, (i + 1) * Q_BLOCK
        s = jnp.einsum('bqhd,bkhd->bhqk', q[:, qs:qe], k[:, :qe]).astype(jnp.float32)
        s = s + cum[:, :, qs:qe, None] - cum[:, :, None, :qe]
        mask = (qs + jnp.arange(Q_BLOCK))[:, None] >= jnp.arange(qe)[None, :]
        p = jax.nn.softmax(jnp.where(mask, s, -jnp.inf), axis=-1)
        outs.append(jnp.einsum('bhqk,bkhd->bqhd', p.astype(v.dtype), v[:, :qe]))
    return jnp.concatenate(outs, axis=1).reshape(b, l, FOX_INNER)

def peer(h, wq, k1, k2, u, v):
    b, l, d = h.shape
    t = h.reshape(-1, d)
    T = t.shape[0]
    q = (t @ wq).reshape(T, PEER_HEADS, 2, PEER_KEY_DIM // 2)
    s1 = jnp.einsum('thd,hnd->thn', q[:, :, 0], k1).astype(jnp.float32)
    s2 = jnp.einsum('thd,hnd->thn', q[:, :, 1], k2).astype(jnp.float32)
    v1, i1 = lax.top_k(s1, PEER_TOPK)
    v2, i2 = lax.top_k(s2, PEER_TOPK)
    cand = (v1[..., :, None] + v2[..., None, :]).reshape(T, PEER_HEADS, PEER_TOPK * PEER_TOPK)
    cand_idx = (i1[..., :, None] * PEER_N_KEYS + i2[..., None, :]).reshape(T, PEER_HEADS, PEER_TOPK * PEER_TOPK)
    sc, pos = lax.top_k(cand, PEER_TOPK)
    idx = jnp.take_along_axis(cand_idx, pos, axis=-1)
    g = jax.nn.softmax(sc, axis=-1).astype(t.dtype)

    def block(args):
        tb, ib, gb = args
        act = jax.nn.gelu(jnp.einsum('thkd,td->thk', u[ib], tb), approximate=False)
        return jnp.einsum('thk,thkd->td', gb * act, v[ib])

    nb = T // PEER_TOKEN_BLOCK
    out = lax.map(block, (t.reshape(nb, PEER_TOKEN_BLOCK, d),
                          idx.reshape(nb, PEER_TOKEN_BLOCK, PEER_HEADS, PEER_TOPK),
                          g.reshape(nb, PEER_TOKEN_BLOCK, PEER_HEADS, PEER_TOPK)))
    return out.reshape(b, l, d)

def second_inputs(seed: int = 0) -> dict:
    key = jax.random.key(seed)
    ks = jax.random.split(key, 20)
    f32 = jnp.float32
    nrm = lambda k, shape: jax.random.normal(k, shape, f32)
    dt0 = jnp.exp(jax.random.uniform(ks[5], (SSD_HEADS,), f32, np.log(1e-3), np.log(1e-1)))
    return {
        "x": nrm(ks[0], (BATCH, SEQ, D_MODEL)),
        "ln1_w": 1.0 + 0.02 * nrm(ks[1], (D_MODEL,)),
        "w_in": nrm(ks[2], (D_MODEL, IN_PROJ_DIM)) * D_MODEL ** -0.5,
        "conv_w": nrm(ks[3], (SSD_CONV, SSD_CONV_DIM)) * SSD_CONV ** -0.5,
        "conv_b": 0.02 * nrm(ks[4], (SSD_CONV_DIM,)),
        "dt_bias": dt0 + jnp.log(-jnp.expm1(-dt0)),
        "a_log": jnp.log(jax.random.uniform(ks[6], (SSD_HEADS,), f32, 1.0, 16.0)),
        "d_skip": 1.0 + 0.1 * nrm(ks[7], (SSD_HEADS,)),
        "ssd_norm_w": 1.0 + 0.02 * nrm(ks[8], (SSD_INNER,)),
        "fox_f_bias": jnp.linspace(1.0, 6.0, FOX_HEADS, dtype=f32) + 0.1 * nrm(ks[9], (FOX_HEADS,)),
        "w_out": nrm(ks[10], (MIX_WIDTH, D_MODEL)) * MIX_WIDTH ** -0.5,
        "ln2_w": 1.0 + 0.02 * nrm(ks[11], (D_MODEL,)),
        "peer_wq": nrm(ks[12], (D_MODEL, PEER_HEADS * PEER_KEY_DIM)) * D_MODEL ** -0.5,
        "peer_k1": nrm(ks[13], (PEER_HEADS, PEER_N_KEYS, PEER_KEY_DIM // 2)) * (PEER_KEY_DIM // 2) ** -0.5,
        "peer_k2": nrm(ks[14], (PEER_HEADS, PEER_N_KEYS, PEER_KEY_DIM // 2)) * (PEER_KEY_DIM // 2) ** -0.5,
        "peer_u": nrm(ks[15], (PEER_N_EXPERTS, D_MODEL)) * D_MODEL ** -0.5,
        "peer_v": nrm(ks[16], (PEER_N_EXPERTS, D_MODEL)) * PEER_HEADS ** -0.5,
        "lnf_w": 1.0 + 0.02 * nrm(ks[17], (D_MODEL,)),
    }

def second_block(x, ln1_w, w_in, conv_w, conv_b, dt_bias, a_log, d_skip, ssd_norm_w,
              fox_f_bias, w_out, ln2_w, peer_wq, peer_k1, peer_k2, peer_u, peer_v, lnf_w):
    split_at = [int(s) for s in np.cumsum(IN_SPLITS)[:-1]]
    for _ in range(DEPTH_2):
        h = rmsnorm_2(x, ln1_w)
        proj = h @ w_in
        z, xbc, dt_raw, q, k, v, f_raw = jnp.split(proj, split_at, axis=-1)
        y_ssd = ssd_group(z, xbc, dt_raw, conv_w, conv_b, dt_bias, a_log, d_skip, ssd_norm_w)
        y_fox = fox_group(q, k, v, f_raw, fox_f_bias)
        x = x + jnp.concatenate([y_ssd, y_fox], axis=-1) @ w_out
        x = x + peer(rmsnorm_2(x, ln2_w), peer_wq, peer_k1, peer_k2, peer_u, peer_v)
    return rmsnorm_2(x, lnf_w)


def setup_inputs(seed=0):
    out = dict(first_inputs(seed))
    for name, value in second_inputs(seed + 1).items():
        if name != "x":
            out[name + "_2"] = value
    return out


def reference(
    x, ln_even, w_in_even, q_norm_a, k_norm_a, sinks_a, lower_bounds, g_norm_b, w_out_even,
    ln_odd, w_in_odd, w_out_odd, ln1_w_2, w_in_2, conv_w_2, conv_b_2, dt_bias_2, a_log_2,
    d_skip_2, ssd_norm_w_2, fox_f_bias_2, w_out_2, ln2_w_2, peer_wq_2, peer_k1_2, peer_k2_2,
    peer_u_2, peer_v_2, lnf_w_2,
):
    x = first_block(
        x, ln_even, w_in_even, q_norm_a, k_norm_a, sinks_a, lower_bounds, g_norm_b, w_out_even,
        ln_odd, w_in_odd, w_out_odd,
    )
    return second_block(
        x, ln1_w_2, w_in_2, conv_w_2, conv_b_2, dt_bias_2, a_log_2, d_skip_2, ssd_norm_w_2,
        fox_f_bias_2, w_out_2, ln2_w_2, peer_wq_2, peer_k1_2, peer_k2_2, peer_u_2, peer_v_2,
        lnf_w_2,
    )


_drawn_inputs = setup_inputs


def setup_inputs(seed=0):
    import zlib

    import numpy as np

    out = dict(_drawn_inputs(seed))
    spreads = {}
    factors = {'q_norm_a': 8.0,
     'k_norm_a': 8.0,
     'sinks_a': 27.459,
     'g_norm_b': 3.469,
     'ln_odd': 2.881,
     'conv_b_2': 2.722,
     'ssd_norm_w_2': 18.788,
     'ln2_w_2': 16.911,
     'lnf_w_2': 7.884,
     'ln1_w_2': 4.268}
    for name, (base, spread) in spreads.items():
        noise = np.random.default_rng([zlib.crc32(name.encode()), seed]).standard_normal(out[name].shape)
        drawn = base * np.exp(spread * noise) if base else spread * noise
        out[name] = __import__('jax').numpy.asarray(drawn.astype(out[name].dtype))
    for name, factor in factors.items():
        out[name] = (out[name] * factor).astype(out[name].dtype)
    return out
```

```python
from contextlib import ExitStack

import numpy as np

import concourse.bass as bass
from concourse import mybir

F32 = mybir.dt.float32
F32R = mybir.dt.float32r
U32 = mybir.dt.uint32
ALU = mybir.AluOpType
ACT = mybir.ActivationFunctionType
AX = mybir.AxisListType

P = 128
T = 256
MT = T // P
D = 2048
KT = D // P
NW = 512
EPS = 1e-6
NEG = -1e30
LN2 = 0.6931471805599453

A_HEADS, A_KV, A_HD = 16, 2, 64
B_HEADS, B_HD = 8, 128
C_HEADS, C_HD = 16, 128
S_HEADS, S_HD, S_STATE = 16, 64, 128
F_HEADS, F_HD = 16, 64
LEVELS = 7
PE_HEADS, PE_KEYS, PE_TOP = 8, 128, 16
HALVES = 2
EXP_ROWS = PE_KEYS // HALVES

V_LN = 0
V_SSDN = 64
V_CB = 72
V_LB = 84
V_GN = 92
V_ROWS = 93
V_CW = 93
V_COLS = V_CW + 48


def runs():
    out = []
    base = 0
    for phase, rs in (
        ("even_in", [("w_in_even", 0, 512, 2, "tok", 0), ("w_in_even", 1024, 256, 1, "tok", 2),
                     ("w_in_even", 1280, 512, 4, "silu", 3), ("w_in_even", 3328, 512, 2, "chan", 7),
                     ("w_in_even", 4352, 512, 2, "tok", 9), ("w_in_even", 5376, 512, 2, "silu", 11)]),
        ("even_out", [("w_out_even", 0, 512, 4, "res", 0)]),
        ("odd_in", [("w_in_odd", 0, 512, 4, "scaled", 0), ("w_in_odd", 2048, 512, 4, "chan", 4),
                    ("w_in_odd", 4096, 512, 4, "tok", 8), ("w_in_odd", 6144, 512, 4, "silu", 12)]),
        ("odd_out", [("w_out_odd", 0, 512, 4, "res", 0)]),
        ("two_in", [("w_in_2", 0, 512, 2, "silu", 0), ("w_in_2", 1024, 512, 3, "chan", 2),
                    ("w_in_2", 2560, 16, 1, "gate", 0), ("w_in_2", 2576, 512, 2, "eighth", 5),
                    ("w_in_2", 3600, 512, 2, "chan", 7), ("w_in_2", 4624, 512, 2, "tok", 9),
                    ("w_in_2", 5648, 16, 1, "gate", 1)]),
        ("two_out", [("w_out_2", 0, 512, 4, "res", 0)]),
        ("peer_q", [("peer_wq_2", 0, 512, 4, "chan", 0)]),
    ):
        for w, c0, width, n, kind, dest in rs:
            out.append(dict(phase=phase, w=w, c0=c0, width=width, n=n, kind=kind, dest=dest, base=base))
            base += n
    return out


RUNS = runs()
PHASES = ["even_in", "even_out", "odd_in", "odd_out", "two_in", "two_out", "peer_q"]


def last_tile(phase):
    return max(r["base"] + r["n"] for r in RUNS if r["phase"] == phase) - 1


N_TILES = last_tile("peer_q") + 1


def over_tiles(eng, phase, body):
    for r in [r for r in RUNS if r["phase"] == phase]:
        body(r, 0, r["base"] % 2, True)
        pairs = (r["n"] - 1) // 2
        if pairs > 1:
            with eng.Fori(0, pairs) as q:
                for j in range(2):
                    body(r, 2 * q + (1 + j), (r["base"] + 1 + j) % 2, False)
        else:
            for i in range(1, 1 + 2 * pairs):
                body(r, i, (r["base"] + i) % 2, False)
        for i in range(1 + 2 * pairs, r["n"]):
            body(r, i, (r["base"] + i) % 2, False)


class Chain:

    def __init__(self, eng, sem):
        self.eng, self.sem, self.n = eng, sem, 0

    def link(self, ins):
        self.n += 1
        ins.then_inc(self.sem, 1)
        self.eng.wait_ge(self.sem, self.n)


def two_blocks(nc, a, out):
    ctx = ExitStack()
    with ctx:
        def sb(name, shape, dt=F32):
            return ctx.enter_context(nc.sbuf_tensor(name, shape, dt))

        def sem(name):
            return ctx.enter_context(nc.semaphore(name))

        HH = sb("HH", [P, KT, T], F32R)
        HL = sb("HL", [P, KT, T], F32R)
        WH = sb("WH", [P, 8, NW], F32R)
        WL = sb("WL", [P, 8, NW], F32R)
        PS = sb("PS", [P, 2, 2, T], F32R)
        RAW = sb("RAW", [P, 4, 2048])
        XR = sb("XR", [P, MT, D])
        BIG = sb("BIG", [P, 16, 1024])
        WORK = sb("WORK", [P, 4096])
        YB = sb("YB", [P, 2, T])
        ID = sb("ID", [P, P])
        LE = sb("LE", [P, P])
        GT = sb("GT", [P, P])
        ONES = sb("ONES", [P, P])
        NTRI = sb("NTRI", [P, P])
        NONES = sb("NONES", [P, P])
        AMASK = sb("AMASK", [P, 384])
        FMASK = sb("FMASK", [P, 384])
        COLS = sb("COLS", [P, V_COLS])
        ROPE = sb("ROPE", [P, 2, MT, 32])
        BC = sb("BC", [P, 208])
        SM = sb("SM", [P, 160])
        DTF = sb("DTF", [P, 2, MT, 16])
        bank = [ctx.enter_context(nc.psum_tensor(f"bank{i}", [P, 512], F32)) for i in range(8)]

        names = """
            const_in vec_in masks vec_t cols_set x_in lnf_in out_done eps_set act_chain dve_chain pool_chain
            w_full0 w_full1 w_full2 w_full3 wh_done wl_done ws_used tile_free
            n_rstd n_x n_t n_h n_l y_ready y_h y_l
            aq_ready qk_t qk_c
            a_score a_soft a_exp a_rcp a_pn a_pt a_ptc a_pv
            f_score f_soft f_exp f_rcp f_pn f_pt f_ptc f_pv f_lg f_lf
            b_vec b_e b_lsg b_kin b_x b_ml b_lt b_lf b_es b_ex b_qe b_ke b_att b_am b_cross b_cx b_kx b_lev b_ov
            b_sq b_ss b_rs
            c_mask c_z c_exp c_sp c_e c_min c_w c_pv
            s_dt s_e s_a s_conv s_xbc s_xt s_xd s_cb s_cbm s_ag s_seg s_ex s_l s_y s_yg s_sq s_ss s_rs
            k_in k_t k_c q_s q_sc tk_iota tk_idx tk_e tk_g tk_t tk_tc oh1 oh_eq oh2 g_mm g_free
            u_full0 u_full1 u_full2 u_full3 u_used t_t t_h t_l a_gelu a_p
            v_full0 v_full1 v_full2 v_full3 p_h p_l v_h v_l o_mm o_add
            """.split()
        s = {n: sem(n) for n in names}

        A_QN, A_KN, A_SINK, S_DTB, S_AL, F_FB, S_DSK, S_DSKC = 0, 64, 128, 144, 160, 176, 192, 152
        DSK = SM[:, 0:8]
        bq, bf, bi, bg = BIG[:, 5:7, :], BIG[:, 7:9, :], BIG[:, 9:11, :], BIG[:, 11:13, :]
        even_spare = BIG[:, 13:16, :].rearrange("p a b -> p (a b)")
        MS = even_spare[:, 0:LEVELS * P].rearrange("p (l i) -> p l i", l=LEVELS)
        MK = even_spare[:, 896:896 + 1024].rearrange("p (l i) -> p l i", l=8)
        KX = even_spare[:, 1920:2048]
        CX = even_spare[:, 2048:2176]
        LFT = even_spare[:, 2176:2432].rearrange("p (b c) -> p b c", b=2)
        BSQ = even_spare[:, 2432:2688]
        BRS = even_spare[:, 2688:2944]
        CM = WORK[:, 3072:3456]
        CN = WORK[:, 3456:3840]

        def chan(tile0, kt):
            return BIG[:, tile0 + kt // 4, (kt % 4) * T:(kt % 4 + 1) * T]

        block = ctx.enter_context(nc.Block())

        @block.sync
        def _(sp):
            def load_tile(r, i, parity, first):
                t = r["base"] + i
                w = a[r["w"]]
                src = w.rearrange("(k p) n -> p k n", p=P)
                for j in range(4):
                    if r["base"] > 0 or not first:
                        sp.wait_ge(s["wl_done"], 8 * (t - 1) + 2 * (j + 1))
                    dst = RAW[:, j, :].rearrange("p (k n) -> p k n", k=4)[:, :, 0:r["width"]]
                    c = bass.ds(r["c0"] + i * r["width"], r["width"])
                    sp.dma_start(dst, src[:, 4 * j:4 * j + 4, c]).then_inc(s[f"w_full{j}"], 16)

            for ph in PHASES:
                over_tiles(sp, ph, load_tile)

            sp.wait_ge(s["wl_done"], 8 * N_TILES)
            keys = RAW[:, 0, :].rearrange("p (h f d) -> p h f d", h=PE_HEADS, f=2)
            for f, name in enumerate(("peer_k1_2", "peer_k2_2")):
                sp.dma_start(keys[:, :, f, :], a[name].rearrange("h n d -> n h d")).then_inc(s["k_in"], 16)

            for half in range(HALVES):
                for what, used in (("u", "t_l"), ("v", "v_l")):
                    rows = a["peer_u_2" if what == "u" else "peer_v_2"].rearrange("(i j) d -> i j d", j=PE_KEYS)
                    per = 4 if what == "u" else 1
                    tiles0 = half * EXP_ROWS

                    def load_rows(n, j, fresh):
                        if not fresh:
                            sp.wait_ge(s[used], per * (n - 3))
                        sp.dma_start(RAW[:, j, :], rows[n, :, :]).then_inc(s[f"{what}_full{j}"], 16)

                    if half == 0 and what == "u":
                        sp.wait_ge(s["k_t"], 4)
                    elif what == "u":
                        sp.wait_ge(s["v_l"], tiles0)
                    else:
                        sp.wait_ge(s["t_l"], 4 * (tiles0 + EXP_ROWS))
                    for j in range(4):
                        load_rows(tiles0 + j, j, True)
                    with sp.Fori(1, EXP_ROWS // 4) as q:
                        for j in range(4):
                            load_rows(4 * q + (tiles0 + j), j, False)

            for m in range(MT):
                sp.wait_ge(s["n_x"], 9 + m)
                sp.dma_start(out[0].rearrange("(m p) d -> p m d", p=P)[:, m, :],
                             BIG[:, 2 * m:2 * m + 2, :].rearrange("p a b -> p (a b)")).then_inc(s["out_done"], 16)
            sp.wait_ge(s["out_done"], 16 * MT)

        N_CONST = 9
        N_VEC = 12

        @block.gpsimd
        def _(pool):
            ch = Chain(pool, s["pool_chain"])
            link = ch.link
            pool.dma_start(XR[:, :, :], a["x"][0].rearrange("(m p) d -> p m d", p=P)).then_inc(s["x_in"], 16)
            vec, vecw = WORK[:, 0:P], WORK[:, P:2 * P]
            row = 0
            for name, n in (("ln_even", 16), ("ln_odd", 16), ("ln1_w_2", 16), ("ln2_w_2", 16),
                            ("ssd_norm_w_2", 8), ("conv_b_2", 12), ("lower_bounds", 8), ("g_norm_b", 1)):
                v = a[name]
                if name in ("ln_even", "ln_odd", "lower_bounds", "g_norm_b"):
                    v = v[0]
                pool.dma_start(vec[row:row + n, :], v.rearrange("(k p) -> k p", p=P)).then_inc(s["vec_in"], 16)
                row += n
            for tap in range(4):
                pool.dma_start(vecw[12 * tap:12 * tap + 12, :],
                               a["conv_w_2"][tap].rearrange("(k p) -> k p", p=P)).then_inc(s["vec_in"], 16)
            for name, at, n in (("q_norm_a", A_QN, 64), ("k_norm_a", A_KN, 64), ("sinks_a", A_SINK, 16),
                                ("dt_bias_2", S_DTB, 16), ("a_log_2", S_AL, 16), ("fox_f_bias_2", F_FB, 16),
                                ("d_skip_2", S_DSK, 16)):
                v = a[name][0] if name in ("q_norm_a", "k_norm_a", "sinks_a") else a[name]
                pool.dma_start(BC[:, at:at + n], v.partition_broadcast(P)).then_inc(s["const_in"], 16)
            for i, name in enumerate(("rope_cos", "rope_sin")):
                pool.dma_start(ROPE[:, i, :, :], a[name].rearrange("(m p) f -> p m f", p=P)).then_inc(s["const_in"], 16)

            def select(view, op, fill, base, pattern, cm):
                link(pool.affine_select(out=view, in_=view, compare_op=op, fill=fill, base=base,
                                        pattern=pattern, channel_multiplier=cm))

            for tile, v in ((ONES, 1.0), (ID, 1.0), (LE, 1.0), (GT, 1.0), (NTRI, -1.0), (NONES, -1.0),
                            (AMASK, 0.0), (FMASK, 0.0)):
                link(pool.memset(tile[:, :], v))
            select(ID[:, :], ALU.is_equal, 0.0, 0, [[-1, P]], 1)
            pool.sem_inc(s["masks"], 1)
            select(LE[:, :], ALU.is_ge, 0.0, 0, [[1, P]], -1)
            select(GT[:, :], ALU.is_gt, 0.0, 0, [[-1, P]], 1)
            select(NTRI[:, :], ALU.is_ge, 0.0, 0, [[-1, P]], 1)
            select(AMASK[:, 0:P], ALU.is_ge, NEG, 0, [[-1, P]], 1)
            select(AMASK[:, P:2 * P], ALU.is_gt, NEG, 0, [[1, P]], -1)
            select(AMASK[:, 2 * P:3 * P], ALU.is_ge, NEG, 0, [[-1, P]], 1)
            select(FMASK[:, 0:P], ALU.is_ge, NEG, 0, [[-1, P]], 1)
            select(FMASK[:, 2 * P:3 * P], ALU.is_ge, NEG, 0, [[-1, P]], 1)
            link(pool.memset(even_spare[:, 0:1920], 1.0))
            for l in range(LEVELS):
                h = 1 << l
                nb = P // (2 * h)
                ms = MS[:, l, :].rearrange("p (b s r) -> p b s r", b=nb, s=2)
                select(ms[:, :, 1, :], ALU.is_ge, 0.0, -h, [[-2 * h, nb], [0, h]], 1)
                select(ms[:, :, 1, :], ALU.is_ge, 0.0, h, [[2 * h, nb], [1, h]], -1)
                select(ms[:, :, 0, :], ALU.is_gt, 0.0, 0, [[-2 * h, nb], [-1, h]], 1)
                select(ms[:, :, 0, :], ALU.is_gt, 0.0, h, [[2 * h, nb], [0, h]], -1)
                mk = MK[:, l, :].rearrange("p (b s r) -> p b s r", b=nb, s=2)
                select(mk[:, :, 1, :], ALU.is_ge, 0.0, 0, [[-2 * h, nb], [0, h]], 1)
                select(mk[:, :, 1, :], ALU.is_gt, 0.0, h, [[2 * h, nb], [0, h]], -1)
                link(pool.memset(mk[:, :, 0, :], 0.0))
            select(MK[:, LEVELS, :], ALU.is_equal, 0.0, 0, [[-1, P]], 1)
            pool.wait_ge(s["const_in"], 16 * N_CONST)
            link(pool.tensor_copy(DSK[0:64, :], BC[0:64, S_DSK:S_DSK + 16:2]))
            link(pool.tensor_copy(DSK[64:128, :], BC[64:128, S_DSK + 1:S_DSK + 16:2]))
            pool.sem_inc(s["masks"], 1)

            def normalise(p, probs):
                for h in range(16):
                    pool.wait_ge(s[p + "rcp"], h + 1)
                    rc = SM[:, 24 + 2 * (h % 2):26 + 2 * (h % 2)]
                    pr = probs[:, h % 2, :]
                    pool.tensor_scalar(pr[:, 0:P], pr[:, 0:P], rc[:, 0:1], None, ALU.mult)
                    pool.tensor_scalar(pr[:, P:384], pr[:, P:384], rc[:, 1:2], None, ALU.mult)\
                        .then_inc(s[p + "pn"], 1)

            normalise("a_", BIG[:, 0, 0:768].rearrange("p (b c) -> p b c", b=2))

            ke = WORK[:, 2048:3072].rearrange("p (l i) -> p l i", l=8)
            for u in range(2 * B_HEADS):
                h, m = u // 2, u % 2
                pool.wait_ge(s["b_ex"], u + 1)
                if u >= 1:
                    pool.wait_ge(s["b_att"], u)
                ex = WORK[:, 0:1024].rearrange("p (l i) -> p l i", l=8)
                k = chan(7, h)[:, m * P:(m + 1) * P]
                kk = k.unsqueeze(1).broadcast_to([P, 8, P])
                pool.tensor_tensor(ke, ex, kk, ALU.mult).then_inc(s["b_ke"], 1)
                if m == 0:
                    if h >= 1:
                        pool.wait_ge(s["b_cross"], h)
                    pool.tensor_tensor(KX, ex[:, 7, :], k, ALU.mult).then_inc(s["b_kx"], 1)

            pool.wait_ge(s["y_l"], 16)
            link(pool.memset(CM, 1.0))
            link(pool.memset(CN, 0.0))
            for d0 in (0, 256):
                select(CM[:, d0:d0 + P], ALU.is_gt, 0.0, 0, [[1, P]], -1)
                select(CN[:, d0:d0 + P], ALU.is_gt, NEG, 0, [[1, P]], -1)
            pool.sem_inc(s["c_mask"], 1)

            ag = WORK[:, 0:768].rearrange("p (b c) -> p b c", b=2)
            pool.wait_ge(s["s_a"], 1)
            acol = SM[:, 64:96].rearrange("p (m h) -> p m h", m=2)
            for h in range(S_HEADS):
                if h >= 2:
                    pool.wait_ge(s["s_seg"], h - 1)
                g = ag[:, h % 2, :]
                pool.tensor_scalar(g[:, 0:P], GT[:, :], acol[:, 0, h:h + 1], None, ALU.mult)
                pool.tensor_scalar(g[:, P:256], ONES[:, :], acol[:, 1, h:h + 1], None, ALU.mult)
                pool.tensor_scalar(g[:, 256:384], GT[:, :], acol[:, 1, h:h + 1], None, ALU.mult)\
                    .then_inc(s["s_ag"], 1)

            lg = WORK[:, 0:768].rearrange("p (b c) -> p b c", b=2)
            lf = SM[:, 96:128].rearrange("p (m h) -> p m h", m=2)
            pool.wait_ge(s["f_lf"], 1)
            pool.wait_ge(s["s_seg"], S_HEADS)
            probs = WORK[:, 1536:2304].rearrange("p (b c) -> p b c", b=2)
            for i in range(F_HEADS + 2):
                if i < F_HEADS:
                    h = i
                    if h >= 2:
                        pool.wait_ge(s["f_score"], h - 1)
                    g = lg[:, h % 2, :]
                    pool.tensor_scalar(g[:, 0:P], GT[:, :], lf[:, 0, h:h + 1], None, ALU.mult)
                    pool.tensor_scalar(g[:, P:256], ONES[:, :], lf[:, 1, h:h + 1], None, ALU.mult)
                    pool.tensor_scalar(g[:, 256:384], GT[:, :], lf[:, 1, h:h + 1], None, ALU.mult)\
                        .then_inc(s["f_lg"], 1)
                if i >= 2:
                    h = i - 2
                    pool.wait_ge(s["f_rcp"], h + 1)
                    rc = SM[:, 24 + 2 * (h % 2):26 + 2 * (h % 2)]
                    pr = probs[:, h % 2, :]
                    pool.tensor_scalar(pr[:, 0:P], pr[:, 0:P], rc[:, 0:1], None, ALU.mult)
                    pool.tensor_scalar(pr[:, P:384], pr[:, P:384], rc[:, 1:2], None, ALU.mult)\
                        .then_inc(s["f_pn"], 1)

            pool.wait_ge(s["y_l"], 48)
            iota_i = WORK[:, 3968:4096].bitcast(mybir.dt.int32)
            link(pool.iota(iota_i, [[1, P]], base=0, channel_multiplier=0))
            iota = WORK[:, 3840:3968]
            pool.tensor_copy(iota, iota_i).then_inc(s["tk_iota"], 1)
            pool.wait_ge(s["tk_tc"], 6)
            tkT = WORK[:, 3072:3840].rearrange("p (a t) -> p a t", a=3)
            for half in range(HALVES):
                def one_hot_gates(g, slot):
                    pool.wait_ge(s["oh_eq"], g + 1)
                    o = WORK[:, 2048 + 512 * slot:2560 + 512 * slot].rearrange("p (t i) -> p t i", t=8)
                    t0 = (g - 32 * half) * 8
                    gate = tkT[:, 2, bass.ds(t0, 8)].unsqueeze(2).broadcast_to([P, 8, EXP_ROWS])
                    pool.tensor_tensor(o, o, gate, ALU.mult).then_inc(s["oh2"], 1)

                for g in range(2):
                    one_hot_gates(32 * half + g, g)
                with pool.Fori(1, 16) as q:
                    for j in range(2):
                        one_hot_gates(2 * q + (32 * half + j), j)

            pool.wait_ge(s["g_mm"], 32 * HALVES)
            pool.dma_start(WORK[:, 0:2048], a["lnf_w_2"].partition_broadcast(P)).then_inc(s["lnf_in"], 16)

        @block.scalar
        def _(act):
            ch = Chain(act, s["act_chain"])
            link = ch.link
            pending = []

            def leave(r, i, parity, t):
                kind = r["kind"]
                act.wait_ge(s["ws_used"], 8 * (t + 1))
                if kind == "res":
                    return
                for b in range(2):
                    ps = bank[2 * parity + b]
                    if kind == "gate":
                        dst, src = DTF[:, r["dest"], b, :], ps[:, 0:16]
                    elif kind == "tok" or kind in ("chan", "silu", "scaled", "eighth"):
                        w = r["width"]
                        dst = BIG[:, bass.ds(r["dest"] + i, 1), b * 512:b * 512 + w].rearrange("p o n -> p (o n)")
                        src = ps[:, 0:w]
                    if kind == "silu":
                        ins = act.activation(dst, src, ACT.Silu)
                    elif kind == "scaled":
                        ins = act.activation(dst, src, ACT.Copy, scale=float(C_HD) ** -0.5)
                    elif kind == "eighth":
                        ins = act.activation(dst, src, ACT.Copy, scale=float(F_HD) ** -0.5)
                    else:
                        ins = act.activation(dst, src, ACT.Copy)
                ins.then_inc(s["tile_free"], 1)

            def split(r, i, parity, first):
                t = r["base"] + i
                w = r["width"]
                for sub in range(8):
                    if sub == 4:
                        if not first:
                            leave(r, i - 1, 1 - parity, t - 1)
                        elif pending:
                            leave(*pending.pop())
                    if sub % 2 == 0:
                        act.wait_ge(s[f"w_full{sub // 2}"], 16 * (t + 1))
                    if r["base"] > 0 or not first or sub >= 4:
                        act.wait_ge(s["ws_used"], 8 * t + (sub - 3))
                    raw = RAW[:, sub // 2, :].rearrange("p (k n) -> p k n", k=4)
                    k0 = 2 * (sub % 2)
                    sl = 2 * (sub % 4)
                    act.activation(WH[:, sl:sl + 2, 0:w], raw[:, k0:k0 + 2, 0:w], ACT.Copy)\
                        .then_inc(s["wh_done"], 1)
                if isinstance(i, int) and i == r["n"] - 1:
                    pending.append((r, i, parity, t))

            def phase(name):
                over_tiles(act, name, split)
                leave(*pending.pop())

            def rms(n, scratch):
                ss = SM[:, 16:18]
                for m in range(MT):
                    link(act.activation(scratch, XR[:, m, :], ACT.Square, accum_out=ss[:, m:m + 1]))
                link(act.activation(SM[:, 18:20], ss, ACT.Ln, bias=SM[:, 22:23], scale=1.0 / D))
                act.activation(SM[:, 20:22], SM[:, 18:20], ACT.Exp, scale=-0.5).then_inc(s["n_rstd"], 1)

            def norm_high(n):
                for g in range(8):
                    act.wait_ge(s["n_t"], 8 * n + g + 1)
                    for kk in range(2):
                        kt = 2 * g + kk
                        act.activation(HH[:, kt, :], bank[4 + g % 4][:, kk * T:(kk + 1) * T], ACT.Copy,
                                       scale=COLS[:, V_LN + 16 * n + kt:V_LN + 16 * n + kt + 1])\
                            .then_inc(s["n_h"], 1)

            def y_high(c):
                act.wait_ge(s["y_ready"], c + 1)
                act.activation(HH[:, c % 16, :], YB[:, c % 2, :], ACT.Copy).then_inc(s["y_h"], 1)

            big_scratch = BIG[:, 4:6, :].rearrange("p a b -> p (a b)")

            act.wait_ge(s["vec_t"], 1)
            act.activation(COLS[:, 0:V_ROWS], bank[0][:, 0:V_ROWS], ACT.Copy)
            act.activation(COLS[:, V_CW:V_COLS], bank[0][:, V_ROWS:V_ROWS + 48], ACT.Copy).then_inc(s["cols_set"], 1)
            act.wait_ge(s["x_in"], 16)
            act.wait_ge(s["eps_set"], 1)
            act.wait_ge(s["cols_set"], 1)
            rms(0, big_scratch)
            norm_high(0)
            phase("even_in")

            st = SM[:, 96:132]
            act.wait_ge(s["aq_ready"], 1)
            link(act.activation(st, st, ACT.Ln, bias=SM[:, 22:23], scale=1.0 / A_HD))
            link(act.activation(st, st, ACT.Exp, scale=-0.5))
            act.sem_inc(s["aq_ready"], 1)
            qT = WORK[:, 0:2048].rearrange("p (k t) -> p k t", k=8)
            kT = WORK[:, 2048:2560].rearrange("p (k t) -> p k t", k=2)
            for g in range(5):
                act.wait_ge(s["qk_t"], g + 1)
                dst = qT[:, 2 * g:2 * g + 2, :] if g < 4 else kT[:, :, :]
                act.activation(dst, bank[4 + g % 4][:, :].rearrange("p (k t) -> p k t", k=2), ACT.Copy)\
                    .then_inc(s["qk_c"], 1)

            def attend(p, S, probs, pt, sinks, c0):
                for i in range(16 + 3):
                    if i < 16:
                        h = i
                        act.wait_ge(s[p + "soft"], h + 1)
                        if h >= 2:
                            act.wait_ge(s[p + "pt"], h - 1)
                        nm = SM[:, 32 + 2 * (h % 2):34 + 2 * (h % 2)]
                        den = SM[:, 36 + 2 * (h % 2):38 + 2 * (h % 2)]
                        act.activation(probs[:, h % 2, 0:P], S[:, h % 2, 0:P], ACT.Exp, bias=nm[:, 0:1],
                                       accum_out=den[:, 0:1])
                        if sinks is not None:
                            act.activation(SM[:, 40 + 2 * (h % 2):42 + 2 * (h % 2)], nm, ACT.Exp,
                                           bias=sinks[:, h:h + 1])
                        act.activation(probs[:, h % 2, P:384], S[:, h % 2, P:384], ACT.Exp, bias=nm[:, 1:2],
                                       accum_out=den[:, 1:2]).then_inc(s[p + "exp"], 1)
                    if 1 <= i <= 16:
                        h = i - 1
                        act.wait_ge(s[p + "pt"], h + 1)
                        if h >= 2:
                            act.wait_ge(s[p + "pv"], h - 1)
                        act.activation(pt[:, h % 2, :], bank[6 + h % 2][:, 0:384], ACT.Copy)\
                            .then_inc(s[p + "ptc"], 1)
                    if i >= 4 and i % 2 == 0:
                        y_high(c0 + (i - 4) // 2)

            abuf = BIG[:, 0:2, :].rearrange("p a b -> p (a b)")
            attend("a_", WORK[:, 2560:3328].rearrange("p (b c) -> p b c", b=2),
                   abuf[:, 0:768].rearrange("p (b c) -> p b c", b=2),
                   abuf[:, 1024:1792].rearrange("p (b c) -> p b c", b=2), BC[:, A_SINK:A_SINK + 16], 0)

            T1 = BIG[:, 0:2, :].rearrange("p a b -> p (a b)")
            T2 = BIG[:, 3:5, :].rearrange("p a b -> p (a b)")
            bfv = bf.rearrange("p a b -> p (a b)")
            lbz = SM[:, 44:52]
            act.wait_ge(s["b_vec"], 1)
            link(act.activation(SM[:, 52:60], lbz, ACT.Exp))
            act.sem_inc(s["b_vec"], 1)
            act.wait_ge(s["b_vec"], 3)
            link(act.activation(SM[:, 68:76], SM[:, 68:76], ACT.Ln, scale=2.0 ** 64))
            link(act.activation(SM[:, 76:84], SM[:, 60:68], ACT.Ln, scale=-1.0, bias=SM[:, 23:24]))
            act.sem_inc(s["b_vec"], 1)
            link(act.activation(T1, bfv, ACT.Abs))
            link(act.activation(T1, T1, ACT.Exp, scale=-1.0))
            act.activation(T1, T1, ACT.Ln, bias=SM[:, 23:24]).then_inc(s["b_e"], 1)
            act.wait_ge(s["b_lsg"], 2)
            act.wait_ge(s["b_vec"], 6)
            for h in range(B_HEADS):
                act.activation(bfv[:, h * T:(h + 1) * T], T2[:, h * T:(h + 1) * T], ACT.Exp,
                               bias=SM[:, 76 + h:77 + h]).then_inc(s["b_kin"], 1)
            act.wait_ge(s["b_ml"], B_HEADS)
            for h in range(B_HEADS):
                link(act.activation(T1[:, h * T:(h + 1) * T], T1[:, h * T:(h + 1) * T], ACT.Abs,
                                    bias=SM[:, 84 + h:85 + h]))
            link(act.activation(T1, T1, ACT.Exp, scale=-1.0))
            act.activation(T1, T1, ACT.Ln, bias=SM[:, 23:24]).then_inc(s["b_x"], 1)

            def decays(u):
                act.wait_ge(s["b_lt"], u + 1)
                if u >= 2:
                    act.wait_ge(s["b_es"], u - 1)
                act.activation(LFT[:, u % 2, :], bank[4][:, (u % 2) * P:(u % 2 + 1) * P], ACT.Copy)\
                    .then_inc(s["b_lf"], 1)
                act.wait_ge(s["b_es"], u + 1)
                if u >= 1:
                    act.wait_ge(s["b_qe"], u)
                    act.wait_ge(s["b_ke"], u)
                    act.wait_ge(s["b_kx"], (u + 1) // 2)
                for b in range(2):
                    ins = act.activation(WORK[:, 512 * b:512 * (b + 1)], bank[b][:, :], ACT.Exp)
                ins.then_inc(s["b_ex"], 1)

            def head_norm(h):
                act.wait_ge(s["b_ov"], h + 1)
                if h >= 1:
                    act.wait_ge(s["b_ss"], h)
                act.activation(BSQ, bank[5 + 2 * (h % 2)][:, 0:T], ACT.Square).then_inc(s["b_sq"], 1)
                act.wait_ge(s["b_ss"], h + 1)
                if h >= 1:
                    act.wait_ge(s["y_ready"], 8 + h)
                link(act.activation(BRS, bank[5 + 2 * (h % 2)][:, T:2 * T], ACT.Ln, bias=SM[:, 22:23], scale=1.0 / B_HD))
                act.activation(BRS, BRS, ACT.Exp, scale=-0.5).then_inc(s["b_rs"], 1)

            for i in range(2 * B_HEADS + 4):
                if i < 2 * B_HEADS:
                    decays(i)
                if i >= 2 and i % 2 == 0 and i - 2 < 2 * B_HEADS:
                    h = (i - 2) // 2
                    act.wait_ge(s["b_cross"], h + 1)
                    if h >= 1:
                        act.wait_ge(s["b_ov"], h)
                    act.activation(CX, bank[6][:, 0:P], ACT.Copy).then_inc(s["b_cx"], 1)
                if i >= 4 and i % 2 == 0:
                    head_norm((i - 4) // 2)
                    y_high(8 + (i - 4) // 2)
            phase("even_out")

            act.wait_ge(s["tile_free"], last_tile("even_out") + 1)
            rms(1, big_scratch)
            norm_high(1)
            phase("odd_in")
            cT = WORK[:, 0:768].rearrange("p (b c) -> p b c", b=2)
            cW = WORK[:, 1536:2304].rearrange("p (b c) -> p b c", b=2)
            for i in range(C_HEADS + 3):
                if i < C_HEADS:
                    h = i
                    act.wait_ge(s["c_z"], h + 1)
                    if h >= 2:
                        act.wait_ge(s["c_sp"], 2 * (h - 1))
                    t = cT[:, h % 2, :]
                    link(act.activation(t, bank[4 + h % 2][:, 0:384], ACT.Abs))
                    link(act.activation(t, t, ACT.Exp, scale=-1.0))
                    act.activation(t, t, ACT.Ln, bias=SM[:, 23:24]).then_inc(s["c_exp"], 1)
                if 1 <= i <= C_HEADS:
                    h = i - 1
                    act.wait_ge(s["c_min"], h + 1)
                    act.activation(cW[:, h % 2, :], cW[:, h % 2, :], ACT.Exp).then_inc(s["c_w"], 1)
                if i >= 3:
                    y_high(16 + i - 3)
            phase("odd_out")

            act.wait_ge(s["tile_free"], last_tile("odd_out") + 1)
            rms(2, big_scratch)
            norm_high(2)
            phase("two_in")
            act.wait_ge(s["s_dt"], 1)
            g64 = SM[:, 64:128]
            link(act.activation(WORK[:, 2560:2624], g64, ACT.Abs))
            link(act.activation(WORK[:, 2560:2624], WORK[:, 2560:2624], ACT.Exp, scale=-1.0))
            link(act.activation(WORK[:, 2560:2624], WORK[:, 2560:2624], ACT.Ln, bias=SM[:, 23:24]))
            act.activation(WORK[:, 2624:2640], BC[:, S_AL:S_AL + 16], ACT.Exp).then_inc(s["s_e"], 1)
            XBC = BIG[:, 11:14, :].rearrange("p a b -> p (a b)")
            for g in range(3):
                act.wait_ge(s["s_conv"], 4 * (g + 1))
                act.activation(XBC[:, g * 1024:(g + 1) * 1024], XBC[:, g * 1024:(g + 1) * 1024], ACT.Silu)\
                    .then_inc(s["s_xbc"], 1)
            sE = WORK[:, 768:1536].rearrange("p (b c) -> p b c", b=2)
            for h in range(S_HEADS):
                act.wait_ge(s["s_seg"], h + 1)
                if h >= 2:
                    act.wait_ge(s["s_l"], h - 1)
                act.activation(sE[:, h % 2, :], bank[4 + h % 2][:, 0:384], ACT.Exp).then_inc(s["s_ex"], 1)
            ZS = BIG[:, 0:2, :].rearrange("p a b -> p (a b)")
            SQ = WORK[:, 768:1792]
            for g in range(2):
                act.wait_ge(s["s_yg"], 4 * (g + 1))
                act.wait_ge(s["s_l"], S_HEADS)
                if g == 1:
                    act.wait_ge(s["s_ss"], 1)
                act.activation(SQ, ZS[:, g * 1024:(g + 1) * 1024], ACT.Square).then_inc(s["s_sq"], 1)
                act.wait_ge(s["s_ss"], g + 1)
                if g == 1:
                    act.wait_ge(s["y_ready"], 36)
                link(act.activation(WORK[:, 3456:3712], bank[6][:, 0:T], ACT.Ln, bias=SM[:, 22:23],
                                    scale=1.0 / 512))
                act.activation(WORK[:, 3456:3712], WORK[:, 3456:3712], ACT.Exp, scale=-0.5)\
                    .then_inc(s["s_rs"], 1)
                for j in range(4):
                    y_high(32 + 4 * g + j)

            attend("f_", WORK[:, 768:1536].rearrange("p (b c) -> p b c", b=2),
                   WORK[:, 1536:2304].rearrange("p (b c) -> p b c", b=2),
                   WORK[:, 2304:3072].rearrange("p (b c) -> p b c", b=2), None, 40)
            phase("two_out")

            act.wait_ge(s["tile_free"], last_tile("two_out") + 1)
            rms(3, big_scratch)
            norm_high(3)
            phase("peer_q")
            kTp = BIG[:, 4:6, :].rearrange("p a b -> p (a b)")
            for g in range(4):
                act.wait_ge(s["k_t"], g + 1)
                act.activation(kTp[:, g * 512:(g + 1) * 512], bank[4 + g][:, :], ACT.Copy).then_inc(s["k_c"], 1)
            SC = BIG[:, 6:10, :].rearrange("p a b -> p (a b)")
            for g in range(8):
                act.wait_ge(s["q_s"], g + 1)
                act.activation(SC[:, g * 512:(g + 1) * 512], bank[g % 4][:, :], ACT.Copy).then_inc(s["q_sc"], 1)
            for m in range(MT):
                act.wait_ge(s["tk_e"], m + 1)
                act.activation(WORK[:, 1024 + 128 * m:1152 + 128 * m], WORK[:, 1024 + 128 * m:1152 + 128 * m],
                               ACT.Exp).then_inc(s["tk_g"], 1)
            tkT = WORK[:, 3072:3840].rearrange("p (a t) -> p a t", a=3)
            for n in range(6):
                act.wait_ge(s["tk_t"], n + 1)
                act.activation(tkT[:, n % 3, (n // 3) * P:(n // 3 + 1) * P], bank[4 + n % 2][:, 0:P], ACT.Copy)\
                    .then_inc(s["tk_tc"], 1)

            GB = BIG[:, :, :].rearrange("p a b -> p (a b)").rearrange("p (i t) -> p i t", t=T)
            for half in range(HALVES):
                def gates_out(g, slot):
                    act.wait_ge(s["g_mm"], g + 1)
                    t0 = (g - 32 * half) * 8
                    act.activation(GB[:, :, bass.ds(t0, 8)],
                                   bank[4 + slot][:, :].rearrange("p (t i) -> p i t", t=8), ACT.Copy)\
                        .then_inc(s["g_free"], 1)

                if half == 1:
                    act.wait_ge(s["o_mm"], EXP_ROWS)
                gates_out(32 * half, 0)
                gates_out(32 * half + 1, 1)
                with act.Fori(1, 16) as q:
                    for j in range(2):
                        gates_out(2 * q + (32 * half + j), j)

                def rows_high(n, j, fresh):
                    for g in range(4):
                        act.wait_ge(s["t_t"], 4 * n + g + 1)
                        if not fresh:
                            act.wait_ge(s["u_used"], 4 * n + (g - 7))
                        act.activation(WH[:, 4 * (j % 2) + g, :], bank[4 + g][:, :], ACT.Copy)\
                            .then_inc(s["t_h"], 1)

                def gelu(n, j, fresh):
                    act.wait_ge(s["u_used"], 4 * n + 4)
                    if not fresh:
                        act.wait_ge(s["a_p"], n - 1)
                    act.activation(YB[:, j % 2, :], bank[j % 2][:, 0:T], ACT.Gelu).then_inc(s["a_gelu"], 1)

                n0 = half * EXP_ROWS
                if half == 1:
                    act.wait_ge(s["o_mm"], EXP_ROWS)
                rows_high(n0, 0, True)
                rows_high(n0 + 1, 1, True)
                gelu(n0, 0, half == 0)
                rows_high(n0 + 2, 0, False)
                gelu(n0 + 1, 1, half == 0)
                rows_high(n0 + 3, 1, False)
                gelu(n0 + 2, 0, False)
                with act.Fori(1, EXP_ROWS // 4) as q:
                    for j in range(4):
                        rows_high(4 * q + (n0 + j), j, False)
                        gelu(4 * q + (n0 + j - 1), (j + 1) % 2, False)
                gelu(n0 + EXP_ROWS - 1, 1, False)

                def rows_out_high(n, j, fresh, full):
                    i = n - n0
                    if not fresh:
                        act.wait_ge(s["o_mm"], n - 1)
                    act.activation(PS[:, j % 2, 0, :], GB[:, bass.ds(i, 1), :].rearrange("p o t -> p (o t)"),
                                   ACT.Copy).then_inc(s["p_h"], 1)
                    act.wait_ge(s[f"v_full{j}"], full)
                    act.activation(WH[:, 4 * (j % 2):4 * (j % 2) + 4, :],
                                   RAW[:, j, :].rearrange("p (g n) -> p g n", g=4), ACT.Copy)\
                        .then_inc(s["v_h"], 1)

                act.wait_ge(s["a_p"], n0 + EXP_ROWS)
                for j in range(4):
                    rows_out_high(n0 + j, j, j < 2, 16 * (n0 // 4 + 1))
                with act.Fori(1, EXP_ROWS // 4) as q:
                    for j in range(4):
                        rows_out_high(4 * q + (n0 + j), j, False, 16 * q + 16 * (n0 // 4 + 1))

            act.wait_ge(s["o_add"], 2)
            rms(4, big_scratch)

        @block.vector
        def _(dve):
            ch = Chain(dve, s["dve_chain"])
            link = ch.link
            pending = []

            def leave(r, i, parity, t):
                if r["kind"] != "res":
                    return
                dve.wait_ge(s["ws_used"], 8 * (t + 1))
                for m in range(MT):
                    x = XR[:, m, bass.ds(r["c0"] + i * NW, NW)]
                    ins = dve.tensor_tensor(x, x, bank[2 * parity + m][:, :], ALU.add)
                ins.then_inc(s["tile_free"], 1)

            def split(r, i, parity, first):
                t = r["base"] + i
                w = r["width"]
                for sub in range(8):
                    if sub == 4:
                        if not first:
                            leave(r, i - 1, 1 - parity, t - 1)
                        elif pending:
                            leave(*pending.pop())
                    dve.wait_ge(s["wh_done"], 8 * t + sub + 1)
                    raw = RAW[:, sub // 2, :].rearrange("p (k n) -> p k n", k=4)
                    k0 = 2 * (sub % 2)
                    sl = 2 * (sub % 4)
                    dve.tensor_tensor(WL[:, sl:sl + 2, 0:w], raw[:, k0:k0 + 2, 0:w],
                                      WH[:, sl:sl + 2, 0:w].bitcast(F32), ALU.subtract).then_inc(s["wl_done"], 1)
                if isinstance(i, int) and i == r["n"] - 1:
                    pending.append((r, i, parity, t))

            def phase(name):
                over_tiles(dve, name, split)
                leave(*pending.pop())

            xn = BIG[:, 0:4, :].rearrange("p (m a) b -> p m (a b)", m=2)

            def norm_low(n):
                dve.wait_ge(s["n_rstd"], n + 1)
                for m in range(MT):
                    dve.tensor_scalar(xn[:, m, :], XR[:, m, :], SM[:, 20 + m:21 + m], None, ALU.mult)\
                        .then_inc(s["n_x"], 1)
                for g in range(8):
                    dve.wait_ge(s["n_h"], 16 * n + 2 * g + 2)
                    for kk in range(2):
                        kt = 2 * g + kk
                        dve.scalar_tensor_tensor(
                            HL[:, kt, :], bank[4 + g % 4][:, kk * T:(kk + 1) * T],
                            COLS[:, V_LN + 16 * n + kt:V_LN + 16 * n + kt + 1],
                            HH[:, kt, :].bitcast(F32), ALU.mult, ALU.subtract).then_inc(s["n_l"], 1)

            def y_wait(c):
                if c >= 2:
                    dve.wait_ge(s["y_l"], c - 1)

            def y_low(c):
                dve.wait_ge(s["y_h"], c + 1)
                dve.tensor_tensor(HL[:, c % 16, :], YB[:, c % 2, :], HH[:, c % 16, :].bitcast(F32),
                                  ALU.subtract).then_inc(s["y_l"], 1)

            link(dve.memset(SM[:, 22:23], EPS))
            dve.memset(SM[:, 23:24], 1.0).then_inc(s["eps_set"], 1)
            norm_low(0)
            phase("even_in")

            dve.wait_ge(s["const_in"], 16 * N_CONST)
            dve.wait_ge(s["tile_free"], 13)
            q_t = BIG[:, 0:2, :].rearrange("p a b -> p (a b)")
            kv = BIG[:, 2, :].rearrange("p (m n) -> p m n", m=2)
            kcol = kv[:, :, 0:P]
            w1, w2 = WORK[:, 0:2048], WORK[:, 2048:4096]
            st = SM[:, 96:132]
            link(dve.tensor_tensor(w1, q_t, q_t, ALU.mult))
            link(dve.tensor_reduce(st[:, 0:32], w1.rearrange("p (h d) -> p h d", d=64), AX.X, ALU.add))
            k2 = w2[:, 0:256].rearrange("p (m n) -> p m n", m=2)
            link(dve.tensor_tensor(k2, kcol, kcol, ALU.mult))
            link(dve.tensor_reduce(st[:, 32:36], w2[:, 0:256].rearrange("p (h d) -> p h d", d=64), AX.X, ALU.add))
            dve.sem_inc(s["aq_ready"], 1)
            dve.wait_ge(s["aq_ready"], 2)
            kc = w2[:, 1024:1280].rearrange("p (h d) -> p h d", d=64)
            q3 = q_t.rearrange("p (h d) -> p h d", d=64)
            link(dve.tensor_tensor(q3, q3, st[:, 0:32].unsqueeze(2).broadcast_to([P, 32, 64]), ALU.mult))
            link(dve.tensor_tensor(q3, q3, BC[:, A_QN:A_QN + 64].unsqueeze(1).broadcast_to([P, 32, 64]), ALU.mult))
            link(dve.tensor_tensor(kc.rearrange("p (m g) d -> p m g d", m=2), kcol.rearrange("p m (g d) -> p m g d", g=2),
                                   st[:, 32:36].rearrange("p (m g) -> p m g", m=2).unsqueeze(3).broadcast_to([P, 2, 2, 64]),
                                   ALU.mult))
            link(dve.tensor_tensor(kc, kc, BC[:, A_KN:A_KN + 64].unsqueeze(1).broadcast_to([P, 4, 64]), ALU.mult))
            for tt in range(2):
                for m in range(MT):
                    o = tt * 1024 + m * 512
                    x = q_t[:, o:o + 512].rearrange("p (h d) -> p h d", h=16)
                    c = ROPE[:, 0, m, :].unsqueeze(1).broadcast_to([P, 16, 32])
                    sn = ROPE[:, 1, m, :].unsqueeze(1).broadcast_to([P, 16, 32])
                    y1 = w1[:, 0:512].rearrange("p (h d) -> p h d", h=16)
                    y2 = w1[:, 512:1024].rearrange("p (h d) -> p h d", h=16)
                    link(dve.tensor_tensor(y1, x, c, ALU.mult))
                    link(dve.tensor_tensor(y2, x, sn, ALU.mult))
                    xh = q_t[:, o:o + 512].rearrange("p (h f d) -> p h f d", h=8, f=2)
                    y1h = w1[:, 0:512].rearrange("p (h f d) -> p h f d", h=8, f=2)
                    y2h = w1[:, 512:1024].rearrange("p (h f d) -> p h f d", h=8, f=2)
                    link(dve.tensor_tensor(xh[:, :, 0, :], y1h[:, :, 0, :], y2h[:, :, 1, :], ALU.subtract))
                    link(dve.tensor_tensor(xh[:, :, 1, :], y1h[:, :, 1, :], y2h[:, :, 0, :], ALU.add))
            kd = w2[:, 1536:2048].rearrange("p (m g c d) -> p m g c d", m=2, g=2, c=2)
            for m in range(MT):
                x = kc[:, 2 * m:2 * m + 2, :].rearrange("p h (f d) -> p (h f) d", f=2)
                c = ROPE[:, 0, m, :].unsqueeze(1).broadcast_to([P, 4, 32])
                sn = ROPE[:, 1, m, :].unsqueeze(1).broadcast_to([P, 4, 32])
                y1 = w1[:, 0:128].rearrange("p (h d) -> p h d", h=4)
                y2 = w1[:, 128:256].rearrange("p (h d) -> p h d", h=4)
                link(dve.tensor_tensor(y1, x, c, ALU.mult))
                link(dve.tensor_tensor(y2, x, sn, ALU.mult))
                y1h = w1[:, 0:128].rearrange("p (h f d) -> p h f d", h=2, f=2)
                y2h = w1[:, 128:256].rearrange("p (h f d) -> p h f d", h=2, f=2)
                for c2 in range(2):
                    link(dve.tensor_tensor(kd[:, m, :, c2, 0:32], y1h[:, :, 0, :], y2h[:, :, 1, :], ALU.subtract))
                    link(dve.tensor_tensor(kd[:, m, :, c2, 32:64], y1h[:, :, 1, :], y2h[:, :, 0, :], ALU.add))
            dve.sem_inc(s["aq_ready"], 1)

            def attend(p, S, mask, scale, sinks, gate, c0):
                for i in range(16 + 3):
                    if i < 16:
                        h = i
                        dve.wait_ge(s[p + "score"], h + 1)
                        if h >= 2:
                            dve.wait_ge(s[p + "exp"], h - 1)
                        z = S[:, h % 2, :]
                        link(dve.scalar_tensor_tensor(z, bank[4 + h % 2][:, 0:384], scale, mask, ALU.mult, ALU.add))
                        mx = SM[:, 28 + 2 * (h % 2):30 + 2 * (h % 2)]
                        nm = SM[:, 32 + 2 * (h % 2):34 + 2 * (h % 2)]
                        link(dve.tensor_reduce(mx[:, 0:1], z[:, 0:P], AX.X, ALU.max))
                        link(dve.tensor_reduce(mx[:, 1:2], z[:, P:384], AX.X, ALU.max))
                        if sinks is not None:
                            dve.tensor_scalar(nm, mx, sinks[:, h:h + 1], -1.0, ALU.max, ALU.mult)\
                                .then_inc(s[p + "soft"], 1)
                        else:
                            dve.tensor_scalar(nm, mx, -1.0, None, ALU.mult).then_inc(s[p + "soft"], 1)
                    if 1 <= i <= 16:
                        h = i - 1
                        den = SM[:, 36 + 2 * (h % 2):38 + 2 * (h % 2)]
                        rc = SM[:, 24 + 2 * (h % 2):26 + 2 * (h % 2)]
                        dve.wait_ge(s[p + "exp"], h + 1)
                        if h >= 2:
                            dve.wait_ge(s[p + "pn"], h - 1)
                        if sinks is not None:
                            link(dve.tensor_tensor(den, den, SM[:, 40 + 2 * (h % 2):42 + 2 * (h % 2)], ALU.add))
                        dve.reciprocal(rc, den).then_inc(s[p + "rcp"], 1)
                    if i >= 4 and i % 2 == 0:
                        j = (i - 4) // 2
                        c = c0 + j
                        if j >= 1:
                            y_low(c - 1)
                        dve.wait_ge(s[p + "pv"], 2 * j + 2)
                        y_wait(c)
                        o = bank[j % 2][:, 0:T]
                        if gate is not None:
                            dve.tensor_tensor(YB[:, c % 2, :], o, gate(j), ALU.mult).then_inc(s["y_ready"], 1)
                        else:
                            dve.tensor_copy(YB[:, c % 2, :], o).then_inc(s["y_ready"], 1)
                y_low(c0 + 7)

            attend("a_", WORK[:, 2560:3328].rearrange("p (b c) -> p b c", b=2), AMASK[:, :],
                   float(A_HD) ** -0.5, BC[:, A_SINK:A_SINK + 16], lambda j: chan(3, j), 0)

            T1 = BIG[:, 0:2, :].rearrange("p a b -> p (a b)")
            T2 = BIG[:, 3:5, :].rearrange("p a b -> p (a b)")
            bfv = bf.rearrange("p a b -> p (a b)")
            link(dve.tensor_tensor(SM[:, 44:52], COLS[:, V_LB:V_LB + 8], COLS[:, V_LB:V_LB + 8], ALU.subtract))
            dve.sem_inc(s["b_vec"], 1)
            dve.wait_ge(s["b_vec"], 2)
            link(dve.reciprocal(SM[:, 60:68], SM[:, 52:60]))
            link(dve.tensor_tensor(SM[:, 52:60], SM[:, 52:60], SM[:, 60:68], ALU.mult))
            link(dve.tensor_tensor(SM[:, 60:68], SM[:, 52:60], SM[:, 52:60], ALU.subtract))
            link(dve.tensor_scalar(SM[:, 68:76], SM[:, 60:68], 1e-30, None, ALU.max))
            link(dve.tensor_tensor(SM[:, 92:100], SM[:, 60:68], SM[:, 68:76], ALU.subtract))
            dve.sem_inc(s["b_vec"], 1)
            dve.wait_ge(s["b_vec"], 4)
            link(dve.tensor_scalar(SM[:, 68:76], SM[:, 68:76], -64.0 * LN2, None, ALU.add))
            link(dve.tensor_tensor(SM[:, 84:92], SM[:, 76:84], SM[:, 68:76], ALU.subtract))
            dve.sem_inc(s["b_vec"], 2)
            dve.wait_ge(s["b_e"], 1)
            link(dve.scalar_tensor_tensor(T1, bfv, 0.0, T1, ALU.min, ALU.subtract))
            dve.sem_inc(s["b_lsg"], 1)
            dve.tensor_tensor(T2, T1, bfv, ALU.subtract).then_inc(s["b_lsg"], 1)
            for h in range(B_HEADS):
                dve.wait_ge(s["b_kin"], h + 1)
                c = slice(h * T, (h + 1) * T)
                link(dve.tensor_scalar(bfv[:, c], bfv[:, c], SM[:, 92 + h:93 + h], None, ALU.add))
                dve.tensor_scalar(T2[:, c], T1[:, c], SM[:, 76 + h:77 + h], SM[:, 68 + h:69 + h], ALU.add, ALU.max)\
                    .then_inc(s["b_ml"], 1)
            dve.wait_ge(s["b_x"], 1)
            link(dve.tensor_tensor(T1, T1, T2, ALU.add))
            dve.sem_inc(s["b_x"], 1)
            qe = WORK[:, 1024:2048].rearrange("p (l i) -> p l i", l=8)
            am = WORK[:, 3072:4096]
            ex = WORK[:, 0:1024].rearrange("p (l i) -> p l i", l=8)
            for i in range(1, 2 * B_HEADS + 4):
                if 0 <= i - 2 < 2 * B_HEADS:
                    u = i - 2
                    dve.wait_ge(s["b_att"], u + 1)
                    if u >= 1:
                        dve.wait_ge(s["b_lev"], u)
                    for b in range(2):
                        ins = dve.tensor_tensor(am[:, 512 * b:512 * (b + 1)], bank[2 + b][:, :],
                                                MK[:, 4 * b:4 * b + 4, :].rearrange("p l i -> p (l i)"), ALU.mult)
                    ins.then_inc(s["b_am"], 1)
                if i - 1 < 2 * B_HEADS:
                    u = i - 1
                    h, m = u // 2, u % 2
                    dve.wait_ge(s["b_ex"], u + 1)
                    if m == 0 and h >= 1:
                        dve.wait_ge(s["b_cross"], h)
                    qq = chan(5, h)[:, m * P:(m + 1) * P].unsqueeze(1).broadcast_to([P, 8, P])
                    dve.tensor_tensor(qe, ex, qq, ALU.mult).then_inc(s["b_qe"], 1)
                if i >= 5 and i % 2 == 1:
                    h = (i - 5) // 2
                    c = 8 + h
                    if h >= 1:
                        y_low(c - 1)
                    dve.wait_ge(s["b_rs"], h + 1)
                    y_wait(c)
                    y = YB[:, c % 2, :]
                    link(dve.scalar_tensor_tensor(y, bank[5 + 2 * (h % 2)][:, 0:T], COLS[:, V_GN:V_GN + 1], BRS,
                                                  ALU.mult, ALU.mult))
                    dve.tensor_tensor(y, y, chan(11, h), ALU.mult).then_inc(s["y_ready"], 1)
            y_low(15)
            phase("even_out")

            norm_low(1)
            phase("odd_in")
            dve.wait_ge(s["c_mask"], 1)
            cT = WORK[:, 0:768].rearrange("p (b c) -> p b c", b=2)
            cS = WORK[:, 768:1536].rearrange("p (b c) -> p b c", b=2)
            cW = WORK[:, 1536:2304].rearrange("p (b c) -> p b c", b=2)
            for i in range(C_HEADS + 3):
                if i < C_HEADS:
                    h = i
                    dve.wait_ge(s["c_exp"], h + 1)
                    if h >= 2:
                        dve.wait_ge(s["c_e"], h - 1)
                    sp_ = cS[:, h % 2, :]
                    dve.scalar_tensor_tensor(sp_, bank[4 + h % 2][:, 0:384], 0.0, cT[:, h % 2, :], ALU.max,
                                             ALU.add).then_inc(s["c_sp"], 1)
                    dve.wait_ge(s["c_sp"], 2 * h + 1)
                    dve.tensor_tensor(sp_, sp_, CM, ALU.mult).then_inc(s["c_sp"], 1)
                if 1 <= i <= C_HEADS:
                    h = i - 1
                    dve.wait_ge(s["c_e"], h + 1)
                    if h >= 2:
                        dve.wait_ge(s["c_pv"], h - 1)
                    dve.tensor_tensor(cW[:, h % 2, :], bank[4 + h % 2][:, 0:384], CN, ALU.min).then_inc(s["c_min"], 1)
                if i >= 3:
                    h = i - 3
                    c = 16 + h
                    if h >= 1:
                        y_low(c - 1)
                    dve.wait_ge(s["c_pv"], h + 1)
                    y_wait(c)
                    dve.tensor_tensor(YB[:, c % 2, :], bank[6 + h % 2][:, 0:T], chan(12, h), ALU.mult)\
                        .then_inc(s["y_ready"], 1)
            y_low(31)
            phase("odd_out")

            norm_low(2)
            phase("two_in")
            dve.wait_ge(s["tile_free"], last_tile("two_in") + 1)
            g64 = SM[:, 64:128]
            dt_, lf = SM[:, 64:96], SM[:, 96:128]

            def per_head(at):
                return BC[:, at:at + 16].unsqueeze(1).broadcast_to([P, 2, 16])

            two = "p (m h) -> p m h"
            link(dve.tensor_tensor(dt_.rearrange(two, m=2), DTF[:, 0, :, :], per_head(S_DTB), ALU.add))
            link(dve.tensor_tensor(lf.rearrange(two, m=2), DTF[:, 1, :, :], per_head(F_FB), ALU.add))
            link(dve.tensor_scalar(lf, lf, -1.0, None, ALU.mult))
            dve.sem_inc(s["s_dt"], 1)
            XB = BIG[:, 2:5, :].rearrange("p a b -> p (a b)")
            XBC = BIG[:, 11:14, :].rearrange("p a b -> p (a b)")
            for k in range(12):
                x, y = XB[:, k * T:(k + 1) * T], XBC[:, k * T:(k + 1) * T]

                def tap(j):
                    return COLS[:, V_CW + 12 * j + k:V_CW + 12 * j + k + 1]

                link(dve.tensor_scalar(y, x, tap(3), COLS[:, V_CB + k:V_CB + k + 1], ALU.mult, ALU.add))
                for back in (1, 2, 3):
                    ins = dve.scalar_tensor_tensor(y[:, back:T], x[:, 0:T - back], tap(3 - back), y[:, back:T],
                                                   ALU.mult, ALU.add)
                    if back < 3:
                        link(ins)
                    else:
                        ins.then_inc(s["s_conv"], 1)
            dve.wait_ge(s["s_e"], 1)
            link(dve.scalar_tensor_tensor(g64, g64, 0.0, WORK[:, 2560:2624], ALU.max, ALU.add))
            link(dve.tensor_scalar(lf, lf, -1.0, None, ALU.mult))
            DT = WORK[:, 2640:2672]
            link(dve.tensor_copy(DT, dt_))
            link(dve.tensor_scalar(WORK[:, 2624:2640], WORK[:, 2624:2640], -1.0, None, ALU.mult))
            link(dve.tensor_tensor(dt_.rearrange(two, m=2), dt_.rearrange(two, m=2),
                                   WORK[:, 2624:2640].unsqueeze(1).broadcast_to([P, 2, 16]), ALU.mult))
            dve.sem_inc(s["s_a"], 1)
            dve.sem_inc(s["f_lf"], 1)
            XD = BIG[:, 14:16, :].rearrange("p a b -> p (a b)").rearrange("p (m h d) -> p m h d", m=2, h=16)
            for g in range(4):
                m, hh = g // 2, g % 2
                dve.wait_ge(s["s_xt"], g + 1)
                dve.tensor_tensor(XD[:, m, 8 * hh:8 * hh + 8, :],
                                  bank[g % 2][:, :].rearrange("p (h d) -> p h d", h=8),
                                  DT[:, 16 * m + 8 * hh:16 * m + 8 * hh + 8].unsqueeze(2).broadcast_to([P, 8, 64]),
                                  ALU.mult).then_inc(s["s_xd"], 1)
            CB = WORK[:, 2688:3456].rearrange("p (g c) -> p g c", g=2)
            for g in range(2):
                dve.wait_ge(s["s_cb"], g + 1)
                dve.tensor_tensor(CB[:, g, 0:P], bank[2 + g][:, 0:P], LE[:, :], ALU.mult)
                dve.tensor_copy(CB[:, g, P:256], bank[2 + g][:, P:256])
                dve.tensor_tensor(CB[:, g, 256:384], bank[2 + g][:, 256:384], LE[:, :], ALU.mult)\
                    .then_inc(s["s_cbm"], 1)
            dve.wait_ge(s["s_cbm"], 2)
            sE = WORK[:, 768:1536].rearrange("p (b c) -> p b c", b=2)
            sL = WORK[:, 1792:2560].rearrange("p (b c) -> p b c", b=2)
            ZS = BIG[:, 0:2, :].rearrange("p a b -> p (a b)")
            dve.wait_ge(s["masks"], 2)
            for i in range(S_HEADS + 2):
                if i < S_HEADS:
                    h = i
                    dve.wait_ge(s["s_ex"], h + 1)
                    if h >= 2:
                        dve.wait_ge(s["s_y"], h - 1)
                    dve.tensor_tensor(sL[:, h % 2, :], sE[:, h % 2, :], CB[:, h // 8, :], ALU.mult)\
                        .then_inc(s["s_l"], 1)
                if i >= 2 and i % 2 == 1:
                    j = (i - 2) // 2
                    dve.wait_ge(s["s_y"], 2 * j + 2)
                    xs = XBC[:, j * T:(j + 1) * T]
                    link(dve.scalar_tensor_tensor(xs, xs, DSK[:, j:j + 1], bank[j % 2][:, 0:T], ALU.mult, ALU.add))
                    z = ZS[:, j * T:(j + 1) * T]
                    dve.tensor_tensor(z, z, xs, ALU.mult).then_inc(s["s_yg"], 1)
            for g in range(2):
                dve.wait_ge(s["s_rs"], g + 1)
                for j in range(4 * g, 4 * g + 4):
                    c = 32 + j
                    y_wait(c)
                    dve.scalar_tensor_tensor(YB[:, c % 2, :], ZS[:, j * T:(j + 1) * T],
                                             COLS[:, V_SSDN + j:V_SSDN + j + 1], WORK[:, 3456:3712],
                                             ALU.mult, ALU.mult).then_inc(s["y_ready"], 1)
                    y_low(c)

            attend("f_", WORK[:, 768:1536].rearrange("p (b c) -> p b c", b=2), FMASK[:, :], 1.0, None, None, 40)
            phase("two_out")

            norm_low(3)
            phase("peer_q")
            dve.wait_ge(s["q_sc"], 8)
            SC = BIG[:, 6:10, :].rearrange("p (m a) b -> p m (a b)", m=2)
            v16 = WORK[:, 0:256].rearrange("p (f k) -> p f k", k=16)
            i16 = WORK[:, 256:512].bitcast(U32).rearrange("p (f k) -> p f k", k=16)
            if16 = WORK[:, 512:768].rearrange("p (h f k) -> p h f k", f=2, k=16)
            s16 = WORK[:, 768:896].rearrange("p (h k) -> p h k", k=16)
            p16 = WORK[:, 896:1024].bitcast(U32)
            gate = WORK[:, 1024:1280].rearrange("p (m n) -> p m n", m=2)
            pa_u = WORK[:, 1280:1408].bitcast(U32)
            pb_u = WORK[:, 1408:1536].bitcast(U32)
            pa_f, pb_f = WORK[:, 1536:1664], WORK[:, 1664:1792]
            sel = WORK[:, 2048:2560].rearrange("p (m f n) -> p m f n", m=2, f=2)
            gsum = SM[:, 96:104]
            cand = BIG[:, 10:12, :].rearrange("p a b -> p (a b)")
            oh = BIG[:, 12:14, :].rearrange("p a b -> p (a b)").rearrange("p (h k j) -> p h k j", h=8, k=16)
            dve.wait_ge(s["tk_iota"], 1)
            iota = WORK[:, 3840:3968]
            for m in range(MT):
                for f in range(16):
                    x = SC[:, m, f * P:(f + 1) * P]
                    link(dve.max(v16[:, f, 0:8], x))
                    link(dve.max_index(i16[:, f, 0:8], v16[:, f, 0:8], x))
                    link(dve.match_replace(x, v16[:, f, 0:8], x, -3.0e38))
                    link(dve.max(v16[:, f, 8:16], x))
                    link(dve.max_index(i16[:, f, 8:16], v16[:, f, 8:16], x))
                link(dve.tensor_copy(WORK[:, 512:768], WORK[:, 256:512].bitcast(U32)))
                v4 = WORK[:, 0:256].rearrange("p (h f k) -> p h f k", f=2, k=16)
                link(dve.tensor_tensor(cand.rearrange("p (h a b) -> p h a b", h=8, a=16),
                                       v4[:, :, 0, :].unsqueeze(3).broadcast_to([P, 8, 16, 16]),
                                       v4[:, :, 1, :].unsqueeze(2).broadcast_to([P, 8, 16, 16]), ALU.add))
                for h in range(PE_HEADS):
                    x = cand[:, h * 256:(h + 1) * 256]
                    p_ = p16[:, h * 16:(h + 1) * 16]
                    link(dve.max(s16[:, h, 0:8], x))
                    link(dve.max_index(p_[:, 0:8], s16[:, h, 0:8], x))
                    link(dve.match_replace(x, s16[:, h, 0:8], x, -3.0e38))
                    link(dve.max(s16[:, h, 8:16], x))
                    link(dve.max_index(p_[:, 8:16], s16[:, h, 8:16], x))
                dve.tensor_tensor(gate[:, m, :].rearrange("p (h k) -> p h k", k=16), s16,
                                  s16[:, :, 0:1].broadcast_to([P, 8, 16]), ALU.subtract).then_inc(s["tk_e"], 1)
                link(dve.tensor_scalar(pa_u, p16, 4, None, ALU.logical_shift_right))
                link(dve.tensor_scalar(pb_u, p16, 15, None, ALU.bitwise_and))
                link(dve.tensor_copy(pa_f, pa_u))
                link(dve.tensor_copy(pb_f, pb_u))
                for f, pf in enumerate((pa_f, pb_f)):
                    link(dve.tensor_tensor(oh, iota[:, 0:16].unsqueeze(1).unsqueeze(1).broadcast_to([P, 8, 16, 16]),
                                           pf.rearrange("p (h k) -> p h k", k=16).unsqueeze(3).broadcast_to([P, 8, 16, 16]),
                                           ALU.is_equal))
                    link(dve.tensor_tensor(oh, oh, if16[:, :, f, :].unsqueeze(2).broadcast_to([P, 8, 16, 16]), ALU.mult))
                    link(dve.tensor_reduce(sel[:, m, f, :].rearrange("p (h k) -> p h k", k=16), oh, AX.X, ALU.add))
                dve.wait_ge(s["tk_g"], m + 1)
                g3 = gate[:, m, :].rearrange("p (h k) -> p h k", k=16)
                link(dve.tensor_reduce(gsum, g3, AX.X, ALU.add))
                link(dve.reciprocal(gsum, gsum))
                link(dve.tensor_tensor(g3, g3, gsum.unsqueeze(2).broadcast_to([P, 8, 16]), ALU.mult))
                dve.sem_inc(s["tk_idx"], 1)

            dve.wait_ge(s["tk_tc"], 6)
            tkT = WORK[:, 3072:3840].rearrange("p (a t) -> p a t", a=3)
            GB = BIG[:, :, :].rearrange("p a b -> p (a b)").rearrange("p (i t) -> p i t", t=T)
            for half in range(HALVES):
                def one_hot(g, slot, fresh):
                    if not fresh:
                        dve.wait_ge(s["g_mm"], g - 1)
                    t0 = (g - 32 * half) * 8
                    o = WORK[:, 1024 * slot:1024 * (slot + 1)].rearrange("p (t i) -> p t i", t=8)
                    dve.tensor_tensor(o, iota.unsqueeze(1).broadcast_to([P, 8, P]),
                                      tkT[:, 1, bass.ds(t0, 8)].unsqueeze(2).broadcast_to([P, 8, P]),
                                      ALU.is_equal).then_inc(s["oh1"], 1)
                    o = WORK[:, 2048 + 512 * slot:2560 + 512 * slot].rearrange("p (t i) -> p t i", t=8)
                    it = iota[:, half * EXP_ROWS:(half + 1) * EXP_ROWS].unsqueeze(1).broadcast_to([P, 8, EXP_ROWS])
                    dve.tensor_tensor(o, it, tkT[:, 0, bass.ds(t0, 8)].unsqueeze(2).broadcast_to([P, 8, EXP_ROWS]),
                                      ALU.is_equal).then_inc(s["oh_eq"], 1)

                for g in range(2):
                    one_hot(32 * half + g, g, half == 0)
                with dve.Fori(1, 16) as q:
                    for j in range(2):
                        one_hot(2 * q + (32 * half + j), j, False)

                n0 = half * EXP_ROWS

                def rows_low(n, j):
                    for g in range(4):
                        dve.wait_ge(s["t_h"], 4 * n + g + 1)
                        sl = 4 * (j % 2) + g
                        dve.tensor_tensor(WL[:, sl, :], bank[4 + g][:, :], WH[:, sl, :].bitcast(F32), ALU.subtract)\
                            .then_inc(s["t_l"], 1)

                def gated(n, j):
                    dve.wait_ge(s["a_gelu"], n + 1)
                    x = GB[:, bass.ds(n - n0, 1), :].rearrange("p o t -> p (o t)")
                    dve.tensor_tensor(x, x, YB[:, j % 2, :], ALU.mult).then_inc(s["a_p"], 1)

                dve.wait_ge(s["g_free"], 32 * (half + 1))
                rows_low(n0, 0)
                for j in range(1, 4):
                    rows_low(n0 + j, j)
                    gated(n0 + j - 1, j - 1)
                with dve.Fori(1, EXP_ROWS // 4) as q:
                    for j in range(4):
                        rows_low(4 * q + (n0 + j), j)
                        gated(4 * q + (n0 + j - 1), (j + 1) % 2)
                gated(n0 + EXP_ROWS - 1, 1)

                def rows_out_low(n, j):
                    dve.wait_ge(s["p_h"], n + 1)
                    dve.tensor_tensor(PS[:, j % 2, 1, :], GB[:, bass.ds(n - n0, 1), :].rearrange("p o t -> p (o t)"),
                                      PS[:, j % 2, 0, :].bitcast(F32), ALU.subtract).then_inc(s["p_l"], 1)
                    dve.wait_ge(s["v_h"], n + 1)
                    sl = slice(4 * (j % 2), 4 * (j % 2) + 4)
                    dve.tensor_tensor(WL[:, sl, :], RAW[:, j, :].rearrange("p (g n) -> p g n", g=4),
                                      WH[:, sl, :].bitcast(F32), ALU.subtract).then_inc(s["v_l"], 1)

                with dve.Fori(0, EXP_ROWS // 4) as q:
                    for j in range(4):
                        rows_out_low(4 * q + (n0 + j), j)
                dve.wait_ge(s["o_mm"], n0 + EXP_ROWS)
                for m in range(MT):
                    for nn in range(4):
                        x = XR[:, m, nn * NW:(nn + 1) * NW]
                        ins = dve.tensor_tensor(x, x, bank[4 * m + nn][:, :], ALU.add)
                ins.then_inc(s["o_add"], 1)

            dve.wait_ge(s["n_rstd"], 5)
            dve.wait_ge(s["lnf_in"], 16)
            for m in range(MT):
                dve.scalar_tensor_tensor(xn[:, m, :], XR[:, m, :], SM[:, 20 + m:21 + m],
                                         WORK[:, 0:2048], ALU.mult, ALU.mult)\
                    .then_inc(s["n_x"], 1)

        @block.tensor
        def _(pe):
            def mm(dst, lhsT, rhs, start, stop):
                return pe.matmul(dst, lhsT, rhs, start=start, stop=stop, skip_group_check=True)

            def tile(r, i, parity, first):
                t = r["base"] + i
                w = r["width"]
                toks = r["kind"] in ("tok", "res", "gate")
                for sub in range(8):
                    if sub == 0 and (r["base"] >= 2 or i >= 2):
                        pe.wait_ge(s["tile_free"], t - 1)
                    pe.wait_ge(s["wl_done"], 8 * t + sub + 1)
                    for kk in range(2):
                        kt = 2 * sub + kk
                        sl = 2 * (sub % 4) + kk
                        last = kt == KT - 1
                        if toks:
                            for m in range(MT):
                                ms = slice(m * P, (m + 1) * P)
                                dst = bank[2 * parity + m][:, 0:w]
                                mm(dst, HH[:, kt, ms], WH[:, sl, 0:w], kt == 0, False)
                                mm(dst, HL[:, kt, ms], WH[:, sl, 0:w], False, False)
                                ins = mm(dst, HH[:, kt, ms], WL[:, sl, 0:w], False, last)
                        else:
                            for c in range(4):
                                cs = slice(c * P, (c + 1) * P)
                                dst = bank[2 * parity + c // 2][:, (c % 2) * T:(c % 2 + 1) * T]
                                mm(dst, WH[:, sl, cs], HH[:, kt, :], kt == 0 and c % 2 == 0, False)
                                mm(dst, WH[:, sl, cs], HL[:, kt, :], False, False)
                                ins = mm(dst, WL[:, sl, cs], HH[:, kt, :], False, last)
                    ins.then_inc(s["ws_used"], 1)

            xn = BIG[:, 0:4, :].rearrange("p (m a) b -> p m (a b)", m=2)

            def norm_t(n):
                pe.wait_ge(s["n_x"], 2 * n + 2)
                for g in range(8):
                    if g >= 4:
                        pe.wait_ge(s["n_l"], 16 * n + 2 * (g - 3))
                    for kk in range(2):
                        for m in range(MT):
                            c0 = (2 * g + kk) * P
                            ins = pe.transpose(bank[4 + g % 4][:, kk * T + m * P:kk * T + (m + 1) * P],
                                               xn[:, m, c0:c0 + P], ID[:, :])
                    ins.then_inc(s["n_t"], 1)
                pe.wait_ge(s["n_l"], 16 * n + 16)

            def phase(name):
                over_tiles(pe, name, tile)
                pe.wait_ge(s["tile_free"], last_tile(name) + 1)

            pe.wait_ge(s["masks"], 1)
            pe.wait_ge(s["vec_in"], 16 * N_VEC)
            pe.transpose(bank[0][:, 0:V_ROWS], WORK[0:V_ROWS, 0:P], ID[0:V_ROWS, 0:V_ROWS])
            pe.transpose(bank[0][:, V_ROWS:V_ROWS + 48], WORK[0:48, P:2 * P], ID[0:48, 0:48]).then_inc(s["vec_t"], 1)
            pe.wait_ge(s["cols_set"], 1)
            norm_t(0)
            phase("even_in")

            pe.wait_ge(s["masks"], 2)
            pe.wait_ge(s["aq_ready"], 3)
            q_t = BIG[:, 0:2, :].rearrange("p a b -> p (a b)")
            kd = WORK[:, 3584:4096].rearrange("p (m g c) -> p m g c", m=2, g=2)
            for g in range(5):
                if g == 4:
                    pe.wait_ge(s["qk_c"], 1)
                for kk in range(2):
                    for m in range(MT):
                        if g < 4:
                            pair = 2 * g + kk
                            o = (pair // 4) * 1024 + m * 512 + (pair % 4) * P
                            src = q_t[:, o:o + P]
                        else:
                            src = kd[:, m, kk, :]
                        ins = pe.transpose(bank[4 + g % 4][:, kk * T + m * P:kk * T + (m + 1) * P], src, ID[:, :])
                ins.then_inc(s["qk_t"], 1)
            pe.wait_ge(s["qk_c"], 5)
            qT = WORK[:, 0:2048].rearrange("p (k t) -> p k t", k=8)
            kT = WORK[:, 2048:2560].rearrange("p (k t) -> p k t", k=2)

            def attend(p, score, probs, pt, value, c0):
                for i in range(16 + 2):
                    if i < 16:
                        h = i
                        if h >= 2:
                            pe.wait_ge(s[p + "soft"], h - 1)
                        score(h, bank[4 + h % 2]).then_inc(s[p + "score"], 1)
                    if 1 <= i <= 16:
                        h = i - 1
                        pe.wait_ge(s[p + "pn"], h + 1)
                        if h >= 2:
                            pe.wait_ge(s[p + "ptc"], h - 1)
                        for b in range(3):
                            ins = pe.transpose(bank[6 + h % 2][:, b * P:(b + 1) * P],
                                               probs[:, h % 2, b * P:(b + 1) * P], ID[:, :])
                        ins.then_inc(s[p + "pt"], 1)
                    if i >= 2:
                        h = i - 2
                        j = h // 2
                        pe.wait_ge(s[p + "ptc"], h + 1)
                        if j >= 2:
                            pe.wait_ge(s["y_ready"], c0 + j - 1)
                        o = bank[j % 2][64 * (h % 2):64 * (h % 2) + 64, :]
                        mm(o[:, 0:T], value(h, 0), pt[:, h % 2, 0:T], True, False)
                        mm(o[:, P:T], value(h, 1), pt[:, h % 2, T:384], False, True).then_inc(s[p + "pv"], 1)

            def a_score(h, ps):
                r = slice(64 * (h % 2), 64 * (h % 2) + 64)
                q, k = qT[r, h // 2, :], kT[r, h // 8, :]
                mm(ps[:, 0:P], q[:, 0:P], k[:, 0:P], True, True)
                return mm(ps[:, P:384], q[:, P:T], k[:, 0:T], True, True)

            def a_value(h, m):
                o = m * 512 + P + 64 * (h // 8)
                return BIG[:, 2, o:o + 64]

            attend("a_", a_score, BIG[:, 0, 0:768].rearrange("p (b c) -> p b c", b=2),
                   BIG[:, 1, 0:768].rearrange("p (b c) -> p b c", b=2), a_value, 0)

            lgf = BIG[:, 0:2, :].rearrange("p a b -> p (a b)")
            msf = MS.rearrange("p l i -> p (l i)")
            qe = WORK[:, 1024:2048].rearrange("p (l i) -> p l i", l=8)
            ke = WORK[:, 2048:3072].rearrange("p (l i) -> p l i", l=8)
            am = WORK[:, 3072:4096].rearrange("p (l i) -> p l i", l=8)
            pe.wait_ge(s["b_x"], 2)
            pe.wait_ge(s["y_ready"], 8)

            def level_sums(u):
                h, m = u // 2, u % 2
                if u >= 1:
                    pe.wait_ge(s["b_lf"], u)
                pe.transpose(bank[4][:, m * P:(m + 1) * P], lgf[:, h * T + m * P:h * T + (m + 1) * P], ID[:, :])\
                    .then_inc(s["b_lt"], 1)
                pe.wait_ge(s["b_lf"], u + 1)
                if u >= 1:
                    pe.wait_ge(s["b_ex"], u)
                mm(bank[0][:, :], LFT[:, m, :], msf[:, 0:512], True, True)
                mm(bank[1][:, 0:384], LFT[:, m, :], msf[:, 512:896], True, True)
                mm(bank[1][:, 384:512], LFT[:, m, :], (GT if m == 0 else LE)[:, :], True, True)\
                    .then_inc(s["b_es"], 1)

            def values(u):
                h, m = u // 2, u % 2
                ts = slice(m * P, (m + 1) * P)
                o = bank[5 + 2 * (h % 2)]
                pe.wait_ge(s["b_am"], u + 1)
                if m == 0 and h >= 2:
                    pe.wait_ge(s["y_ready"], 8 + h - 1)
                v = BIG[:, 9 + h // 4, m * 512 + (h % 4) * P:m * 512 + (h % 4 + 1) * P]
                for l in range(8):
                    ins = mm(o[:, ts], v, am[:, l, :], l == 0, l == 7 and m == 0)
                ins.then_inc(s["b_lev"], 1)
                if m == 1:
                    pe.wait_ge(s["b_cx"], h + 1)
                    v0 = BIG[:, 9 + h // 4, (h % 4) * P:(h % 4 + 1) * P]
                    mm(o[:, ts], v0, CX, False, True).then_inc(s["b_ov"], 1)

            def products(u):
                h, m = u // 2, u % 2
                ts = slice(m * P, (m + 1) * P)
                pe.wait_ge(s["b_qe"], u + 1)
                pe.wait_ge(s["b_ke"], u + 1)
                if u >= 1:
                    pe.wait_ge(s["b_am"], u)
                for l in range(8):
                    dst = bank[2 + l // 4][:, (l % 4) * P:(l % 4 + 1) * P]
                    if l < LEVELS:
                        ins = mm(dst, ke[:, l, :], qe[:, l, :], True, True)
                    else:
                        ins = mm(dst, chan(7, h)[:, ts], chan(5, h)[:, ts], True, True)
                ins.then_inc(s["b_att"], 1)
                if m == 1:
                    pe.wait_ge(s["b_kx"], h + 1)
                    if h >= 1:
                        pe.wait_ge(s["b_cx"], h)
                    mm(bank[6][:, 0:P], KX, qe[:, 7, :], True, True).then_inc(s["b_cross"], 1)

            def square_sums(h):
                pe.wait_ge(s["b_sq"], h + 1)
                if h >= 1:
                    pe.wait_ge(s["b_rs"], h)
                mm(bank[5 + 2 * (h % 2)][:, T:2 * T], ONES[:, :], BSQ, True, True).then_inc(s["b_ss"], 1)

            for i in range(2 * B_HEADS + 4):
                if i < 2 * B_HEADS:
                    level_sums(i)
                if 0 <= i - 2 < 2 * B_HEADS:
                    values(i - 2)
                if 0 <= i - 1 < 2 * B_HEADS:
                    products(i - 1)
                if i >= 4 and i % 2 == 0:
                    square_sums((i - 4) // 2)
            pe.wait_ge(s["y_l"], 16)
            phase("even_out")

            norm_t(1)
            phase("odd_in")
            cS = WORK[:, 768:1536].rearrange("p (b c) -> p b c", b=2)
            cW = WORK[:, 1536:2304].rearrange("p (b c) -> p b c", b=2)
            for i in range(C_HEADS + 2):
                if i < C_HEADS:
                    h = i
                    ps = bank[4 + h % 2]
                    q, k = chan(0, h), chan(4, h)
                    if h >= 2:
                        pe.wait_ge(s["c_min"], h - 1)
                    mm(ps[:, 0:T], k[:, 0:P], q, True, True)
                    mm(ps[:, T:384], k[:, P:T], q[:, P:T], False, True).then_inc(s["c_z"], 1)
                if 1 <= i <= C_HEADS:
                    h = i - 1
                    ps = bank[4 + h % 2]
                    sp_ = cS[:, h % 2, :]
                    pe.wait_ge(s["c_sp"], 2 * (h + 1))
                    mm(ps[:, 0:384], NTRI[:, :], sp_, False, True)
                    mm(ps[:, P:T], NONES[:, :], sp_[:, T:384], False, True).then_inc(s["c_e"], 1)
                if i >= 2:
                    h = i - 2
                    pe.wait_ge(s["c_w"], h + 1)
                    if h >= 2:
                        pe.wait_ge(s["y_ready"], 16 + h - 1)
                    o = bank[6 + h % 2]
                    w = cW[:, h % 2, :]

                    def v(m):
                        return BIG[:, 8 + h // 4, m * 512 + (h % 4) * P:m * 512 + (h % 4 + 1) * P]

                    mm(o[:, 0:T], v(0), w[:, 0:T], True, False)
                    mm(o[:, P:T], v(1), w[:, T:384], False, True).then_inc(s["c_pv"], 1)
            pe.wait_ge(s["y_l"], 32)
            phase("odd_out")

            norm_t(2)
            phase("two_in")
            XBC = BIG[:, 11:14, :].rearrange("p a b -> p (a b)")
            pe.wait_ge(s["s_xbc"], 3)
            for g in range(4):
                m, hh = g // 2, g % 2
                if g >= 2:
                    pe.wait_ge(s["s_xd"], g - 1)
                for j in range(4):
                    k = 4 * hh + j
                    ins = pe.transpose(bank[g % 2][:, j * P:(j + 1) * P],
                                       XBC[:, k * T + m * P:k * T + (m + 1) * P], ID[:, :])
                ins.then_inc(s["s_xt"], 1)
            for g in range(2):
                B, C = XBC[:, (8 + g) * T:(9 + g) * T], XBC[:, (10 + g) * T:(11 + g) * T]
                mm(bank[2 + g][:, 0:T], B[:, 0:P], C, True, True)
                mm(bank[2 + g][:, T:384], B[:, P:T], C[:, P:T], False, True).then_inc(s["s_cb"], 1)
            XD = BIG[:, 14:16, :].rearrange("p a b -> p (a b)").rearrange("p (m h d) -> p m h d", m=2, h=16)
            ag = WORK[:, 0:768].rearrange("p (b c) -> p b c", b=2)
            sL = WORK[:, 1792:2560].rearrange("p (b c) -> p b c", b=2)
            pe.wait_ge(s["s_xd"], 4)
            for i in range(S_HEADS + 1):
                if i < S_HEADS:
                    h = i
                    g = ag[:, h % 2, :]
                    ps = bank[4 + h % 2]
                    pe.wait_ge(s["s_ag"], h + 1)
                    if h >= 2:
                        pe.wait_ge(s["s_ex"], h - 1)
                    mm(ps[:, 0:P], g[:, 0:P], LE[:, :], True, False)
                    mm(ps[:, P:T], g[:, 0:P], ONES[:, :], False, False)
                    mm(ps[:, P:T], g[:, P:T], LE[:, :], False, False)
                    mm(ps[:, T:384], g[:, T:384], LE[:, :], False, True).then_inc(s["s_seg"], 1)
                if i >= 1:
                    h = i - 1
                    j = h // 2
                    pe.wait_ge(s["s_l"], h + 1)
                    if j >= 2:
                        pe.wait_ge(s["s_yg"], j - 1)
                    o = bank[j % 2][64 * (h % 2):64 * (h % 2) + 64, :]
                    mm(o[:, 0:T], XD[:, 0, h, :], sL[:, h % 2, 0:T], True, False)
                    mm(o[:, P:T], XD[:, 1, h, :], sL[:, h % 2, T:384], False, True).then_inc(s["s_y"], 1)
            SQ = WORK[:, 768:1792].rearrange("p (j t) -> p j t", j=4)
            for g in range(2):
                pe.wait_ge(s["s_sq"], g + 1)
                if g == 1:
                    pe.wait_ge(s["s_rs"], 1)
                for j in range(4):
                    ins = mm(bank[6][:, 0:T], ONES[:, :], SQ[:, j, :], j == 0, j == 3)
                ins.then_inc(s["s_ss"], 1)

            lg = WORK[:, 0:768].rearrange("p (b c) -> p b c", b=2)
            pe.wait_ge(s["y_ready"], 40)
            pe.wait_ge(s["s_rs"], 2)

            def f_score(h, ps):
                r = slice(64 * (h % 2), 64 * (h % 2) + 64)
                q, k = chan(5, h // 2)[r, :], chan(7, h // 2)[r, :]
                g = lg[:, h % 2, :]
                pe.wait_ge(s["f_lg"], h + 1)
                mm(ps[:, 0:P], q[:, 0:P], k[:, 0:P], True, False)
                mm(ps[:, P:384], q[:, P:T], k, False, False)
                mm(ps[:, 0:P], LE[:, :], g[:, 0:P], False, False)
                mm(ps[:, P:T], ONES[:, :], g[:, 0:P], False, False)
                return mm(ps[:, P:384], LE[:, :], g[:, P:384], False, True)

            def f_value(h, m):
                o = m * 512 + (h % 8) * 64
                return BIG[:, 9 + h // 8, o:o + 64]

            attend("f_", f_score, WORK[:, 1536:2304].rearrange("p (b c) -> p b c", b=2),
                   WORK[:, 2304:3072].rearrange("p (b c) -> p b c", b=2), f_value, 40)
            pe.wait_ge(s["y_l"], 48)
            phase("two_out")

            norm_t(3)
            phase("peer_q")
            keys = RAW[:, 0, :].rearrange("p (f d) -> p f d", f=16)
            kTp = BIG[:, 4:6, :].rearrange("p a b -> p (a b)").rearrange("p (f d) -> p f d", f=16)
            pe.wait_ge(s["k_in"], 32)
            for g in range(4):
                for j in range(4):
                    ins = pe.transpose(bank[4 + g][:, j * P:(j + 1) * P], keys[:, 4 * g + j, :], ID[:, :])
                ins.then_inc(s["k_t"], 1)
            pe.wait_ge(s["k_c"], 4)
            for g in range(8):
                m = g // 4
                if g >= 4:
                    pe.wait_ge(s["q_sc"], g - 3)
                for j in range(4):
                    f = 4 * (g % 4) + j
                    ins = mm(bank[g % 4][:, j * P:(j + 1) * P], chan(0, f)[:, m * P:(m + 1) * P], kTp[:, f, :],
                             True, True)
                ins.then_inc(s["q_s"], 1)
            sel = WORK[:, 2048:2560].rearrange("p (m f n) -> p m f n", m=2, f=2)
            gate = WORK[:, 1024:1280].rearrange("p (m n) -> p m n", m=2)
            for m in range(MT):
                pe.wait_ge(s["tk_idx"], m + 1)
                for f in range(3):
                    n = 3 * m + f
                    if n >= 2:
                        pe.wait_ge(s["tk_tc"], n - 1)
                    src = sel[:, m, f, :] if f < 2 else gate[:, m, :]
                    pe.transpose(bank[4 + n % 2][:, 0:P], src, ID[:, :]).then_inc(s["tk_t"], 1)
            pe.wait_ge(s["tk_tc"], 6)

            for half in range(HALVES):
                def spread(g, slot, fresh):
                    pe.wait_ge(s["oh1"], g + 1)
                    pe.wait_ge(s["oh2"], g + 1)
                    if not fresh:
                        pe.wait_ge(s["g_free"], g - 1)
                    for t in range(8):
                        ins = mm(bank[4 + slot][:, t * EXP_ROWS:(t + 1) * EXP_ROWS],
                                 WORK[:, 1024 * slot + t * P:1024 * slot + (t + 1) * P],
                                 WORK[:, 2048 + 512 * slot + t * EXP_ROWS:2048 + 512 * slot + (t + 1) * EXP_ROWS],
                                 True, True)
                    ins.then_inc(s["g_mm"], 1)

                if half == 1:
                    pe.wait_ge(s["o_add"], 1)
                spread(32 * half, 0, half == 0)
                spread(32 * half + 1, 1, half == 0)
                with pe.Fori(1, 16) as q:
                    for j in range(2):
                        spread(2 * q + (32 * half + j), j, False)
                pe.wait_ge(s["g_free"], 32 * (half + 1))

                n0 = half * EXP_ROWS

                def turn(n, j, g, fresh, full):
                    if g == 0:
                        pe.wait_ge(s[f"u_full{j}"], full)
                    if not fresh:
                        pe.wait_ge(s["t_l"], 4 * n + (g - 3))
                    for b in range(4):
                        c0 = (4 * g + b) * P
                        ins = pe.transpose(bank[4 + g][:, b * P:(b + 1) * P], RAW[:, j, c0:c0 + P], ID[:, :])
                    ins.then_inc(s["t_t"], 1)

                def products(n, j, g, fresh):
                    if g == 0 and not fresh:
                        pe.wait_ge(s["a_gelu"], n - 1)
                    pe.wait_ge(s["t_l"], 4 * n + g + 1)
                    for b in range(4):
                        kt = 4 * g + b
                        sl, cs = 4 * (j % 2) + g, slice(b * P, (b + 1) * P)
                        dst = bank[j % 2][:, 0:T]
                        mm(dst, WH[:, sl, cs], HH[:, kt, :], kt == 0, False)
                        mm(dst, WH[:, sl, cs], HL[:, kt, :], False, False)
                        ins = mm(dst, WL[:, sl, cs], HH[:, kt, :], False, kt == KT - 1)
                    ins.then_inc(s["u_used"], 1)

                for g in range(4):
                    turn(n0, 0, g, True, 16 * (n0 // 4 + 1))
                for j in range(1, 4):
                    for g in range(4):
                        turn(n0 + j, j, g, False, 16 * (n0 // 4 + 1))
                        products(n0 + j - 1, j - 1, g, half == 0 and j <= 2)
                with pe.Fori(1, EXP_ROWS // 4) as q:
                    for j in range(4):
                        for g in range(4):
                            turn(4 * q + (n0 + j), j, g, False, 16 * q + 16 * (n0 // 4 + 1))
                            products(4 * q + (n0 + j - 1), (j + 3) % 4, g, False)
                for g in range(4):
                    products(n0 + EXP_ROWS - 1, 3, g, False)

                def outputs(n, j, start):
                    pe.wait_ge(s["p_l"], n + 1)
                    pe.wait_ge(s["v_l"], n + 1)
                    for m in range(MT):
                        ms = slice(m * P, (m + 1) * P)
                        for nn in range(4):
                            sl = 4 * (j % 2) + nn
                            dst = bank[4 * m + nn][:, :]
                            mm(dst, PS[:, j % 2, 0, ms], WH[:, sl, :], start, False)
                            mm(dst, PS[:, j % 2, 1, ms], WH[:, sl, :], False, False)
                            ins = mm(dst, PS[:, j % 2, 0, ms], WL[:, sl, :], False, False)
                    ins.then_inc(s["o_mm"], 1)

                pe.wait_ge(s["a_gelu"], n0 + EXP_ROWS)
                for j in range(4):
                    outputs(n0 + j, j, j == 0)
                with pe.Fori(1, EXP_ROWS // 4) as q:
                    for j in range(4):
                        outputs(4 * q + (n0 + j), j, False)


_INS = ["x", "ln_even", "w_in_even", "q_norm_a", "k_norm_a", "sinks_a", "lower_bounds", "g_norm_b",
        "w_out_even", "ln_odd", "w_in_odd", "w_out_odd", "ln1_w_2", "w_in_2", "conv_w_2", "conv_b_2",
        "dt_bias_2", "a_log_2", "d_skip_2", "ssd_norm_w_2", "fox_f_bias_2", "w_out_2", "ln2_w_2",
        "peer_wq_2", "peer_k1_2", "peer_k2_2", "peer_u_2", "peer_v_2", "lnf_w_2"]
_LAYERED = ("w_in_even", "w_out_even", "w_in_odd", "w_out_odd")


def rope_tables():
    half = A_HD // 2
    inv = (1.0 / (np.float32(10000.0) ** (np.arange(half, dtype=np.float32) / np.float32(half)))).astype(np.float32)
    ang = np.arange(T, dtype=np.float32)[:, None] * inv[None, :]
    return np.cos(ang), np.sin(ang)


def kernel(**inputs):
    import concourse.bacc as _bacc
    from concourse.bass_utils import run_bass_kernel_spmd as _run

    nc = _bacc.Bacc("TRN2", target_bir_lowering=False, num_devices=1)
    arrays, args = {}, {}
    cos, sin = rope_tables()
    for name in _INS + ["rope_cos", "rope_sin"]:
        v = cos if name == "rope_cos" else sin if name == "rope_sin" else np.ascontiguousarray(inputs[name])
        arrays[f"in_{name}_dram"] = v
        ap = nc.dram_tensor(f"in_{name}_dram", v.shape, mybir.dt.from_np(v.dtype), kind="ExternalInput").ap()
        args[name] = ap[0] if name in _LAYERED else ap
    out = nc.dram_tensor("out_0_dram", (1, T, D), F32, kind="ExternalOutput").ap()
    two_blocks(nc, args, out)
    r = _run(nc, [arrays], core_ids=[0])
    return r.results[0]["out_0_dram"]
```

```python
from contextlib import ExitStack

import numpy as np

import concourse.bass as bass
from concourse import mybir

F32 = mybir.dt.float32
F32R = mybir.dt.float32r
U32 = mybir.dt.uint32
BF16 = mybir.dt.bfloat16
ALU = mybir.AluOpType
ACT = mybir.ActivationFunctionType
AX = mybir.AxisListType

P = 128
T = 256
MT = T // P
D = 2048
KT = D // P
NW = 512
EPS = 1e-6
NEG = -1e30
LN2 = 0.6931471805599453

A_HEADS, A_KV, A_HD = 16, 2, 64
B_HEADS, B_HD = 8, 128
C_HEADS, C_HD = 16, 128
S_HEADS, S_HD, S_STATE = 16, 64, 128
F_HEADS, F_HD = 16, 64
LEVELS = 7
PE_HEADS, PE_KEYS, PE_TOP = 8, 128, 16
QUARTERS = 4
QR = PE_KEYS // QUARTERS
TG = 8
SEGMENTS = [("in", 0), ("in", 1), ("out", 0), ("in", 2), ("out", 1), ("in", 3), ("out", 2), ("out", 3)]

V_LN = 0
V_SSDN = 64
V_CB = 72
V_LB = 84
V_GN = 92
V_ROWS = 93
V_CW = 93
V_COLS = V_CW + 48


def runs():
    out = []
    base = 0
    for phase, rs in (
        ("even_in", [("w_in_even", 0, 512, 2, "tok", 0), ("w_in_even", 1024, 256, 1, "tok", 2),
                     ("w_in_even", 1280, 512, 4, "silu", 3), ("w_in_even", 3328, 512, 2, "chan", 7),
                     ("w_in_even", 4352, 512, 2, "tok", 9), ("w_in_even", 5376, 512, 2, "silu", 11)]),
        ("even_out", [("w_out_even", 0, 512, 4, "res", 0)]),
        ("odd_in", [("w_in_odd", 0, 512, 4, "scaled", 0), ("w_in_odd", 2048, 512, 4, "chan", 4),
                    ("w_in_odd", 4096, 512, 4, "tok", 8), ("w_in_odd", 6144, 512, 4, "silu", 12)]),
        ("odd_out", [("w_out_odd", 0, 512, 4, "res", 0)]),
        ("two_in", [("w_in_2", 0, 512, 2, "silu", 0), ("w_in_2", 1024, 512, 3, "chan", 2),
                    ("w_in_2", 2560, 16, 1, "gate", 0), ("w_in_2", 2576, 512, 2, "eighth", 5),
                    ("w_in_2", 3600, 512, 2, "chan", 7), ("w_in_2", 4624, 512, 2, "tok", 9),
                    ("w_in_2", 5648, 16, 1, "gate", 1)]),
        ("two_out", [("w_out_2", 0, 512, 4, "res", 0)]),
        ("peer_q", [("peer_wq_2", 0, 512, 4, "chan", 0)]),
    ):
        for w, c0, width, n, kind, dest in rs:
            out.append(dict(phase=phase, w=w, c0=c0, width=width, n=n, kind=kind, dest=dest, base=base))
            base += n
    return out


RUNS = runs()
PHASES = ["even_in", "even_out", "odd_in", "odd_out", "two_in", "two_out", "peer_q"]


def last_tile(phase):
    return max(r["base"] + r["n"] for r in RUNS if r["phase"] == phase) - 1


N_TILES = last_tile("peer_q") + 1


def over_tiles(eng, phase, body):
    for r in [r for r in RUNS if r["phase"] == phase]:
        body(r, 0, r["base"] % 2, True)
        pairs = (r["n"] - 1) // 2
        if pairs > 1:
            with eng.Fori(0, pairs) as q:
                for j in range(2):
                    body(r, 2 * q + (1 + j), (r["base"] + 1 + j) % 2, False)
        else:
            for i in range(1, 1 + 2 * pairs):
                body(r, i, (r["base"] + i) % 2, False)
        for i in range(1 + 2 * pairs, r["n"]):
            body(r, i, (r["base"] + i) % 2, False)


class Chain:

    def __init__(self, eng, sem):
        self.eng, self.sem, self.n = eng, sem, 0

    def link(self, ins):
        self.n += 1
        ins.then_inc(self.sem, 1)
        self.eng.wait_ge(self.sem, self.n)


def two_blocks(nc, a, out):
    ctx = ExitStack()
    with ctx:
        def sb(name, shape, dt=F32):
            return ctx.enter_context(nc.sbuf_tensor(name, shape, dt))

        def sem(name):
            return ctx.enter_context(nc.semaphore(name))

        HH = sb("HH", [P, KT, T], F32R)
        HL = sb("HL", [P, KT, T], F32R)
        WH = sb("WH", [P, 8, NW], F32R)
        WL = sb("WL", [P, 8, NW], F32R)
        PS = sb("PS", [P, 2, 2, T], F32R)
        RAW = sb("RAW", [P, 4, 2048])
        XR = sb("XR", [P, MT, D])
        BIG = sb("BIG", [P, 16, 1024])
        WORK = sb("WORK", [P, 4096])
        YB = sb("YB", [P, 2, T])
        ID = sb("ID", [P, P])
        LE = sb("LE", [P, P])
        GT = sb("GT", [P, P])
        ONES = sb("ONES", [P, P])
        NTRI = sb("NTRI", [P, P])
        NONES = sb("NONES", [P, P])
        AMASK = sb("AMASK", [P, 384])
        FMASK = sb("FMASK", [P, 384])
        COLS = sb("COLS", [P, V_COLS])
        ROPE = sb("ROPE", [P, 2, MT, 32])
        BC = sb("BC", [P, 208])
        SM = sb("SM", [P, 160])
        DTF = sb("DTF", [P, 2, MT, 16])
        bank = [ctx.enter_context(nc.psum_tensor(f"bank{i}", [P, 512], F32)) for i in range(8)]

        names = """
            const_in vec_in masks vec_t cols_set x_in lnf_in out_done eps_set act_chain dve_chain pool_chain
            w_full0 w_full1 w_full2 w_full3 wh_done wl_done ws_used tile_free
            n_rstd n_x n_t n_h n_l y_ready y_h y_l
            aq_ready qk_t qk_c
            a_score a_soft a_exp a_rcp a_pn a_pt a_ptc a_pv
            f_score f_soft f_exp f_rcp f_pn f_pt f_ptc f_pv f_lg f_lf
            b_vec b_e b_lsg b_kin b_x b_ml b_lt b_lf b_es b_ex b_qe b_ke b_att b_am b_cross b_cx b_kx b_lev b_ov
            b_sq b_ss b_rs
            c_mask c_z c_exp c_sp c_e c_min c_w c_pv
            s_dt s_e s_a s_conv s_xbc s_xt s_xd s_cb s_cbm s_ag s_seg s_ex s_l s_y s_yg s_sq s_ss s_rs
            k_in k_t k_c q_s q_sc tk_iota tk_idx tk_e tk_g tk_t tk_tc tk_parts oh1 oh2 ohg g_mm g_mul
            row_full0 row_full1 row_full2 row_full3 u_used t_t t_h t_l a_gelu p_h p_l v_h v_l o_mm o_add
            """.split()
        s = {n: sem(n) for n in names}

        A_QN, A_KN, A_SINK, S_DTB, S_AL, F_FB, S_DSK, S_DSKC = 0, 64, 128, 144, 160, 176, 192, 152
        DSK = SM[:, 0:8]
        bq, bf, bi, bg = BIG[:, 5:7, :], BIG[:, 7:9, :], BIG[:, 9:11, :], BIG[:, 11:13, :]
        even_spare = BIG[:, 13:16, :].rearrange("p a b -> p (a b)")
        MS = even_spare[:, 0:LEVELS * P].rearrange("p (l i) -> p l i", l=LEVELS)
        MK = even_spare[:, 896:896 + 1024].rearrange("p (l i) -> p l i", l=8)
        KX = even_spare[:, 1920:2048]
        CX = even_spare[:, 2048:2176]
        LFT = even_spare[:, 2176:2432].rearrange("p (b c) -> p b c", b=2)
        BSQ = even_spare[:, 2432:2688]
        BRS = even_spare[:, 2688:2944]
        CM = WORK[:, 3072:3456]
        CN = WORK[:, 3456:3840]

        def chan(tile0, kt):
            return BIG[:, tile0 + kt // 4, (kt % 4) * T:(kt % 4 + 1) * T]

        GB = [BIG[:, 8 * b:8 * b + 8, :].rearrange("p a b -> p (a b)").rearrange("p (i t) -> p i t", t=T)
              for b in range(2)]
        OH2 = WORK[:, 0:1024].bitcast(BF16).rearrange("p (b t i) -> p b t i", b=2, t=TG)
        OHG = WORK[:, 1024:1792].bitcast(BF16).rearrange("p (b c t i) -> p b c t i", b=2, c=3, t=TG)
        OH1 = WORK[:, 1792:2048].bitcast(BF16).rearrange("p (b t i) -> p b t i", b=2, t=TG)
        SEL = WORK[:, 2048:2560].rearrange("p (m f n) -> p m f n", m=2, f=2)
        G3 = WORK[:, 2560:2944].bitcast(BF16).rearrange("p (c t) -> p c t", c=3)
        TKT = WORK[:, 3072:3840].rearrange("p (a t) -> p a t", a=3)
        IOTA = WORK[:, 3840:3968]

        block = ctx.enter_context(nc.Block())

        @block.sync
        def _(sp):
            def load_tile(r, i, parity, first):
                t = r["base"] + i
                w = a[r["w"]]
                src = w.rearrange("(k p) n -> p k n", p=P)
                for j in range(4):
                    if r["base"] > 0 or not first:
                        sp.wait_ge(s["wl_done"], 8 * (t - 1) + 2 * (j + 1))
                    dst = RAW[:, j, :].rearrange("p (k n) -> p k n", k=4)[:, :, 0:r["width"]]
                    c = bass.ds(r["c0"] + i * r["width"], r["width"])
                    sp.dma_start(dst, src[:, 4 * j:4 * j + 4, c]).then_inc(s[f"w_full{j}"], 16)

            for ph in PHASES:
                over_tiles(sp, ph, load_tile)

            sp.wait_ge(s["wl_done"], 8 * N_TILES)
            keys = RAW[:, 0, :].rearrange("p (h f d) -> p h f d", h=PE_HEADS, f=2)
            for f, name in enumerate(("peer_k1_2", "peer_k2_2")):
                sp.dma_start(keys[:, :, f, :], a[name].rearrange("h n d -> n h d")).then_inc(s["k_in"], 16)

            u_rows = a["peer_u_2"].rearrange("(i j) d -> i j d", j=PE_KEYS)
            v_rows = a["peer_v_2"].rearrange("(i j) d -> i j d", j=PE_KEYS)

            def load_rows(kind, n, j):
                sp.dma_start(RAW[:, j, :], (u_rows if kind == "in" else v_rows)[n, :, :])\
                    .then_inc(s[f"row_full{j}"], 16)

            def wait_split(kind, tiles):
                sp.wait_ge(s["t_l" if kind == "in" else "v_l"], tiles * (4 if kind == "in" else 1))

            for seg, (kind, k) in enumerate(SEGMENTS):
                n0 = QR * k
                for j in range(4):
                    if seg == 0:
                        if j == 0:
                            sp.wait_ge(s["k_t"], 4)
                    else:
                        before, kb = SEGMENTS[seg - 1]
                        wait_split(before, QR * (kb + 1) - 3 + j)
                    load_rows(kind, n0 + j, j)
                with sp.Fori(1, QR // 4) as q:
                    for j in range(4):
                        wait_split(kind, 4 * q + (n0 + j - 3))
                        load_rows(kind, 4 * q + (n0 + j), j)

            for m in range(MT):
                sp.wait_ge(s["n_x"], 9 + m)
                sp.dma_start(out[0].rearrange("(m p) d -> p m d", p=P)[:, m, :],
                             BIG[:, 2 * m:2 * m + 2, :].rearrange("p a b -> p (a b)")).then_inc(s["out_done"], 16)
            sp.wait_ge(s["out_done"], 16 * MT)

        N_CONST = 9
        N_VEC = 12

        @block.gpsimd
        def _(pool):
            ch = Chain(pool, s["pool_chain"])
            link = ch.link
            pool.dma_start(XR[:, :, :], a["x"][0].rearrange("(m p) d -> p m d", p=P)).then_inc(s["x_in"], 16)
            vec, vecw = WORK[:, 0:P], WORK[:, P:2 * P]
            row = 0
            for name, n in (("ln_even", 16), ("ln_odd", 16), ("ln1_w_2", 16), ("ln2_w_2", 16),
                            ("ssd_norm_w_2", 8), ("conv_b_2", 12), ("lower_bounds", 8), ("g_norm_b", 1)):
                v = a[name]
                if name in ("ln_even", "ln_odd", "lower_bounds", "g_norm_b"):
                    v = v[0]
                pool.dma_start(vec[row:row + n, :], v.rearrange("(k p) -> k p", p=P)).then_inc(s["vec_in"], 16)
                row += n
            for tap in range(4):
                pool.dma_start(vecw[12 * tap:12 * tap + 12, :],
                               a["conv_w_2"][tap].rearrange("(k p) -> k p", p=P)).then_inc(s["vec_in"], 16)
            for name, at, n in (("q_norm_a", A_QN, 64), ("k_norm_a", A_KN, 64), ("sinks_a", A_SINK, 16),
                                ("dt_bias_2", S_DTB, 16), ("a_log_2", S_AL, 16), ("fox_f_bias_2", F_FB, 16),
                                ("d_skip_2", S_DSK, 16)):
                v = a[name][0] if name in ("q_norm_a", "k_norm_a", "sinks_a") else a[name]
                pool.dma_start(BC[:, at:at + n], v.partition_broadcast(P)).then_inc(s["const_in"], 16)
            for i, name in enumerate(("rope_cos", "rope_sin")):
                pool.dma_start(ROPE[:, i, :, :], a[name].rearrange("(m p) f -> p m f", p=P)).then_inc(s["const_in"], 16)

            def select(view, op, fill, base, pattern, cm):
                link(pool.affine_select(out=view, in_=view, compare_op=op, fill=fill, base=base,
                                        pattern=pattern, channel_multiplier=cm))

            for tile, v in ((ONES, 1.0), (ID, 1.0), (LE, 1.0), (GT, 1.0), (NTRI, -1.0), (NONES, -1.0),
                            (AMASK, 0.0), (FMASK, 0.0)):
                link(pool.memset(tile[:, :], v))
            select(ID[:, :], ALU.is_equal, 0.0, 0, [[-1, P]], 1)
            pool.sem_inc(s["masks"], 1)
            select(LE[:, :], ALU.is_ge, 0.0, 0, [[1, P]], -1)
            select(GT[:, :], ALU.is_gt, 0.0, 0, [[-1, P]], 1)
            select(NTRI[:, :], ALU.is_ge, 0.0, 0, [[-1, P]], 1)
            select(AMASK[:, 0:P], ALU.is_ge, NEG, 0, [[-1, P]], 1)
            select(AMASK[:, P:2 * P], ALU.is_gt, NEG, 0, [[1, P]], -1)
            select(AMASK[:, 2 * P:3 * P], ALU.is_ge, NEG, 0, [[-1, P]], 1)
            select(FMASK[:, 0:P], ALU.is_ge, NEG, 0, [[-1, P]], 1)
            select(FMASK[:, 2 * P:3 * P], ALU.is_ge, NEG, 0, [[-1, P]], 1)
            link(pool.memset(even_spare[:, 0:1920], 1.0))
            for l in range(LEVELS):
                h = 1 << l
                nb = P // (2 * h)
                ms = MS[:, l, :].rearrange("p (b s r) -> p b s r", b=nb, s=2)
                select(ms[:, :, 1, :], ALU.is_ge, 0.0, -h, [[-2 * h, nb], [0, h]], 1)
                select(ms[:, :, 1, :], ALU.is_ge, 0.0, h, [[2 * h, nb], [1, h]], -1)
                select(ms[:, :, 0, :], ALU.is_gt, 0.0, 0, [[-2 * h, nb], [-1, h]], 1)
                select(ms[:, :, 0, :], ALU.is_gt, 0.0, h, [[2 * h, nb], [0, h]], -1)
                mk = MK[:, l, :].rearrange("p (b s r) -> p b s r", b=nb, s=2)
                select(mk[:, :, 1, :], ALU.is_ge, 0.0, 0, [[-2 * h, nb], [0, h]], 1)
                select(mk[:, :, 1, :], ALU.is_gt, 0.0, h, [[2 * h, nb], [0, h]], -1)
                link(pool.memset(mk[:, :, 0, :], 0.0))
            select(MK[:, LEVELS, :], ALU.is_equal, 0.0, 0, [[-1, P]], 1)
            pool.wait_ge(s["const_in"], 16 * N_CONST)
            link(pool.tensor_copy(DSK[0:64, :], BC[0:64, S_DSK:S_DSK + 16:2]))
            link(pool.tensor_copy(DSK[64:128, :], BC[64:128, S_DSK + 1:S_DSK + 16:2]))
            pool.sem_inc(s["masks"], 1)

            def normalise(p, probs):
                for h in range(16):
                    pool.wait_ge(s[p + "rcp"], h + 1)
                    rc = SM[:, 24 + 2 * (h % 2):26 + 2 * (h % 2)]
                    pr = probs[:, h % 2, :]
                    pool.tensor_scalar(pr[:, 0:P], pr[:, 0:P], rc[:, 0:1], None, ALU.mult)
                    pool.tensor_scalar(pr[:, P:384], pr[:, P:384], rc[:, 1:2], None, ALU.mult)\
                        .then_inc(s[p + "pn"], 1)

            normalise("a_", BIG[:, 0, 0:768].rearrange("p (b c) -> p b c", b=2))

            ke = WORK[:, 2048:3072].rearrange("p (l i) -> p l i", l=8)
            for u in range(2 * B_HEADS):
                h, m = u // 2, u % 2
                pool.wait_ge(s["b_ex"], u + 1)
                if u >= 1:
                    pool.wait_ge(s["b_att"], u)
                ex = WORK[:, 0:1024].rearrange("p (l i) -> p l i", l=8)
                k = chan(7, h)[:, m * P:(m + 1) * P]
                kk = k.unsqueeze(1).broadcast_to([P, 8, P])
                pool.tensor_tensor(ke, ex, kk, ALU.mult).then_inc(s["b_ke"], 1)
                if m == 0:
                    if h >= 1:
                        pool.wait_ge(s["b_cross"], h)
                    pool.tensor_tensor(KX, ex[:, 7, :], k, ALU.mult).then_inc(s["b_kx"], 1)

            pool.wait_ge(s["y_l"], 16)
            link(pool.memset(CM, 1.0))
            link(pool.memset(CN, 0.0))
            for d0 in (0, 256):
                select(CM[:, d0:d0 + P], ALU.is_gt, 0.0, 0, [[1, P]], -1)
                select(CN[:, d0:d0 + P], ALU.is_gt, NEG, 0, [[1, P]], -1)
            pool.sem_inc(s["c_mask"], 1)

            ag = WORK[:, 0:768].rearrange("p (b c) -> p b c", b=2)
            pool.wait_ge(s["s_a"], 1)
            acol = SM[:, 64:96].rearrange("p (m h) -> p m h", m=2)
            for h in range(S_HEADS):
                if h >= 2:
                    pool.wait_ge(s["s_seg"], h - 1)
                g = ag[:, h % 2, :]
                pool.tensor_scalar(g[:, 0:P], GT[:, :], acol[:, 0, h:h + 1], None, ALU.mult)
                pool.tensor_scalar(g[:, P:256], ONES[:, :], acol[:, 1, h:h + 1], None, ALU.mult)
                pool.tensor_scalar(g[:, 256:384], GT[:, :], acol[:, 1, h:h + 1], None, ALU.mult)\
                    .then_inc(s["s_ag"], 1)

            lg = WORK[:, 0:768].rearrange("p (b c) -> p b c", b=2)
            lf = SM[:, 96:128].rearrange("p (m h) -> p m h", m=2)
            pool.wait_ge(s["f_lf"], 1)
            pool.wait_ge(s["s_seg"], S_HEADS)
            probs = WORK[:, 1536:2304].rearrange("p (b c) -> p b c", b=2)
            for i in range(F_HEADS + 2):
                if i < F_HEADS:
                    h = i
                    if h >= 2:
                        pool.wait_ge(s["f_score"], h - 1)
                    g = lg[:, h % 2, :]
                    pool.tensor_scalar(g[:, 0:P], GT[:, :], lf[:, 0, h:h + 1], None, ALU.mult)
                    pool.tensor_scalar(g[:, P:256], ONES[:, :], lf[:, 1, h:h + 1], None, ALU.mult)
                    pool.tensor_scalar(g[:, 256:384], GT[:, :], lf[:, 1, h:h + 1], None, ALU.mult)\
                        .then_inc(s["f_lg"], 1)
                if i >= 2:
                    h = i - 2
                    pool.wait_ge(s["f_rcp"], h + 1)
                    rc = SM[:, 24 + 2 * (h % 2):26 + 2 * (h % 2)]
                    pr = probs[:, h % 2, :]
                    pool.tensor_scalar(pr[:, 0:P], pr[:, 0:P], rc[:, 0:1], None, ALU.mult)
                    pool.tensor_scalar(pr[:, P:384], pr[:, P:384], rc[:, 1:2], None, ALU.mult)\
                        .then_inc(s["f_pn"], 1)

            pool.wait_ge(s["y_l"], 48)
            iota_i = WORK[:, 3968:4096].bitcast(mybir.dt.int32)
            link(pool.iota(iota_i, [[1, P]], base=0, channel_multiplier=0))
            pool.tensor_copy(IOTA, iota_i).then_inc(s["tk_iota"], 1)
            pool.wait_ge(s["tk_parts"], 1)
            for k in range(QUARTERS):
                with pool.Fori(0, QR // 2) as q:
                    for b in range(2):
                        pool.wait_ge(s["oh1"], 2 * q + (QR * k + b + 1))
                        t0 = 2 * TG * q + TG * b
                        pool.tensor_tensor(OHG[:, b, :, :, :],
                                           OH1[:, b, :, :].unsqueeze(1).broadcast_to([P, 3, TG, QR]),
                                           G3[:, :, bass.ds(t0, TG)].unsqueeze(3).broadcast_to([P, 3, TG, QR]),
                                           ALU.mult).then_inc(s["ohg"], 1)

            pool.wait_ge(s["g_mm"], QR * QUARTERS)
            pool.dma_start(WORK[:, 0:2048], a["lnf_w_2"].partition_broadcast(P)).then_inc(s["lnf_in"], 16)

        @block.scalar
        def _(act):
            ch = Chain(act, s["act_chain"])
            link = ch.link
            pending = []

            def leave(r, i, parity, t):
                kind = r["kind"]
                act.wait_ge(s["ws_used"], 8 * (t + 1))
                if kind == "res":
                    return
                for b in range(2):
                    ps = bank[2 * parity + b]
                    if kind == "gate":
                        dst, src = DTF[:, r["dest"], b, :], ps[:, 0:16]
                    elif kind == "tok" or kind in ("chan", "silu", "scaled", "eighth"):
                        w = r["width"]
                        dst = BIG[:, bass.ds(r["dest"] + i, 1), b * 512:b * 512 + w].rearrange("p o n -> p (o n)")
                        src = ps[:, 0:w]
                    if kind == "silu":
                        ins = act.activation(dst, src, ACT.Silu)
                    elif kind == "scaled":
                        ins = act.activation(dst, src, ACT.Copy, scale=float(C_HD) ** -0.5)
                    elif kind == "eighth":
                        ins = act.activation(dst, src, ACT.Copy, scale=float(F_HD) ** -0.5)
                    else:
                        ins = act.activation(dst, src, ACT.Copy)
                ins.then_inc(s["tile_free"], 1)

            def split(r, i, parity, first):
                t = r["base"] + i
                w = r["width"]
                for sub in range(8):
                    if sub == 4:
                        if not first:
                            leave(r, i - 1, 1 - parity, t - 1)
                        elif pending:
                            leave(*pending.pop())
                    if sub % 2 == 0:
                        act.wait_ge(s[f"w_full{sub // 2}"], 16 * (t + 1))
                    if r["base"] > 0 or not first or sub >= 4:
                        act.wait_ge(s["ws_used"], 8 * t + (sub - 3))
                    raw = RAW[:, sub // 2, :].rearrange("p (k n) -> p k n", k=4)
                    k0 = 2 * (sub % 2)
                    sl = 2 * (sub % 4)
                    act.activation(WH[:, sl:sl + 2, 0:w], raw[:, k0:k0 + 2, 0:w], ACT.Copy)\
                        .then_inc(s["wh_done"], 1)
                if isinstance(i, int) and i == r["n"] - 1:
                    pending.append((r, i, parity, t))

            def phase(name):
                over_tiles(act, name, split)
                leave(*pending.pop())

            def rms(n, scratch):
                ss = SM[:, 16:18]
                for m in range(MT):
                    link(act.activation(scratch, XR[:, m, :], ACT.Square, accum_out=ss[:, m:m + 1]))
                link(act.activation(SM[:, 18:20], ss, ACT.Ln, bias=SM[:, 22:23], scale=1.0 / D))
                act.activation(SM[:, 20:22], SM[:, 18:20], ACT.Exp, scale=-0.5).then_inc(s["n_rstd"], 1)

            def norm_high(n):
                for g in range(8):
                    act.wait_ge(s["n_t"], 8 * n + g + 1)
                    for kk in range(2):
                        kt = 2 * g + kk
                        act.activation(HH[:, kt, :], bank[4 + g % 4][:, kk * T:(kk + 1) * T], ACT.Copy,
                                       scale=COLS[:, V_LN + 16 * n + kt:V_LN + 16 * n + kt + 1])\
                            .then_inc(s["n_h"], 1)

            def y_high(c):
                act.wait_ge(s["y_ready"], c + 1)
                act.activation(HH[:, c % 16, :], YB[:, c % 2, :], ACT.Copy).then_inc(s["y_h"], 1)

            big_scratch = BIG[:, 4:6, :].rearrange("p a b -> p (a b)")

            act.wait_ge(s["vec_t"], 1)
            act.activation(COLS[:, 0:V_ROWS], bank[0][:, 0:V_ROWS], ACT.Copy)
            act.activation(COLS[:, V_CW:V_COLS], bank[0][:, V_ROWS:V_ROWS + 48], ACT.Copy).then_inc(s["cols_set"], 1)
            act.wait_ge(s["x_in"], 16)
            act.wait_ge(s["eps_set"], 1)
            act.wait_ge(s["cols_set"], 1)
            rms(0, big_scratch)
            norm_high(0)
            phase("even_in")

            st = SM[:, 96:132]
            act.wait_ge(s["aq_ready"], 1)
            link(act.activation(st, st, ACT.Ln, bias=SM[:, 22:23], scale=1.0 / A_HD))
            link(act.activation(st, st, ACT.Exp, scale=-0.5))
            act.sem_inc(s["aq_ready"], 1)
            qT = WORK[:, 0:2048].rearrange("p (k t) -> p k t", k=8)
            kT = WORK[:, 2048:2560].rearrange("p (k t) -> p k t", k=2)
            for g in range(5):
                act.wait_ge(s["qk_t"], g + 1)
                dst = qT[:, 2 * g:2 * g + 2, :] if g < 4 else kT[:, :, :]
                act.activation(dst, bank[4 + g % 4][:, :].rearrange("p (k t) -> p k t", k=2), ACT.Copy)\
                    .then_inc(s["qk_c"], 1)

            def attend(p, S, probs, pt, sinks, c0):
                for i in range(16 + 3):
                    if i < 16:
                        h = i
                        act.wait_ge(s[p + "soft"], h + 1)
                        if h >= 2:
                            act.wait_ge(s[p + "pt"], h - 1)
                        nm = SM[:, 32 + 2 * (h % 2):34 + 2 * (h % 2)]
                        den = SM[:, 36 + 2 * (h % 2):38 + 2 * (h % 2)]
                        act.activation(probs[:, h % 2, 0:P], S[:, h % 2, 0:P], ACT.Exp, bias=nm[:, 0:1],
                                       accum_out=den[:, 0:1])
                        if sinks is not None:
                            act.activation(SM[:, 40 + 2 * (h % 2):42 + 2 * (h % 2)], nm, ACT.Exp,
                                           bias=sinks[:, h:h + 1])
                        act.activation(probs[:, h % 2, P:384], S[:, h % 2, P:384], ACT.Exp, bias=nm[:, 1:2],
                                       accum_out=den[:, 1:2]).then_inc(s[p + "exp"], 1)
                    if 1 <= i <= 16:
                        h = i - 1
                        act.wait_ge(s[p + "pt"], h + 1)
                        if h >= 2:
                            act.wait_ge(s[p + "pv"], h - 1)
                        act.activation(pt[:, h % 2, :], bank[6 + h % 2][:, 0:384], ACT.Copy)\
                            .then_inc(s[p + "ptc"], 1)
                    if i >= 4 and i % 2 == 0:
                        y_high(c0 + (i - 4) // 2)

            abuf = BIG[:, 0:2, :].rearrange("p a b -> p (a b)")
            attend("a_", WORK[:, 2560:3328].rearrange("p (b c) -> p b c", b=2),
                   abuf[:, 0:768].rearrange("p (b c) -> p b c", b=2),
                   abuf[:, 1024:1792].rearrange("p (b c) -> p b c", b=2), BC[:, A_SINK:A_SINK + 16], 0)

            T1 = BIG[:, 0:2, :].rearrange("p a b -> p (a b)")
            T2 = BIG[:, 3:5, :].rearrange("p a b -> p (a b)")
            bfv = bf.rearrange("p a b -> p (a b)")
            lbz = SM[:, 44:52]
            act.wait_ge(s["b_vec"], 1)
            link(act.activation(SM[:, 52:60], lbz, ACT.Exp))
            act.sem_inc(s["b_vec"], 1)
            act.wait_ge(s["b_vec"], 3)
            link(act.activation(SM[:, 68:76], SM[:, 68:76], ACT.Ln, scale=2.0 ** 64))
            link(act.activation(SM[:, 76:84], SM[:, 60:68], ACT.Ln, scale=-1.0, bias=SM[:, 23:24]))
            act.sem_inc(s["b_vec"], 1)
            link(act.activation(T1, bfv, ACT.Abs))
            link(act.activation(T1, T1, ACT.Exp, scale=-1.0))
            act.activation(T1, T1, ACT.Ln, bias=SM[:, 23:24]).then_inc(s["b_e"], 1)
            act.wait_ge(s["b_lsg"], 2)
            act.wait_ge(s["b_vec"], 6)
            for h in range(B_HEADS):
                act.activation(bfv[:, h * T:(h + 1) * T], T2[:, h * T:(h + 1) * T], ACT.Exp,
                               bias=SM[:, 76 + h:77 + h]).then_inc(s["b_kin"], 1)
            act.wait_ge(s["b_ml"], B_HEADS)
            for h in range(B_HEADS):
                link(act.activation(T1[:, h * T:(h + 1) * T], T1[:, h * T:(h + 1) * T], ACT.Abs,
                                    bias=SM[:, 84 + h:85 + h]))
            link(act.activation(T1, T1, ACT.Exp, scale=-1.0))
            act.activation(T1, T1, ACT.Ln, bias=SM[:, 23:24]).then_inc(s["b_x"], 1)

            def decays(u):
                act.wait_ge(s["b_lt"], u + 1)
                if u >= 2:
                    act.wait_ge(s["b_es"], u - 1)
                act.activation(LFT[:, u % 2, :], bank[4][:, (u % 2) * P:(u % 2 + 1) * P], ACT.Copy)\
                    .then_inc(s["b_lf"], 1)
                act.wait_ge(s["b_es"], u + 1)
                if u >= 1:
                    act.wait_ge(s["b_qe"], u)
                    act.wait_ge(s["b_ke"], u)
                    act.wait_ge(s["b_kx"], (u + 1) // 2)
                for b in range(2):
                    ins = act.activation(WORK[:, 512 * b:512 * (b + 1)], bank[b][:, :], ACT.Exp)
                ins.then_inc(s["b_ex"], 1)

            def head_norm(h):
                act.wait_ge(s["b_ov"], h + 1)
                if h >= 1:
                    act.wait_ge(s["b_ss"], h)
                act.activation(BSQ, bank[5 + 2 * (h % 2)][:, 0:T], ACT.Square).then_inc(s["b_sq"], 1)
                act.wait_ge(s["b_ss"], h + 1)
                if h >= 1:
                    act.wait_ge(s["y_ready"], 8 + h)
                link(act.activation(BRS, bank[5 + 2 * (h % 2)][:, T:2 * T], ACT.Ln, bias=SM[:, 22:23], scale=1.0 / B_HD))
                act.activation(BRS, BRS, ACT.Exp, scale=-0.5).then_inc(s["b_rs"], 1)

            for i in range(2 * B_HEADS + 4):
                if i < 2 * B_HEADS:
                    decays(i)
                if i >= 2 and i % 2 == 0 and i - 2 < 2 * B_HEADS:
                    h = (i - 2) // 2
                    act.wait_ge(s["b_cross"], h + 1)
                    if h >= 1:
                        act.wait_ge(s["b_ov"], h)
                    act.activation(CX, bank[6][:, 0:P], ACT.Copy).then_inc(s["b_cx"], 1)
                if i >= 4 and i % 2 == 0:
                    head_norm((i - 4) // 2)
                    y_high(8 + (i - 4) // 2)
            phase("even_out")

            act.wait_ge(s["tile_free"], last_tile("even_out") + 1)
            rms(1, big_scratch)
            norm_high(1)
            phase("odd_in")
            cT = WORK[:, 0:768].rearrange("p (b c) -> p b c", b=2)
            cW = WORK[:, 1536:2304].rearrange("p (b c) -> p b c", b=2)
            for i in range(C_HEADS + 3):
                if i < C_HEADS:
                    h = i
                    act.wait_ge(s["c_z"], h + 1)
                    if h >= 2:
                        act.wait_ge(s["c_sp"], 2 * (h - 1))
                    t = cT[:, h % 2, :]
                    link(act.activation(t, bank[4 + h % 2][:, 0:384], ACT.Abs))
                    link(act.activation(t, t, ACT.Exp, scale=-1.0))
                    act.activation(t, t, ACT.Ln, bias=SM[:, 23:24]).then_inc(s["c_exp"], 1)
                if 1 <= i <= C_HEADS:
                    h = i - 1
                    act.wait_ge(s["c_min"], h + 1)
                    act.activation(cW[:, h % 2, :], cW[:, h % 2, :], ACT.Exp).then_inc(s["c_w"], 1)
                if i >= 3:
                    y_high(16 + i - 3)
            phase("odd_out")

            act.wait_ge(s["tile_free"], last_tile("odd_out") + 1)
            rms(2, big_scratch)
            norm_high(2)
            phase("two_in")
            act.wait_ge(s["s_dt"], 1)
            g64 = SM[:, 64:128]
            link(act.activation(WORK[:, 2560:2624], g64, ACT.Abs))
            link(act.activation(WORK[:, 2560:2624], WORK[:, 2560:2624], ACT.Exp, scale=-1.0))
            link(act.activation(WORK[:, 2560:2624], WORK[:, 2560:2624], ACT.Ln, bias=SM[:, 23:24]))
            act.activation(WORK[:, 2624:2640], BC[:, S_AL:S_AL + 16], ACT.Exp).then_inc(s["s_e"], 1)
            XBC = BIG[:, 11:14, :].rearrange("p a b -> p (a b)")
            for g in range(3):
                act.wait_ge(s["s_conv"], 4 * (g + 1))
                act.activation(XBC[:, g * 1024:(g + 1) * 1024], XBC[:, g * 1024:(g + 1) * 1024], ACT.Silu)\
                    .then_inc(s["s_xbc"], 1)
            sE = WORK[:, 768:1536].rearrange("p (b c) -> p b c", b=2)
            for h in range(S_HEADS):
                act.wait_ge(s["s_seg"], h + 1)
                if h >= 2:
                    act.wait_ge(s["s_l"], h - 1)
                act.activation(sE[:, h % 2, :], bank[4 + h % 2][:, 0:384], ACT.Exp).then_inc(s["s_ex"], 1)
            ZS = BIG[:, 0:2, :].rearrange("p a b -> p (a b)")
            SQ = WORK[:, 768:1792]
            for g in range(2):
                act.wait_ge(s["s_yg"], 4 * (g + 1))
                act.wait_ge(s["s_l"], S_HEADS)
                if g == 1:
                    act.wait_ge(s["s_ss"], 1)
                act.activation(SQ, ZS[:, g * 1024:(g + 1) * 1024], ACT.Square).then_inc(s["s_sq"], 1)
                act.wait_ge(s["s_ss"], g + 1)
                if g == 1:
                    act.wait_ge(s["y_ready"], 36)
                link(act.activation(WORK[:, 3456:3712], bank[6][:, 0:T], ACT.Ln, bias=SM[:, 22:23],
                                    scale=1.0 / 512))
                act.activation(WORK[:, 3456:3712], WORK[:, 3456:3712], ACT.Exp, scale=-0.5)\
                    .then_inc(s["s_rs"], 1)
                for j in range(4):
                    y_high(32 + 4 * g + j)

            attend("f_", WORK[:, 768:1536].rearrange("p (b c) -> p b c", b=2),
                   WORK[:, 1536:2304].rearrange("p (b c) -> p b c", b=2),
                   WORK[:, 2304:3072].rearrange("p (b c) -> p b c", b=2), None, 40)
            phase("two_out")

            act.wait_ge(s["tile_free"], last_tile("two_out") + 1)
            rms(3, big_scratch)
            norm_high(3)
            phase("peer_q")
            kTp = BIG[:, 4:6, :].rearrange("p a b -> p (a b)")
            for g in range(4):
                act.wait_ge(s["k_t"], g + 1)
                act.activation(kTp[:, g * 512:(g + 1) * 512], bank[4 + g][:, :], ACT.Copy).then_inc(s["k_c"], 1)
            SC = BIG[:, 8:12, :].rearrange("p a b -> p (a b)")
            for g in range(8):
                act.wait_ge(s["q_s"], g + 1)
                act.activation(SC[:, g * 512:(g + 1) * 512], bank[g % 4][:, :], ACT.Copy).then_inc(s["q_sc"], 1)

            def rows_high(n, j, g0=0):
                for g in range(4):
                    act.wait_ge(s["t_t"], 4 * n + g + 1)
                    if not (isinstance(n, int) and (n < 2 or (n >= 2 * QR and n % QR < 2))):
                        act.wait_ge(s["u_used"], 4 * n + (g - 7))
                    act.activation(WH[:, 4 * (j % 2) + g, :], bank[4 + g][:, :], ACT.Copy).then_inc(s["t_h"], 1)

            def gelu(n, j, k):
                act.wait_ge(s["u_used"], 4 * n + 4)
                act.activation(GB[k % 2][:, bass.ds(n - QR * k, 1), :].rearrange("p o t -> p (o t)"),
                               bank[j % 2][:, 0:T], ACT.Gelu).then_inc(s["a_gelu"], 1)

            def v_high(n, j, full):
                act.wait_ge(s[f"row_full{j}"], full)
                act.activation(WH[:, 4 * (j % 2):4 * (j % 2) + 4, :],
                               RAW[:, j, :].rearrange("p (g n) -> p g n", g=4), ACT.Copy).then_inc(s["v_h"], 1)

            def p_high(n, j, k):
                if not (isinstance(n, int) and n < 2):
                    act.wait_ge(s["o_mm"], n - 1)
                act.activation(PS[:, j % 2, 0, :], GB[k % 2][:, bass.ds(n - QR * k, 1), :].rearrange("p o t -> p (o t)"),
                               ACT.Copy).then_inc(s["p_h"], 1)

            for seg, (kind, k) in enumerate(SEGMENTS):
                n0 = QR * k
                full = (QR // 4) * seg
                after = SEGMENTS[seg + 1] if seg + 1 < len(SEGMENTS) else None
                if kind == "in":
                    for j in range(4):
                        if seg > 0 and SEGMENTS[seg - 1][0] == "out" and j < 2:
                            act.wait_ge(s["o_mm"], QR * (SEGMENTS[seg - 1][1] + 1) - 1 + j)
                        rows_high(n0 + j, j)
                        if j == 1 and k == 1:
                            act.wait_ge(s["tk_idx"], 2)
                        if j >= 1:
                            gelu(n0 + j - 1, j - 1, k)
                    with act.Fori(1, QR // 4) as q:
                        for j in range(4):
                            rows_high(4 * q + (n0 + j), j)
                            gelu(4 * q + (n0 + j - 1), (j + 3) % 4, k)
                    if after[0] == "out":
                        act.wait_ge(s["u_used"], 4 * (n0 + QR - 1))
                        v_high(QR * after[1], 0, 16 * (QR // 4 * (seg + 1) + 1))
                    gelu(n0 + QR - 1, 3, k)
                    if k == 0:
                        for m in range(MT):
                            g = WORK[:, 1024 + 128 * m:1152 + 128 * m]
                            act.wait_ge(s["tk_e"], m + 1)
                            act.activation(g, g, ACT.Exp).then_inc(s["tk_g"], 1)
                        for n in range(6):
                            act.wait_ge(s["tk_t"], n + 1)
                            act.activation(TKT[:, n % 3, (n // 3) * P:(n // 3 + 1) * P], bank[2 + n % 2][:, 0:P],
                                           ACT.Copy).then_inc(s["tk_tc"], 1)
                else:
                    if seg > 0 and SEGMENTS[seg - 1][0] == "out":
                        act.wait_ge(s["o_mm"], n0 - 1)
                        v_high(n0, 0, 16 * (full + 1))
                    act.wait_ge(s["g_mul"], n0 + QR)

                    def out_high(n, j, k, full, more=True):
                        p_high(n, j, k)
                        if more:
                            if j == 0 and isinstance(n, int) and n == QR * k:
                                act.wait_ge(s["u_used"], 4 * u_tiles)
                                if n > 0:
                                    act.wait_ge(s["o_mm"], n)
                            else:
                                act.wait_ge(s["o_mm"], n)
                            v_high(n + 1, (j + 1) % 4, full)

                    u_tiles = QR * (1 + max(kk for kd, kk in SEGMENTS[:seg] if kd == "in"))
                    for j in range(4):
                        out_high(n0 + j, j, k, 16 * (full + 1 + (j == 3)))
                    with act.Fori(1, QR // 4 - 1) as q:
                        for j in range(4):
                            out_high(4 * q + (n0 + j), j, k, 16 * q + 16 * (full + 1 + (j == 3)))
                    for j in range(4):
                        out_high(n0 + QR - 4 + j, j, k, 16 * (full + QR // 4), j < 3)

            act.wait_ge(s["o_add"], 8 * QUARTERS)
            rms(4, big_scratch)

        @block.vector
        def _(dve):
            ch = Chain(dve, s["dve_chain"])
            link = ch.link
            pending = []

            def leave(r, i, parity, t):
                if r["kind"] != "res":
                    return
                dve.wait_ge(s["ws_used"], 8 * (t + 1))
                for m in range(MT):
                    x = XR[:, m, bass.ds(r["c0"] + i * NW, NW)]
                    ins = dve.tensor_tensor(x, x, bank[2 * parity + m][:, :], ALU.add)
                ins.then_inc(s["tile_free"], 1)

            def split(r, i, parity, first):
                t = r["base"] + i
                w = r["width"]
                for sub in range(8):
                    if sub == 4:
                        if not first:
                            leave(r, i - 1, 1 - parity, t - 1)
                        elif pending:
                            leave(*pending.pop())
                    dve.wait_ge(s["wh_done"], 8 * t + sub + 1)
                    raw = RAW[:, sub // 2, :].rearrange("p (k n) -> p k n", k=4)
                    k0 = 2 * (sub % 2)
                    sl = 2 * (sub % 4)
                    dve.tensor_tensor(WL[:, sl:sl + 2, 0:w], raw[:, k0:k0 + 2, 0:w],
                                      WH[:, sl:sl + 2, 0:w].bitcast(F32), ALU.subtract).then_inc(s["wl_done"], 1)
                if isinstance(i, int) and i == r["n"] - 1:
                    pending.append((r, i, parity, t))

            def phase(name):
                over_tiles(dve, name, split)
                leave(*pending.pop())

            xn = BIG[:, 0:4, :].rearrange("p (m a) b -> p m (a b)", m=2)

            def norm_low(n):
                dve.wait_ge(s["n_rstd"], n + 1)
                for m in range(MT):
                    dve.tensor_scalar(xn[:, m, :], XR[:, m, :], SM[:, 20 + m:21 + m], None, ALU.mult)\
                        .then_inc(s["n_x"], 1)
                for g in range(8):
                    dve.wait_ge(s["n_h"], 16 * n + 2 * g + 2)
                    for kk in range(2):
                        kt = 2 * g + kk
                        dve.scalar_tensor_tensor(
                            HL[:, kt, :], bank[4 + g % 4][:, kk * T:(kk + 1) * T],
                            COLS[:, V_LN + 16 * n + kt:V_LN + 16 * n + kt + 1],
                            HH[:, kt, :].bitcast(F32), ALU.mult, ALU.subtract).then_inc(s["n_l"], 1)

            def y_wait(c):
                if c >= 2:
                    dve.wait_ge(s["y_l"], c - 1)

            def y_low(c):
                dve.wait_ge(s["y_h"], c + 1)
                dve.tensor_tensor(HL[:, c % 16, :], YB[:, c % 2, :], HH[:, c % 16, :].bitcast(F32),
                                  ALU.subtract).then_inc(s["y_l"], 1)

            link(dve.memset(SM[:, 22:23], EPS))
            dve.memset(SM[:, 23:24], 1.0).then_inc(s["eps_set"], 1)
            norm_low(0)
            phase("even_in")

            dve.wait_ge(s["const_in"], 16 * N_CONST)
            dve.wait_ge(s["tile_free"], 13)
            q_t = BIG[:, 0:2, :].rearrange("p a b -> p (a b)")
            kv = BIG[:, 2, :].rearrange("p (m n) -> p m n", m=2)
            kcol = kv[:, :, 0:P]
            w1, w2 = WORK[:, 0:2048], WORK[:, 2048:4096]
            st = SM[:, 96:132]
            link(dve.tensor_tensor(w1, q_t, q_t, ALU.mult))
            link(dve.tensor_reduce(st[:, 0:32], w1.rearrange("p (h d) -> p h d", d=64), AX.X, ALU.add))
            k2 = w2[:, 0:256].rearrange("p (m n) -> p m n", m=2)
            link(dve.tensor_tensor(k2, kcol, kcol, ALU.mult))
            link(dve.tensor_reduce(st[:, 32:36], w2[:, 0:256].rearrange("p (h d) -> p h d", d=64), AX.X, ALU.add))
            dve.sem_inc(s["aq_ready"], 1)
            dve.wait_ge(s["aq_ready"], 2)
            kc = w2[:, 1024:1280].rearrange("p (h d) -> p h d", d=64)
            q3 = q_t.rearrange("p (h d) -> p h d", d=64)
            link(dve.tensor_tensor(q3, q3, st[:, 0:32].unsqueeze(2).broadcast_to([P, 32, 64]), ALU.mult))
            link(dve.tensor_tensor(q3, q3, BC[:, A_QN:A_QN + 64].unsqueeze(1).broadcast_to([P, 32, 64]), ALU.mult))
            link(dve.tensor_tensor(kc.rearrange("p (m g) d -> p m g d", m=2), kcol.rearrange("p m (g d) -> p m g d", g=2),
                                   st[:, 32:36].rearrange("p (m g) -> p m g", m=2).unsqueeze(3).broadcast_to([P, 2, 2, 64]),
                                   ALU.mult))
            link(dve.tensor_tensor(kc, kc, BC[:, A_KN:A_KN + 64].unsqueeze(1).broadcast_to([P, 4, 64]), ALU.mult))
            for tt in range(2):
                for m in range(MT):
                    o = tt * 1024 + m * 512
                    x = q_t[:, o:o + 512].rearrange("p (h d) -> p h d", h=16)
                    c = ROPE[:, 0, m, :].unsqueeze(1).broadcast_to([P, 16, 32])
                    sn = ROPE[:, 1, m, :].unsqueeze(1).broadcast_to([P, 16, 32])
                    y1 = w1[:, 0:512].rearrange("p (h d) -> p h d", h=16)
                    y2 = w1[:, 512:1024].rearrange("p (h d) -> p h d", h=16)
                    link(dve.tensor_tensor(y1, x, c, ALU.mult))
                    link(dve.tensor_tensor(y2, x, sn, ALU.mult))
                    xh = q_t[:, o:o + 512].rearrange("p (h f d) -> p h f d", h=8, f=2)
                    y1h = w1[:, 0:512].rearrange("p (h f d) -> p h f d", h=8, f=2)
                    y2h = w1[:, 512:1024].rearrange("p (h f d) -> p h f d", h=8, f=2)
                    link(dve.tensor_tensor(xh[:, :, 0, :], y1h[:, :, 0, :], y2h[:, :, 1, :], ALU.subtract))
                    link(dve.tensor_tensor(xh[:, :, 1, :], y1h[:, :, 1, :], y2h[:, :, 0, :], ALU.add))
            kd = w2[:, 1536:2048].rearrange("p (m g c d) -> p m g c d", m=2, g=2, c=2)
            for m in range(MT):
                x = kc[:, 2 * m:2 * m + 2, :].rearrange("p h (f d) -> p (h f) d", f=2)
                c = ROPE[:, 0, m, :].unsqueeze(1).broadcast_to([P, 4, 32])
                sn = ROPE[:, 1, m, :].unsqueeze(1).broadcast_to([P, 4, 32])
                y1 = w1[:, 0:128].rearrange("p (h d) -> p h d", h=4)
                y2 = w1[:, 128:256].rearrange("p (h d) -> p h d", h=4)
                link(dve.tensor_tensor(y1, x, c, ALU.mult))
                link(dve.tensor_tensor(y2, x, sn, ALU.mult))
                y1h = w1[:, 0:128].rearrange("p (h f d) -> p h f d", h=2, f=2)
                y2h = w1[:, 128:256].rearrange("p (h f d) -> p h f d", h=2, f=2)
                for c2 in range(2):
                    link(dve.tensor_tensor(kd[:, m, :, c2, 0:32], y1h[:, :, 0, :], y2h[:, :, 1, :], ALU.subtract))
                    link(dve.tensor_tensor(kd[:, m, :, c2, 32:64], y1h[:, :, 1, :], y2h[:, :, 0, :], ALU.add))
            dve.sem_inc(s["aq_ready"], 1)

            def attend(p, S, mask, scale, sinks, gate, c0):
                for i in range(16 + 3):
                    if i < 16:
                        h = i
                        dve.wait_ge(s[p + "score"], h + 1)
                        if h >= 2:
                            dve.wait_ge(s[p + "exp"], h - 1)
                        z = S[:, h % 2, :]
                        link(dve.scalar_tensor_tensor(z, bank[4 + h % 2][:, 0:384], scale, mask, ALU.mult, ALU.add))
                        mx = SM[:, 28 + 2 * (h % 2):30 + 2 * (h % 2)]
                        nm = SM[:, 32 + 2 * (h % 2):34 + 2 * (h % 2)]
                        link(dve.tensor_reduce(mx[:, 0:1], z[:, 0:P], AX.X, ALU.max))
                        link(dve.tensor_reduce(mx[:, 1:2], z[:, P:384], AX.X, ALU.max))
                        if sinks is not None:
                            dve.tensor_scalar(nm, mx, sinks[:, h:h + 1], -1.0, ALU.max, ALU.mult)\
                                .then_inc(s[p + "soft"], 1)
                        else:
                            dve.tensor_scalar(nm, mx, -1.0, None, ALU.mult).then_inc(s[p + "soft"], 1)
                    if 1 <= i <= 16:
                        h = i - 1
                        den = SM[:, 36 + 2 * (h % 2):38 + 2 * (h % 2)]
                        rc = SM[:, 24 + 2 * (h % 2):26 + 2 * (h % 2)]
                        dve.wait_ge(s[p + "exp"], h + 1)
                        if h >= 2:
                            dve.wait_ge(s[p + "pn"], h - 1)
                        if sinks is not None:
                            link(dve.tensor_tensor(den, den, SM[:, 40 + 2 * (h % 2):42 + 2 * (h % 2)], ALU.add))
                        dve.reciprocal(rc, den).then_inc(s[p + "rcp"], 1)
                    if i >= 4 and i % 2 == 0:
                        j = (i - 4) // 2
                        c = c0 + j
                        if j >= 1:
                            y_low(c - 1)
                        dve.wait_ge(s[p + "pv"], 2 * j + 2)
                        y_wait(c)
                        o = bank[j % 2][:, 0:T]
                        if gate is not None:
                            dve.tensor_tensor(YB[:, c % 2, :], o, gate(j), ALU.mult).then_inc(s["y_ready"], 1)
                        else:
                            dve.tensor_copy(YB[:, c % 2, :], o).then_inc(s["y_ready"], 1)
                y_low(c0 + 7)

            attend("a_", WORK[:, 2560:3328].rearrange("p (b c) -> p b c", b=2), AMASK[:, :],
                   float(A_HD) ** -0.5, BC[:, A_SINK:A_SINK + 16], lambda j: chan(3, j), 0)

            T1 = BIG[:, 0:2, :].rearrange("p a b -> p (a b)")
            T2 = BIG[:, 3:5, :].rearrange("p a b -> p (a b)")
            bfv = bf.rearrange("p a b -> p (a b)")
            link(dve.tensor_tensor(SM[:, 44:52], COLS[:, V_LB:V_LB + 8], COLS[:, V_LB:V_LB + 8], ALU.subtract))
            dve.sem_inc(s["b_vec"], 1)
            dve.wait_ge(s["b_vec"], 2)
            link(dve.reciprocal(SM[:, 60:68], SM[:, 52:60]))
            link(dve.tensor_tensor(SM[:, 52:60], SM[:, 52:60], SM[:, 60:68], ALU.mult))
            link(dve.tensor_tensor(SM[:, 60:68], SM[:, 52:60], SM[:, 52:60], ALU.subtract))
            link(dve.tensor_scalar(SM[:, 68:76], SM[:, 60:68], 1e-30, None, ALU.max))
            link(dve.tensor_tensor(SM[:, 92:100], SM[:, 60:68], SM[:, 68:76], ALU.subtract))
            dve.sem_inc(s["b_vec"], 1)
            dve.wait_ge(s["b_vec"], 4)
            link(dve.tensor_scalar(SM[:, 68:76], SM[:, 68:76], -64.0 * LN2, None, ALU.add))
            link(dve.tensor_tensor(SM[:, 84:92], SM[:, 76:84], SM[:, 68:76], ALU.subtract))
            dve.sem_inc(s["b_vec"], 2)
            dve.wait_ge(s["b_e"], 1)
            link(dve.scalar_tensor_tensor(T1, bfv, 0.0, T1, ALU.min, ALU.subtract))
            dve.sem_inc(s["b_lsg"], 1)
            dve.tensor_tensor(T2, T1, bfv, ALU.subtract).then_inc(s["b_lsg"], 1)
            for h in range(B_HEADS):
                dve.wait_ge(s["b_kin"], h + 1)
                c = slice(h * T, (h + 1) * T)
                link(dve.tensor_scalar(bfv[:, c], bfv[:, c], SM[:, 92 + h:93 + h], None, ALU.add))
                dve.tensor_scalar(T2[:, c], T1[:, c], SM[:, 76 + h:77 + h], SM[:, 68 + h:69 + h], ALU.add, ALU.max)\
                    .then_inc(s["b_ml"], 1)
            dve.wait_ge(s["b_x"], 1)
            link(dve.tensor_tensor(T1, T1, T2, ALU.add))
            dve.sem_inc(s["b_x"], 1)
            qe = WORK[:, 1024:2048].rearrange("p (l i) -> p l i", l=8)
            am = WORK[:, 3072:4096]
            ex = WORK[:, 0:1024].rearrange("p (l i) -> p l i", l=8)
            for i in range(1, 2 * B_HEADS + 4):
                if 0 <= i - 2 < 2 * B_HEADS:
                    u = i - 2
                    dve.wait_ge(s["b_att"], u + 1)
                    if u >= 1:
                        dve.wait_ge(s["b_lev"], u)
                    for b in range(2):
                        ins = dve.tensor_tensor(am[:, 512 * b:512 * (b + 1)], bank[2 + b][:, :],
                                                MK[:, 4 * b:4 * b + 4, :].rearrange("p l i -> p (l i)"), ALU.mult)
                    ins.then_inc(s["b_am"], 1)
                if i - 1 < 2 * B_HEADS:
                    u = i - 1
                    h, m = u // 2, u % 2
                    dve.wait_ge(s["b_ex"], u + 1)
                    if m == 0 and h >= 1:
                        dve.wait_ge(s["b_cross"], h)
                    qq = chan(5, h)[:, m * P:(m + 1) * P].unsqueeze(1).broadcast_to([P, 8, P])
                    dve.tensor_tensor(qe, ex, qq, ALU.mult).then_inc(s["b_qe"], 1)
                if i >= 5 and i % 2 == 1:
                    h = (i - 5) // 2
                    c = 8 + h
                    if h >= 1:
                        y_low(c - 1)
                    dve.wait_ge(s["b_rs"], h + 1)
                    y_wait(c)
                    y = YB[:, c % 2, :]
                    link(dve.scalar_tensor_tensor(y, bank[5 + 2 * (h % 2)][:, 0:T], COLS[:, V_GN:V_GN + 1], BRS,
                                                  ALU.mult, ALU.mult))
                    dve.tensor_tensor(y, y, chan(11, h), ALU.mult).then_inc(s["y_ready"], 1)
            y_low(15)
            phase("even_out")

            norm_low(1)
            phase("odd_in")
            dve.wait_ge(s["c_mask"], 1)
            cT = WORK[:, 0:768].rearrange("p (b c) -> p b c", b=2)
            cS = WORK[:, 768:1536].rearrange("p (b c) -> p b c", b=2)
            cW = WORK[:, 1536:2304].rearrange("p (b c) -> p b c", b=2)
            for i in range(C_HEADS + 3):
                if i < C_HEADS:
                    h = i
                    dve.wait_ge(s["c_exp"], h + 1)
                    if h >= 2:
                        dve.wait_ge(s["c_e"], h - 1)
                    sp_ = cS[:, h % 2, :]
                    dve.scalar_tensor_tensor(sp_, bank[4 + h % 2][:, 0:384], 0.0, cT[:, h % 2, :], ALU.max,
                                             ALU.add).then_inc(s["c_sp"], 1)
                    dve.wait_ge(s["c_sp"], 2 * h + 1)
                    dve.tensor_tensor(sp_, sp_, CM, ALU.mult).then_inc(s["c_sp"], 1)
                if 1 <= i <= C_HEADS:
                    h = i - 1
                    dve.wait_ge(s["c_e"], h + 1)
                    if h >= 2:
                        dve.wait_ge(s["c_pv"], h - 1)
                    dve.tensor_tensor(cW[:, h % 2, :], bank[4 + h % 2][:, 0:384], CN, ALU.min).then_inc(s["c_min"], 1)
                if i >= 3:
                    h = i - 3
                    c = 16 + h
                    if h >= 1:
                        y_low(c - 1)
                    dve.wait_ge(s["c_pv"], h + 1)
                    y_wait(c)
                    dve.tensor_tensor(YB[:, c % 2, :], bank[6 + h % 2][:, 0:T], chan(12, h), ALU.mult)\
                        .then_inc(s["y_ready"], 1)
            y_low(31)
            phase("odd_out")

            norm_low(2)
            phase("two_in")
            dve.wait_ge(s["tile_free"], last_tile("two_in") + 1)
            g64 = SM[:, 64:128]
            dt_, lf = SM[:, 64:96], SM[:, 96:128]

            def per_head(at):
                return BC[:, at:at + 16].unsqueeze(1).broadcast_to([P, 2, 16])

            two = "p (m h) -> p m h"
            link(dve.tensor_tensor(dt_.rearrange(two, m=2), DTF[:, 0, :, :], per_head(S_DTB), ALU.add))
            link(dve.tensor_tensor(lf.rearrange(two, m=2), DTF[:, 1, :, :], per_head(F_FB), ALU.add))
            link(dve.tensor_scalar(lf, lf, -1.0, None, ALU.mult))
            dve.sem_inc(s["s_dt"], 1)
            XB = BIG[:, 2:5, :].rearrange("p a b -> p (a b)")
            XBC = BIG[:, 11:14, :].rearrange("p a b -> p (a b)")
            for k in range(12):
                x, y = XB[:, k * T:(k + 1) * T], XBC[:, k * T:(k + 1) * T]

                def tap(j):
                    return COLS[:, V_CW + 12 * j + k:V_CW + 12 * j + k + 1]

                link(dve.tensor_scalar(y, x, tap(3), COLS[:, V_CB + k:V_CB + k + 1], ALU.mult, ALU.add))
                for back in (1, 2, 3):
                    ins = dve.scalar_tensor_tensor(y[:, back:T], x[:, 0:T - back], tap(3 - back), y[:, back:T],
                                                   ALU.mult, ALU.add)
                    if back < 3:
                        link(ins)
                    else:
                        ins.then_inc(s["s_conv"], 1)
            dve.wait_ge(s["s_e"], 1)
            link(dve.scalar_tensor_tensor(g64, g64, 0.0, WORK[:, 2560:2624], ALU.max, ALU.add))
            link(dve.tensor_scalar(lf, lf, -1.0, None, ALU.mult))
            DT = WORK[:, 2640:2672]
            link(dve.tensor_copy(DT, dt_))
            link(dve.tensor_scalar(WORK[:, 2624:2640], WORK[:, 2624:2640], -1.0, None, ALU.mult))
            link(dve.tensor_tensor(dt_.rearrange(two, m=2), dt_.rearrange(two, m=2),
                                   WORK[:, 2624:2640].unsqueeze(1).broadcast_to([P, 2, 16]), ALU.mult))
            dve.sem_inc(s["s_a"], 1)
            dve.sem_inc(s["f_lf"], 1)
            XD = BIG[:, 14:16, :].rearrange("p a b -> p (a b)").rearrange("p (m h d) -> p m h d", m=2, h=16)
            for g in range(4):
                m, hh = g // 2, g % 2
                dve.wait_ge(s["s_xt"], g + 1)
                dve.tensor_tensor(XD[:, m, 8 * hh:8 * hh + 8, :],
                                  bank[g % 2][:, :].rearrange("p (h d) -> p h d", h=8),
                                  DT[:, 16 * m + 8 * hh:16 * m + 8 * hh + 8].unsqueeze(2).broadcast_to([P, 8, 64]),
                                  ALU.mult).then_inc(s["s_xd"], 1)
            CB = WORK[:, 2688:3456].rearrange("p (g c) -> p g c", g=2)
            for g in range(2):
                dve.wait_ge(s["s_cb"], g + 1)
                dve.tensor_tensor(CB[:, g, 0:P], bank[2 + g][:, 0:P], LE[:, :], ALU.mult)
                dve.tensor_copy(CB[:, g, P:256], bank[2 + g][:, P:256])
                dve.tensor_tensor(CB[:, g, 256:384], bank[2 + g][:, 256:384], LE[:, :], ALU.mult)\
                    .then_inc(s["s_cbm"], 1)
            dve.wait_ge(s["s_cbm"], 2)
            sE = WORK[:, 768:1536].rearrange("p (b c) -> p b c", b=2)
            sL = WORK[:, 1792:2560].rearrange("p (b c) -> p b c", b=2)
            ZS = BIG[:, 0:2, :].rearrange("p a b -> p (a b)")
            dve.wait_ge(s["masks"], 2)
            for i in range(S_HEADS + 2):
                if i < S_HEADS:
                    h = i
                    dve.wait_ge(s["s_ex"], h + 1)
                    if h >= 2:
                        dve.wait_ge(s["s_y"], h - 1)
                    dve.tensor_tensor(sL[:, h % 2, :], sE[:, h % 2, :], CB[:, h // 8, :], ALU.mult)\
                        .then_inc(s["s_l"], 1)
                if i >= 2 and i % 2 == 1:
                    j = (i - 2) // 2
                    dve.wait_ge(s["s_y"], 2 * j + 2)
                    xs = XBC[:, j * T:(j + 1) * T]
                    link(dve.scalar_tensor_tensor(xs, xs, DSK[:, j:j + 1], bank[j % 2][:, 0:T], ALU.mult, ALU.add))
                    z = ZS[:, j * T:(j + 1) * T]
                    dve.tensor_tensor(z, z, xs, ALU.mult).then_inc(s["s_yg"], 1)
            for g in range(2):
                dve.wait_ge(s["s_rs"], g + 1)
                for j in range(4 * g, 4 * g + 4):
                    c = 32 + j
                    y_wait(c)
                    dve.scalar_tensor_tensor(YB[:, c % 2, :], ZS[:, j * T:(j + 1) * T],
                                             COLS[:, V_SSDN + j:V_SSDN + j + 1], WORK[:, 3456:3712],
                                             ALU.mult, ALU.mult).then_inc(s["y_ready"], 1)
                    y_low(c)

            attend("f_", WORK[:, 768:1536].rearrange("p (b c) -> p b c", b=2), FMASK[:, :], 1.0, None, None, 40)
            phase("two_out")

            norm_low(3)
            phase("peer_q")
            dve.wait_ge(s["q_sc"], 8)
            SC = BIG[:, 8:12, :].rearrange("p (m a) b -> p m (a b)", m=2)
            v16 = WORK[:, 0:256].rearrange("p (f k) -> p f k", k=16)
            v4 = WORK[:, 0:256].rearrange("p (h f k) -> p h f k", f=2, k=16)
            i16 = WORK[:, 256:512].bitcast(U32).rearrange("p (f k) -> p f k", k=16)
            if16 = WORK[:, 512:768].rearrange("p (h f k) -> p h f k", f=2, k=16)
            s16 = WORK[:, 768:896].rearrange("p (h k) -> p h k", k=16)
            p16 = WORK[:, 896:1024].bitcast(U32)
            gate = WORK[:, 1024:1280].rearrange("p (m n) -> p m n", m=2)
            pa_u = WORK[:, 1280:1408].bitcast(U32)
            pb_u = WORK[:, 1408:1536].bitcast(U32)
            pa_f, pb_f = WORK[:, 1536:1664], WORK[:, 1664:1792]
            gsum = SM[:, 96:104]
            cand = BIG[:, 12:14, :].rearrange("p a b -> p (a b)")
            oh = BIG[:, 14:16, :].rearrange("p a b -> p (a b)").rearrange("p (h k j) -> p h k j", h=8, k=16)
            dve.wait_ge(s["tk_iota"], 1)

            def top16(x, values, places):
                link(dve.max(values[:, 0:8], x))
                link(dve.max_index(places[:, 0:8], values[:, 0:8], x))
                link(dve.match_replace(x, values[:, 0:8], x, -3.0e38))
                link(dve.max(values[:, 8:16], x))
                link(dve.max_index(places[:, 8:16], values[:, 8:16], x))

            def top_keys(step):
                m, r = step // 16, step % 16
                if r < 8:
                    for f in (2 * r, 2 * r + 1):
                        top16(SC[:, m, f * P:(f + 1) * P], v16[:, f, :], i16[:, f, :])
                    return
                if r == 8:
                    link(dve.tensor_copy(WORK[:, 512:768], WORK[:, 256:512].bitcast(U32)))
                    link(dve.tensor_tensor(cand.rearrange("p (h a b) -> p h a b", h=8, a=16),
                                           v4[:, :, 0, :].unsqueeze(3).broadcast_to([P, 8, 16, 16]),
                                           v4[:, :, 1, :].unsqueeze(2).broadcast_to([P, 8, 16, 16]), ALU.add))
                if r < 12:
                    for h in (2 * (r - 8), 2 * (r - 8) + 1):
                        top16(cand[:, h * 256:(h + 1) * 256], s16[:, h, :], p16[:, h * 16:(h + 1) * 16])
                    return
                if r == 12:
                    dve.tensor_tensor(gate[:, m, :].rearrange("p (h k) -> p h k", k=16), s16,
                                      s16[:, :, 0:1].broadcast_to([P, 8, 16]), ALU.subtract).then_inc(s["tk_e"], 1)
                    link(dve.tensor_scalar(pa_u, p16, 4, None, ALU.logical_shift_right))
                    link(dve.tensor_scalar(pb_u, p16, 15, None, ALU.bitwise_and))
                    link(dve.tensor_copy(pa_f, pa_u))
                    link(dve.tensor_copy(pb_f, pb_u))
                f, part = (r - 12) // 2, (r - 12) % 2
                pf = (pa_f, pb_f)[f].rearrange("p (h k) -> p h k", k=16)
                if part == 0:
                    link(dve.tensor_tensor(oh, IOTA[:, 0:16].unsqueeze(1).unsqueeze(1).broadcast_to([P, 8, 16, 16]),
                                           pf.unsqueeze(3).broadcast_to([P, 8, 16, 16]), ALU.is_equal))
                else:
                    link(dve.tensor_tensor(oh, oh, if16[:, :, f, :].unsqueeze(2).broadcast_to([P, 8, 16, 16]), ALU.mult))
                    link(dve.tensor_reduce(SEL[:, m, f, :].rearrange("p (h k) -> p h k", k=16), oh, AX.X, ALU.add))

            def rows_low(n, j):
                for g in range(4):
                    dve.wait_ge(s["t_h"], 4 * n + g + 1)
                    sl = 4 * (j % 2) + g
                    dve.tensor_tensor(WL[:, sl, :], bank[4 + g][:, :], WH[:, sl, :].bitcast(F32), ALU.subtract)\
                        .then_inc(s["t_l"], 1)

            def one_hots(g, i, b, k):
                if not (isinstance(g, int) and g < 2):
                    dve.wait_ge(s["g_mm"], g - 1)
                t0 = TG * i
                dve.tensor_tensor(OH2[:, b, :, :], IOTA.unsqueeze(1).broadcast_to([P, TG, P]),
                                  TKT[:, 1, bass.ds(t0, TG)].unsqueeze(2).broadcast_to([P, TG, P]),
                                  ALU.is_equal).then_inc(s["oh2"], 1)
                dve.tensor_tensor(OH1[:, b, :, :], IOTA[:, QR * k:QR * (k + 1)].unsqueeze(1).broadcast_to([P, TG, QR]),
                                  TKT[:, 0, bass.ds(t0, TG)].unsqueeze(2).broadcast_to([P, TG, QR]),
                                  ALU.is_equal).then_inc(s["oh1"], 1)

            def gated(g, i, b, k):
                dve.wait_ge(s["g_mm"], g + 1)
                x = GB[k % 2][:, :, bass.ds(TG * i, TG)]
                dve.tensor_tensor(x, x, bank[2 + b][:, 0:TG * QR].rearrange("p (t i) -> p i t", t=TG), ALU.mult)\
                    .then_inc(s["g_mul"], 1)

            def p_low(n, j, k):
                dve.wait_ge(s["p_h"], n + 1)
                dve.tensor_tensor(PS[:, j % 2, 1, :], GB[k % 2][:, bass.ds(n - QR * k, 1), :].rearrange("p o t -> p (o t)"),
                                  PS[:, j % 2, 0, :].bitcast(F32), ALU.subtract).then_inc(s["p_l"], 1)

            def v_low(n, j):
                dve.wait_ge(s["v_h"], n + 1)
                sl = slice(4 * (j % 2), 4 * (j % 2) + 4)
                dve.tensor_tensor(WL[:, sl, :], RAW[:, j, :].rearrange("p (g n) -> p g n", g=4),
                                  WH[:, sl, :].bitcast(F32), ALU.subtract).then_inc(s["v_l"], 1)

            for seg, (kind, k) in enumerate(SEGMENTS):
                n0 = QR * k
                if kind == "in" and k == 0:
                    for n in range(QR):
                        rows_low(n, n % 4)
                        top_keys(n)
                    for m in range(MT):
                        dve.wait_ge(s["tk_g"], m + 1)
                        g3 = gate[:, m, :].rearrange("p (h k) -> p h k", k=16)
                        link(dve.tensor_reduce(gsum, g3, AX.X, ALU.add))
                        link(dve.reciprocal(gsum, gsum))
                        link(dve.tensor_tensor(g3, g3, gsum.unsqueeze(2).broadcast_to([P, 8, 16]), ALU.mult))
                        dve.sem_inc(s["tk_idx"], 1)
                    dve.wait_ge(s["tk_tc"], 6)
                    left = WORK[:, 512:768]
                    link(dve.tensor_copy(G3[:, 0, :], TKT[:, 2, :]))
                    link(dve.tensor_tensor(left, TKT[:, 2, :], G3[:, 0, :], ALU.subtract))
                    link(dve.tensor_copy(G3[:, 1, :], left))
                    link(dve.tensor_tensor(left, left, G3[:, 1, :], ALU.subtract))
                    link(dve.tensor_copy(G3[:, 2, :], left))
                    dve.sem_inc(s["tk_parts"], 1)
                    one_hots(0, 0, 0, 0)
                elif kind == "in":
                    g0 = QR * (k - 1)
                    dve.wait_ge(s["a_gelu"], g0 + QR)
                    for j in range(4):
                        rows_low(n0 + j, j)
                        if j >= 1:
                            gated(g0 + j - 1, j - 1, (j - 1) % 2, k - 1)
                        one_hots(g0 + j + 1, j + 1, (j + 1) % 2, k - 1)
                    with dve.Fori(1, QR // 4 - 1) as q:
                        for j in range(4):
                            rows_low(4 * q + (n0 + j), j)
                            gated(4 * q + (g0 + j - 1), 4 * q + (j - 1), (j + 1) % 2, k - 1)
                            one_hots(4 * q + (g0 + j + 1), 4 * q + (j + 1), (j + 1) % 2, k - 1)
                    for i in range(QR - 4, QR):
                        rows_low(n0 + i, i % 4)
                        gated(g0 + i - 1, i - 1, (i - 1) % 2, k - 1)
                        if i + 1 < QR:
                            one_hots(g0 + i + 1, i + 1, (i + 1) % 2, k - 1)
                        else:
                            one_hots(g0 + QR, 0, 0, k)
                    v_low(QR * SEGMENTS[seg + 1][1], 0)
                    gated(g0 + QR - 1, QR - 1, 1, k - 1)
                else:
                    if k == QUARTERS - 1:
                        dve.wait_ge(s["a_gelu"], n0 + QR)
                        one_hots(n0 + 1, 1, 1, k)
                        gated(n0, 0, 0, k)
                        with dve.Fori(0, QR // 2 - 1) as q:
                            for b in range(2):
                                one_hots(2 * q + (n0 + b + 2), 2 * q + (b + 2), b, k)
                                gated(2 * q + (n0 + b + 1), 2 * q + (b + 1), 1 - b, k)
                        gated(n0 + QR - 1, QR - 1, 1, k)
                        v_low(n0, 0)
                    with dve.Fori(0, QR // 4 - 1) as q:
                        for j in range(4):
                            p_low(4 * q + (n0 + j), j, k)
                            v_low(4 * q + (n0 + j + 1), (j + 1) % 4)
                    for j in range(4):
                        p_low(n0 + QR - 4 + j, j, k)
                        if j < 3:
                            v_low(n0 + QR - 3 + j, j + 1)
                    dve.wait_ge(s["o_mm"], n0 + QR)
                    for b in (4, 5, 6, 7, 0, 1, 2, 3):
                        x = XR[:, b // 4, (b % 4) * NW:(b % 4 + 1) * NW]
                        dve.tensor_tensor(x, x, bank[b][:, :], ALU.add).then_inc(s["o_add"], 1)

            dve.wait_ge(s["n_rstd"], 5)
            dve.wait_ge(s["lnf_in"], 16)
            for m in range(MT):
                dve.scalar_tensor_tensor(xn[:, m, :], XR[:, m, :], SM[:, 20 + m:21 + m],
                                         WORK[:, 0:2048], ALU.mult, ALU.mult)\
                    .then_inc(s["n_x"], 1)

        @block.tensor
        def _(pe):
            def mm(dst, lhsT, rhs, start, stop):
                return pe.matmul(dst, lhsT, rhs, start=start, stop=stop, skip_group_check=True)

            def tile(r, i, parity, first):
                t = r["base"] + i
                w = r["width"]
                toks = r["kind"] in ("tok", "res", "gate")
                for sub in range(8):
                    if sub == 0 and (r["base"] >= 2 or i >= 2):
                        pe.wait_ge(s["tile_free"], t - 1)
                    pe.wait_ge(s["wl_done"], 8 * t + sub + 1)
                    for kk in range(2):
                        kt = 2 * sub + kk
                        sl = 2 * (sub % 4) + kk
                        last = kt == KT - 1
                        if toks:
                            for m in range(MT):
                                ms = slice(m * P, (m + 1) * P)
                                dst = bank[2 * parity + m][:, 0:w]
                                mm(dst, HH[:, kt, ms], WH[:, sl, 0:w], kt == 0, False)
                                mm(dst, HL[:, kt, ms], WH[:, sl, 0:w], False, False)
                                ins = mm(dst, HH[:, kt, ms], WL[:, sl, 0:w], False, last)
                        else:
                            for c in range(4):
                                cs = slice(c * P, (c + 1) * P)
                                dst = bank[2 * parity + c // 2][:, (c % 2) * T:(c % 2 + 1) * T]
                                mm(dst, WH[:, sl, cs], HH[:, kt, :], kt == 0 and c % 2 == 0, False)
                                mm(dst, WH[:, sl, cs], HL[:, kt, :], False, False)
                                ins = mm(dst, WL[:, sl, cs], HH[:, kt, :], False, last)
                    ins.then_inc(s["ws_used"], 1)

            xn = BIG[:, 0:4, :].rearrange("p (m a) b -> p m (a b)", m=2)

            def norm_t(n):
                pe.wait_ge(s["n_x"], 2 * n + 2)
                for g in range(8):
                    if g >= 4:
                        pe.wait_ge(s["n_l"], 16 * n + 2 * (g - 3))
                    for kk in range(2):
                        for m in range(MT):
                            c0 = (2 * g + kk) * P
                            ins = pe.transpose(bank[4 + g % 4][:, kk * T + m * P:kk * T + (m + 1) * P],
                                               xn[:, m, c0:c0 + P], ID[:, :])
                    ins.then_inc(s["n_t"], 1)
                pe.wait_ge(s["n_l"], 16 * n + 16)

            def phase(name):
                over_tiles(pe, name, tile)
                pe.wait_ge(s["tile_free"], last_tile(name) + 1)

            pe.wait_ge(s["masks"], 1)
            pe.wait_ge(s["vec_in"], 16 * N_VEC)
            pe.transpose(bank[0][:, 0:V_ROWS], WORK[0:V_ROWS, 0:P], ID[0:V_ROWS, 0:V_ROWS])
            pe.transpose(bank[0][:, V_ROWS:V_ROWS + 48], WORK[0:48, P:2 * P], ID[0:48, 0:48]).then_inc(s["vec_t"], 1)
            pe.wait_ge(s["cols_set"], 1)
            norm_t(0)
            phase("even_in")

            pe.wait_ge(s["masks"], 2)
            pe.wait_ge(s["aq_ready"], 3)
            q_t = BIG[:, 0:2, :].rearrange("p a b -> p (a b)")
            kd = WORK[:, 3584:4096].rearrange("p (m g c) -> p m g c", m=2, g=2)
            for g in range(5):
                if g == 4:
                    pe.wait_ge(s["qk_c"], 1)
                for kk in range(2):
                    for m in range(MT):
                        if g < 4:
                            pair = 2 * g + kk
                            o = (pair // 4) * 1024 + m * 512 + (pair % 4) * P
                            src = q_t[:, o:o + P]
                        else:
                            src = kd[:, m, kk, :]
                        ins = pe.transpose(bank[4 + g % 4][:, kk * T + m * P:kk * T + (m + 1) * P], src, ID[:, :])
                ins.then_inc(s["qk_t"], 1)
            pe.wait_ge(s["qk_c"], 5)
            qT = WORK[:, 0:2048].rearrange("p (k t) -> p k t", k=8)
            kT = WORK[:, 2048:2560].rearrange("p (k t) -> p k t", k=2)

            def attend(p, score, probs, pt, value, c0):
                for i in range(16 + 2):
                    if i < 16:
                        h = i
                        if h >= 2:
                            pe.wait_ge(s[p + "soft"], h - 1)
                        score(h, bank[4 + h % 2]).then_inc(s[p + "score"], 1)
                    if 1 <= i <= 16:
                        h = i - 1
                        pe.wait_ge(s[p + "pn"], h + 1)
                        if h >= 2:
                            pe.wait_ge(s[p + "ptc"], h - 1)
                        for b in range(3):
                            ins = pe.transpose(bank[6 + h % 2][:, b * P:(b + 1) * P],
                                               probs[:, h % 2, b * P:(b + 1) * P], ID[:, :])
                        ins.then_inc(s[p + "pt"], 1)
                    if i >= 2:
                        h = i - 2
                        j = h // 2
                        pe.wait_ge(s[p + "ptc"], h + 1)
                        if j >= 2:
                            pe.wait_ge(s["y_ready"], c0 + j - 1)
                        o = bank[j % 2][64 * (h % 2):64 * (h % 2) + 64, :]
                        mm(o[:, 0:T], value(h, 0), pt[:, h % 2, 0:T], True, False)
                        mm(o[:, P:T], value(h, 1), pt[:, h % 2, T:384], False, True).then_inc(s[p + "pv"], 1)

            def a_score(h, ps):
                r = slice(64 * (h % 2), 64 * (h % 2) + 64)
                q, k = qT[r, h // 2, :], kT[r, h // 8, :]
                mm(ps[:, 0:P], q[:, 0:P], k[:, 0:P], True, True)
                return mm(ps[:, P:384], q[:, P:T], k[:, 0:T], True, True)

            def a_value(h, m):
                o = m * 512 + P + 64 * (h // 8)
                return BIG[:, 2, o:o + 64]

            attend("a_", a_score, BIG[:, 0, 0:768].rearrange("p (b c) -> p b c", b=2),
                   BIG[:, 1, 0:768].rearrange("p (b c) -> p b c", b=2), a_value, 0)

            lgf = BIG[:, 0:2, :].rearrange("p a b -> p (a b)")
            msf = MS.rearrange("p l i -> p (l i)")
            qe = WORK[:, 1024:2048].rearrange("p (l i) -> p l i", l=8)
            ke = WORK[:, 2048:3072].rearrange("p (l i) -> p l i", l=8)
            am = WORK[:, 3072:4096].rearrange("p (l i) -> p l i", l=8)
            pe.wait_ge(s["b_x"], 2)
            pe.wait_ge(s["y_ready"], 8)

            def level_sums(u):
                h, m = u // 2, u % 2
                if u >= 1:
                    pe.wait_ge(s["b_lf"], u)
                pe.transpose(bank[4][:, m * P:(m + 1) * P], lgf[:, h * T + m * P:h * T + (m + 1) * P], ID[:, :])\
                    .then_inc(s["b_lt"], 1)
                pe.wait_ge(s["b_lf"], u + 1)
                if u >= 1:
                    pe.wait_ge(s["b_ex"], u)
                mm(bank[0][:, :], LFT[:, m, :], msf[:, 0:512], True, True)
                mm(bank[1][:, 0:384], LFT[:, m, :], msf[:, 512:896], True, True)
                mm(bank[1][:, 384:512], LFT[:, m, :], (GT if m == 0 else LE)[:, :], True, True)\
                    .then_inc(s["b_es"], 1)

            def values(u):
                h, m = u // 2, u % 2
                ts = slice(m * P, (m + 1) * P)
                o = bank[5 + 2 * (h % 2)]
                pe.wait_ge(s["b_am"], u + 1)
                if m == 0 and h >= 2:
                    pe.wait_ge(s["y_ready"], 8 + h - 1)
                v = BIG[:, 9 + h // 4, m * 512 + (h % 4) * P:m * 512 + (h % 4 + 1) * P]
                for l in range(8):
                    ins = mm(o[:, ts], v, am[:, l, :], l == 0, l == 7 and m == 0)
                ins.then_inc(s["b_lev"], 1)
                if m == 1:
                    pe.wait_ge(s["b_cx"], h + 1)
                    v0 = BIG[:, 9 + h // 4, (h % 4) * P:(h % 4 + 1) * P]
                    mm(o[:, ts], v0, CX, False, True).then_inc(s["b_ov"], 1)

            def products(u):
                h, m = u // 2, u % 2
                ts = slice(m * P, (m + 1) * P)
                pe.wait_ge(s["b_qe"], u + 1)
                pe.wait_ge(s["b_ke"], u + 1)
                if u >= 1:
                    pe.wait_ge(s["b_am"], u)
                for l in range(8):
                    dst = bank[2 + l // 4][:, (l % 4) * P:(l % 4 + 1) * P]
                    if l < LEVELS:
                        ins = mm(dst, ke[:, l, :], qe[:, l, :], True, True)
                    else:
                        ins = mm(dst, chan(7, h)[:, ts], chan(5, h)[:, ts], True, True)
                ins.then_inc(s["b_att"], 1)
                if m == 1:
                    pe.wait_ge(s["b_kx"], h + 1)
                    if h >= 1:
                        pe.wait_ge(s["b_cx"], h)
                    mm(bank[6][:, 0:P], KX, qe[:, 7, :], True, True).then_inc(s["b_cross"], 1)

            def square_sums(h):
                pe.wait_ge(s["b_sq"], h + 1)
                if h >= 1:
                    pe.wait_ge(s["b_rs"], h)
                mm(bank[5 + 2 * (h % 2)][:, T:2 * T], ONES[:, :], BSQ, True, True).then_inc(s["b_ss"], 1)

            for i in range(2 * B_HEADS + 4):
                if i < 2 * B_HEADS:
                    level_sums(i)
                if 0 <= i - 2 < 2 * B_HEADS:
                    values(i - 2)
                if 0 <= i - 1 < 2 * B_HEADS:
                    products(i - 1)
                if i >= 4 and i % 2 == 0:
                    square_sums((i - 4) // 2)
            pe.wait_ge(s["y_l"], 16)
            phase("even_out")

            norm_t(1)
            phase("odd_in")
            cS = WORK[:, 768:1536].rearrange("p (b c) -> p b c", b=2)
            cW = WORK[:, 1536:2304].rearrange("p (b c) -> p b c", b=2)
            for i in range(C_HEADS + 2):
                if i < C_HEADS:
                    h = i
                    ps = bank[4 + h % 2]
                    q, k = chan(0, h), chan(4, h)
                    if h >= 2:
                        pe.wait_ge(s["c_min"], h - 1)
                    mm(ps[:, 0:T], k[:, 0:P], q, True, True)
                    mm(ps[:, T:384], k[:, P:T], q[:, P:T], False, True).then_inc(s["c_z"], 1)
                if 1 <= i <= C_HEADS:
                    h = i - 1
                    ps = bank[4 + h % 2]
                    sp_ = cS[:, h % 2, :]
                    pe.wait_ge(s["c_sp"], 2 * (h + 1))
                    mm(ps[:, 0:384], NTRI[:, :], sp_, False, True)
                    mm(ps[:, P:T], NONES[:, :], sp_[:, T:384], False, True).then_inc(s["c_e"], 1)
                if i >= 2:
                    h = i - 2
                    pe.wait_ge(s["c_w"], h + 1)
                    if h >= 2:
                        pe.wait_ge(s["y_ready"], 16 + h - 1)
                    o = bank[6 + h % 2]
                    w = cW[:, h % 2, :]

                    def v(m):
                        return BIG[:, 8 + h // 4, m * 512 + (h % 4) * P:m * 512 + (h % 4 + 1) * P]

                    mm(o[:, 0:T], v(0), w[:, 0:T], True, False)
                    mm(o[:, P:T], v(1), w[:, T:384], False, True).then_inc(s["c_pv"], 1)
            pe.wait_ge(s["y_l"], 32)
            phase("odd_out")

            norm_t(2)
            phase("two_in")
            XBC = BIG[:, 11:14, :].rearrange("p a b -> p (a b)")
            pe.wait_ge(s["s_xbc"], 3)
            for g in range(4):
                m, hh = g // 2, g % 2
                if g >= 2:
                    pe.wait_ge(s["s_xd"], g - 1)
                for j in range(4):
                    k = 4 * hh + j
                    ins = pe.transpose(bank[g % 2][:, j * P:(j + 1) * P],
                                       XBC[:, k * T + m * P:k * T + (m + 1) * P], ID[:, :])
                ins.then_inc(s["s_xt"], 1)
            for g in range(2):
                B, C = XBC[:, (8 + g) * T:(9 + g) * T], XBC[:, (10 + g) * T:(11 + g) * T]
                mm(bank[2 + g][:, 0:T], B[:, 0:P], C, True, True)
                mm(bank[2 + g][:, T:384], B[:, P:T], C[:, P:T], False, True).then_inc(s["s_cb"], 1)
            XD = BIG[:, 14:16, :].rearrange("p a b -> p (a b)").rearrange("p (m h d) -> p m h d", m=2, h=16)
            ag = WORK[:, 0:768].rearrange("p (b c) -> p b c", b=2)
            sL = WORK[:, 1792:2560].rearrange("p (b c) -> p b c", b=2)
            pe.wait_ge(s["s_xd"], 4)
            for i in range(S_HEADS + 1):
                if i < S_HEADS:
                    h = i
                    g = ag[:, h % 2, :]
                    ps = bank[4 + h % 2]
                    pe.wait_ge(s["s_ag"], h + 1)
                    if h >= 2:
                        pe.wait_ge(s["s_ex"], h - 1)
                    mm(ps[:, 0:P], g[:, 0:P], LE[:, :], True, False)
                    mm(ps[:, P:T], g[:, 0:P], ONES[:, :], False, False)
                    mm(ps[:, P:T], g[:, P:T], LE[:, :], False, False)
                    mm(ps[:, T:384], g[:, T:384], LE[:, :], False, True).then_inc(s["s_seg"], 1)
                if i >= 1:
                    h = i - 1
                    j = h // 2
                    pe.wait_ge(s["s_l"], h + 1)
                    if j >= 2:
                        pe.wait_ge(s["s_yg"], j - 1)
                    o = bank[j % 2][64 * (h % 2):64 * (h % 2) + 64, :]
                    mm(o[:, 0:T], XD[:, 0, h, :], sL[:, h % 2, 0:T], True, False)
                    mm(o[:, P:T], XD[:, 1, h, :], sL[:, h % 2, T:384], False, True).then_inc(s["s_y"], 1)
            SQ = WORK[:, 768:1792].rearrange("p (j t) -> p j t", j=4)
            for g in range(2):
                pe.wait_ge(s["s_sq"], g + 1)
                if g == 1:
                    pe.wait_ge(s["s_rs"], 1)
                for j in range(4):
                    ins = mm(bank[6][:, 0:T], ONES[:, :], SQ[:, j, :], j == 0, j == 3)
                ins.then_inc(s["s_ss"], 1)

            lg = WORK[:, 0:768].rearrange("p (b c) -> p b c", b=2)
            pe.wait_ge(s["y_ready"], 40)
            pe.wait_ge(s["s_rs"], 2)

            def f_score(h, ps):
                r = slice(64 * (h % 2), 64 * (h % 2) + 64)
                q, k = chan(5, h // 2)[r, :], chan(7, h // 2)[r, :]
                g = lg[:, h % 2, :]
                pe.wait_ge(s["f_lg"], h + 1)
                mm(ps[:, 0:P], q[:, 0:P], k[:, 0:P], True, False)
                mm(ps[:, P:384], q[:, P:T], k, False, False)
                mm(ps[:, 0:P], LE[:, :], g[:, 0:P], False, False)
                mm(ps[:, P:T], ONES[:, :], g[:, 0:P], False, False)
                return mm(ps[:, P:384], LE[:, :], g[:, P:384], False, True)

            def f_value(h, m):
                o = m * 512 + (h % 8) * 64
                return BIG[:, 9 + h // 8, o:o + 64]

            attend("f_", f_score, WORK[:, 1536:2304].rearrange("p (b c) -> p b c", b=2),
                   WORK[:, 2304:3072].rearrange("p (b c) -> p b c", b=2), f_value, 40)
            pe.wait_ge(s["y_l"], 48)
            phase("two_out")

            norm_t(3)
            phase("peer_q")
            keys = RAW[:, 0, :].rearrange("p (f d) -> p f d", f=16)
            kTp = BIG[:, 4:6, :].rearrange("p a b -> p (a b)").rearrange("p (f d) -> p f d", f=16)
            pe.wait_ge(s["k_in"], 32)
            for g in range(4):
                for j in range(4):
                    ins = pe.transpose(bank[4 + g][:, j * P:(j + 1) * P], keys[:, 4 * g + j, :], ID[:, :])
                ins.then_inc(s["k_t"], 1)
            pe.wait_ge(s["k_c"], 4)
            for g in range(8):
                m = g // 4
                if g >= 4:
                    pe.wait_ge(s["q_sc"], g - 3)
                for j in range(4):
                    f = 4 * (g % 4) + j
                    ins = mm(bank[g % 4][:, j * P:(j + 1) * P], chan(0, f)[:, m * P:(m + 1) * P], kTp[:, f, :],
                             True, True)
                ins.then_inc(s["q_s"], 1)
            gate = WORK[:, 1024:1280].rearrange("p (m n) -> p m n", m=2)

            def turn(n, j, g, full, fresh):
                if g == 0:
                    pe.wait_ge(s[f"row_full{j}"], full)
                if not fresh:
                    pe.wait_ge(s["t_l"], 4 * n + (g - 3))
                for b in range(4):
                    c0 = (4 * g + b) * P
                    ins = pe.transpose(bank[4 + g][:, b * P:(b + 1) * P], RAW[:, j, c0:c0 + P], ID[:, :])
                ins.then_inc(s["t_t"], 1)

            def products(n, j, g, fresh):
                if g == 0 and not fresh:
                    pe.wait_ge(s["a_gelu"], n - 1)
                pe.wait_ge(s["t_l"], 4 * n + g + 1)
                for b in range(4):
                    kt = 4 * g + b
                    sl, cs = 4 * (j % 2) + g, slice(b * P, (b + 1) * P)
                    dst = bank[j % 2][:, 0:T]
                    mm(dst, WH[:, sl, cs], HH[:, kt, :], kt == 0, False)
                    mm(dst, WH[:, sl, cs], HL[:, kt, :], False, False)
                    ins = mm(dst, WL[:, sl, cs], HH[:, kt, :], False, kt == KT - 1)
                ins.then_inc(s["u_used"], 1)

            def spread(g, b, fresh):
                pe.wait_ge(s["oh2"], g + 1)
                pe.wait_ge(s["ohg"], g + 1)
                if not fresh:
                    pe.wait_ge(s["g_mul"], g - 1)
                for t in range(TG):
                    for c in range(3):
                        ins = mm(bank[2 + b][:, t * QR:(t + 1) * QR], OH2[:, b, t, :], OHG[:, b, c, t, :],
                                 c == 0, c == 2)
                ins.then_inc(s["g_mm"], 1)

            def outputs(n, j, start):
                pe.wait_ge(s["p_l"], n + 1)
                pe.wait_ge(s["v_l"], n + 1)
                for m in range(MT):
                    ms = slice(m * P, (m + 1) * P)
                    for nn in range(4):
                        sl = 4 * (j % 2) + nn
                        dst = bank[4 * m + nn][:, :]
                        mm(dst, PS[:, j % 2, 0, ms], WH[:, sl, :], start, False)
                        mm(dst, PS[:, j % 2, 1, ms], WH[:, sl, :], False, False)
                        ins = mm(dst, PS[:, j % 2, 0, ms], WL[:, sl, :], False, False)
                ins.then_inc(s["o_mm"], 1)

            for seg, (kind, k) in enumerate(SEGMENTS):
                n0 = QR * k
                full = (QR // 4) * seg
                g0 = QR * (k - 1)
                after_out = seg > 0 and SEGMENTS[seg - 1][0] == "out"
                added = 8 * (SEGMENTS[seg - 1][1]) if after_out else 0
                if kind == "in":
                    if k == 1:
                        for m in range(MT):
                            pe.wait_ge(s["tk_idx"], m + 1)
                            for f in range(3):
                                n = 3 * m + f
                                if n >= 2:
                                    pe.wait_ge(s["tk_tc"], n - 1)
                                src = SEL[:, m, f, :] if f < 2 else gate[:, m, :]
                                pe.transpose(bank[2 + n % 2][:, 0:P], src, ID[:, :]).then_inc(s["tk_t"], 1)
                        pe.wait_ge(s["tk_tc"], 6)
                    for j in range(4):
                        for g in range(4):
                            if after_out and j == 0:
                                pe.wait_ge(s["o_add"], added + g + 1)
                            turn(n0 + j, j, g, 16 * (full + 1), seg == 0 and j == 0)
                            if j >= 1:
                                if after_out and g == 0 and j <= 2:
                                    pe.wait_ge(s["o_add"], added + 4 + j)
                                products(n0 + j - 1, j - 1, g, seg == 0 and j <= 2)
                        if k >= 1:
                            if after_out and j < 2:
                                pe.wait_ge(s["o_add"], added + 7 + j)
                            spread(g0 + j, j % 2, k == 1 and j < 2)
                    with pe.Fori(1, QR // 4) as q:
                        for j in range(4):
                            for g in range(4):
                                turn(4 * q + (n0 + j), j, g, 16 * q + 16 * (full + 1), False)
                                products(4 * q + (n0 + j - 1), (j + 3) % 4, g, False)
                            if k >= 1:
                                spread(4 * q + (g0 + j), j % 2, False)
                    for g in range(4):
                        products(n0 + QR - 1, 3, g, False)
                else:
                    if k == QUARTERS - 1:
                        pe.wait_ge(s["o_add"], 8 * k)
                        for b in range(2):
                            spread(n0 + b, b, False)
                        with pe.Fori(1, QR // 2) as q:
                            for b in range(2):
                                spread(2 * q + (n0 + b), b, False)
                    u_tiles = QR * (1 + max(kk for kd, kk in SEGMENTS[:seg] if kd == "in"))
                    pe.wait_ge(s["a_gelu"], u_tiles)
                    pe.wait_ge(s["g_mul"], n0 + QR)
                    for j in range(4):
                        outputs(n0 + j, j, j == 0)
                    with pe.Fori(1, QR // 4) as q:
                        for j in range(4):
                            outputs(4 * q + (n0 + j), j, False)


_INS = ["x", "ln_even", "w_in_even", "q_norm_a", "k_norm_a", "sinks_a", "lower_bounds", "g_norm_b",
        "w_out_even", "ln_odd", "w_in_odd", "w_out_odd", "ln1_w_2", "w_in_2", "conv_w_2", "conv_b_2",
        "dt_bias_2", "a_log_2", "d_skip_2", "ssd_norm_w_2", "fox_f_bias_2", "w_out_2", "ln2_w_2",
        "peer_wq_2", "peer_k1_2", "peer_k2_2", "peer_u_2", "peer_v_2", "lnf_w_2"]
_LAYERED = ("w_in_even", "w_out_even", "w_in_odd", "w_out_odd")


def rope_tables():
    half = A_HD // 2
    inv = (1.0 / (np.float32(10000.0) ** (np.arange(half, dtype=np.float32) / np.float32(half)))).astype(np.float32)
    ang = np.arange(T, dtype=np.float32)[:, None] * inv[None, :]
    return np.cos(ang), np.sin(ang)


def kernel(**inputs):
    import concourse.bacc as _bacc
    from concourse.bass_utils import run_bass_kernel_spmd as _run

    nc = _bacc.Bacc("TRN2", target_bir_lowering=False, num_devices=1)
    arrays, args = {}, {}
    cos, sin = rope_tables()
    for name in _INS + ["rope_cos", "rope_sin"]:
        v = cos if name == "rope_cos" else sin if name == "rope_sin" else np.ascontiguousarray(inputs[name])
        arrays[f"in_{name}_dram"] = v
        ap = nc.dram_tensor(f"in_{name}_dram", v.shape, mybir.dt.from_np(v.dtype), kind="ExternalInput").ap()
        args[name] = ap[0] if name in _LAYERED else ap
    out = nc.dram_tensor("out_0_dram", (1, T, D), F32, kind="ExternalOutput").ap()
    two_blocks(nc, args, out)
    r = _run(nc, [arrays], core_ids=[0])
    return r.results[0]["out_0_dram"]
```

```python
from contextlib import ExitStack

import numpy as np

import concourse.bass as bass
from concourse import mybir

F32 = mybir.dt.float32
F32R = mybir.dt.float32r
U32 = mybir.dt.uint32
BF16 = mybir.dt.bfloat16
ALU = mybir.AluOpType
ACT = mybir.ActivationFunctionType
AX = mybir.AxisListType

P = 128
T = 256
MT = T // P
D = 2048
KT = D // P
NW = 512
EPS = 1e-6
NEG = -1e30
LN2 = 0.6931471805599453

A_HEADS, A_KV, A_HD = 16, 2, 64
B_HEADS, B_HD = 8, 128
C_HEADS, C_HD = 16, 128
S_HEADS, S_HD, S_STATE = 16, 64, 128
F_HEADS, F_HD = 16, 64
LEVELS = 7
PE_HEADS, PE_KEYS, PE_TOP = 8, 128, 16
QUARTERS = 4
QR = PE_KEYS // QUARTERS
TG = 8
SEGMENTS = [("in", 0), ("in", 1), ("out", 0), ("in", 2), ("out", 1), ("in", 3), ("out", 2), ("out", 3)]

V_LN = 0
V_SSDN = 64
V_CB = 72
V_LB = 84
V_GN = 92
V_ROWS = 93
V_CW = 93
V_COLS = V_CW + 48


def runs():
    out = []
    base = 0
    for phase, rs in (
        ("even_in", [("w_in_even", 0, 512, 2, "tok", 0), ("w_in_even", 1024, 256, 1, "tok", 2),
                     ("w_in_even", 1280, 512, 4, "silu", 3), ("w_in_even", 3328, 512, 2, "chan", 7),
                     ("w_in_even", 4352, 512, 2, "tok", 9), ("w_in_even", 5376, 512, 2, "silu", 11)]),
        ("even_out", [("w_out_even", 0, 512, 4, "res", 0)]),
        ("odd_in", [("w_in_odd", 0, 512, 4, "scaled", 0), ("w_in_odd", 2048, 512, 4, "chan", 4),
                    ("w_in_odd", 4096, 512, 4, "tok", 8), ("w_in_odd", 6144, 512, 4, "silu", 12)]),
        ("odd_out", [("w_out_odd", 0, 512, 4, "res", 0)]),
        ("two_in", [("w_in_2", 5648, 16, 1, "gate", 1), ("w_in_2", 2576, 512, 2, "eighth", 5),
                    ("w_in_2", 3600, 512, 2, "chan", 7), ("w_in_2", 4624, 512, 2, "tok", 9),
                    ("w_in_2", 2560, 16, 1, "gate", 0), ("w_in_2", 1024, 512, 3, "chan", 2),
                    ("w_in_2", 0, 512, 2, "silu", 0)]),
        ("two_out", [("w_out_2", 0, 512, 4, "res", 0)]),
        ("peer_q", [("peer_wq_2", 0, 512, 4, "chan", 0)]),
    ):
        for w, c0, width, n, kind, dest in rs:
            out.append(dict(phase=phase, w=w, c0=c0, width=width, n=n, kind=kind, dest=dest, base=base))
            base += n
    return out


RUNS = runs()
PHASES = ["even_in", "even_out", "odd_in", "odd_out", "two_in", "two_out", "peer_q"]


def last_tile(phase):
    return max(r["base"] + r["n"] for r in RUNS if r["phase"] == phase) - 1


N_TILES = last_tile("peer_q") + 1

A_PREPARE, A_PREPARE_STEPS = 29, 15
A_TURN = A_PREPARE + 2 * A_PREPARE_STEPS - 2
A_FIRST = A_TURN + 3
TWO_TILE = last_tile("odd_out") + 1
ODD_TILE = last_tile("even_out") + 1
C_FIRST = 8 * ODD_TILE + 70
C_STEPS = C_HEADS + 3
C_ACT_LAG, C_DVE_LAG = 2, 3
F_GATE = 8 * TWO_TILE + 14
F_FIRST = 8 * TWO_TILE + 47
S_GATE = 8 * TWO_TILE + 70
S_CONV = 8 * TWO_TILE + 86
ATTEND_STEPS = 16 + 3
DVE_LAG, ACT_LAG = 2, 3


def step_at(place, first, every, steps):
    k, r = divmod(place - first, every)
    return k if r == 0 and 0 <= k < steps else None


def over_tiles(eng, phase, body):
    for r in [r for r in RUNS if r["phase"] == phase]:
        body(r, 0, r["base"] % 2, True)
        pairs = (r["n"] - 1) // 2
        if pairs > 1:
            with eng.Fori(0, pairs) as q:
                for j in range(2):
                    body(r, 2 * q + (1 + j), (r["base"] + 1 + j) % 2, False)
        else:
            for i in range(1, 1 + 2 * pairs):
                body(r, i, (r["base"] + i) % 2, False)
        for i in range(1 + 2 * pairs, r["n"]):
            body(r, i, (r["base"] + i) % 2, False)


class Chain:

    def __init__(self, eng, sem):
        self.eng, self.sem, self.n = eng, sem, 0

    def link(self, ins):
        self.n += 1
        ins.then_inc(self.sem, 1)
        self.eng.wait_ge(self.sem, self.n)


def two_blocks(nc, a, out):
    ctx = ExitStack()
    with ctx:
        def sb(name, shape, dt=F32):
            return ctx.enter_context(nc.sbuf_tensor(name, shape, dt))

        def sem(name):
            return ctx.enter_context(nc.semaphore(name))

        HH = sb("HH", [P, KT, T], F32R)
        HL = sb("HL", [P, KT, T], F32R)
        WH = sb("WH", [P, 8, NW], F32R)
        WL = sb("WL", [P, 8, NW], F32R)
        PS = sb("PS", [P, 2, 2, T], F32R)
        RAW = sb("RAW", [P, 4, 2048])
        XR = sb("XR", [P, MT, D])
        BIG = sb("BIG", [P, 16, 1024])
        WORK = sb("WORK", [P, 4096])
        YB = sb("YB", [P, 2, T])
        ID = sb("ID", [P, P])
        LE = sb("LE", [P, P])
        GT = sb("GT", [P, P])
        ONES = sb("ONES", [P, P])
        NTRI = sb("NTRI", [P, P])
        NONES = sb("NONES", [P, P])
        AMASK = sb("AMASK", [P, 384])
        FMASK = sb("FMASK", [P, 384])
        COLS = sb("COLS", [P, V_COLS])
        ROPE = sb("ROPE", [P, 2, MT, 32])
        BC = sb("BC", [P, 208])
        SM = sb("SM", [P, 160])
        DTF = sb("DTF", [P, 2, MT, 16])
        bank = [ctx.enter_context(nc.psum_tensor(f"bank{i}", [P, 512], F32)) for i in range(8)]

        names = """
            const_in vec_in masks vec_t cols_set x_in lnf_in out_done eps_set act_chain dve_chain pool_chain
            w_full0 w_full1 w_full2 w_full3 wh_done wl_done ws_used tile_free
            n_rstd n_x n_t n_h n_l y_ready y_h y_l
            aq_ready qk_t qk_c
            a_score a_soft a_exp a_rcp a_pn a_pt a_ptc a_pv
            f_score f_soft f_exp f_rcp f_pn f_pt f_ptc f_pv f_lg f_lf f_v f_e
            b_vec b_e b_lsg b_kin b_x b_ml b_lt b_lf b_es b_ex b_qe b_ke b_att b_am b_cross b_cx b_kx b_lev b_ov
            b_sq b_ss b_rs
            c_mask c_z c_exp c_sp c_e c_min c_w c_pv c_out
            s_dt s_e s_a s_conv s_xbc s_xt s_xd s_cb s_cbm s_ag s_seg s_ex s_l s_y s_yg s_sq s_ss s_rs
            k_in k_t k_c q_s q_sc tk_iota tk_idx tk_e tk_g tk_t tk_tc tk_parts oh1 oh2 ohg g_mm g_mul
            row_full0 row_full1 row_full2 row_full3 u_used t_t t_h t_l a_gelu p_h p_l v_h v_l o_mm o_add
            """.split()
        s = {n: sem(n) for n in names}

        A_QN, A_KN, A_SINK, S_DTB, S_AL, F_FB, S_DSK, S_DSKC = 0, 64, 128, 144, 160, 176, 192, 152
        DSK = SM[:, 0:8]
        bq, bf, bi, bg = BIG[:, 5:7, :], BIG[:, 7:9, :], BIG[:, 9:11, :], BIG[:, 11:13, :]
        even_spare = BIG[:, 13:16, :].rearrange("p a b -> p (a b)")
        MS = even_spare[:, 0:LEVELS * P].rearrange("p (l i) -> p l i", l=LEVELS)
        MK = even_spare[:, 896:896 + 1024].rearrange("p (l i) -> p l i", l=8)
        KX = even_spare[:, 1920:2048]
        CX = even_spare[:, 2048:2176]
        LFT = even_spare[:, 2176:2432].rearrange("p (b c) -> p b c", b=2)
        BSQ = even_spare[:, 2432:2688]
        BRS = even_spare[:, 2688:2944]
        CM = WORK[:, 3072:3456]
        CN = WORK[:, 3456:3840]

        def two_slots(view):
            return view.rearrange("p (b c) -> p b c", b=2)

        A_S, A_PROBS, A_PT = (two_slots(WORK[:, 2560:3328]), two_slots(WORK[:, 3328:4096]),
                              two_slots(even_spare[:, 1920:2688]))
        F_S, F_PROBS, F_PT = (two_slots(WORK[:, 768:1536]), two_slots(WORK[:, 1536:2304]),
                              two_slots(WORK[:, 2304:3072]))
        C_T, C_SP, C_W = (two_slots(WORK[:, 0:768]), two_slots(WORK[:, 768:1536]), two_slots(WORK[:, 1536:2304]))
        S_AEX, S_DT, F_TMP, S_TMP = WORK[:, 3712:3728], WORK[:, 3728:3760], WORK[:, 3760:3792], WORK[:, 3792:3824]

        def chan(tile0, kt):
            return BIG[:, tile0 + kt // 4, (kt % 4) * T:(kt % 4 + 1) * T]

        GB = [BIG[:, 8 * b:8 * b + 8, :].rearrange("p a b -> p (a b)").rearrange("p (i t) -> p i t", t=T)
              for b in range(2)]
        OH2 = WORK[:, 0:1024].bitcast(BF16).rearrange("p (b t i) -> p b t i", b=2, t=TG)
        OHG = WORK[:, 1024:1792].bitcast(BF16).rearrange("p (b c t i) -> p b c t i", b=2, c=3, t=TG)
        OH1 = WORK[:, 1792:2048].bitcast(BF16).rearrange("p (b t i) -> p b t i", b=2, t=TG)
        SEL = WORK[:, 2048:2560].rearrange("p (m f n) -> p m f n", m=2, f=2)
        G3 = WORK[:, 2560:2944].bitcast(BF16).rearrange("p (c t) -> p c t", c=3)
        TKT = WORK[:, 3072:3840].rearrange("p (a t) -> p a t", a=3)
        IOTA = WORK[:, 3840:3968]

        block = ctx.enter_context(nc.Block())

        @block.sync
        def _(sp):
            def load_tile(r, i, parity, first):
                t = r["base"] + i
                w = a[r["w"]]
                src = w.rearrange("(k p) n -> p k n", p=P)
                for j in range(4):
                    if r["base"] > 0 or not first:
                        sp.wait_ge(s["wl_done"], 8 * (t - 1) + 2 * (j + 1))
                    dst = RAW[:, j, :].rearrange("p (k n) -> p k n", k=4)[:, :, 0:r["width"]]
                    c = bass.ds(r["c0"] + i * r["width"], r["width"])
                    sp.dma_start(dst, src[:, 4 * j:4 * j + 4, c]).then_inc(s[f"w_full{j}"], 16)

            for ph in PHASES:
                over_tiles(sp, ph, load_tile)

            sp.wait_ge(s["wl_done"], 8 * N_TILES)
            keys = RAW[:, 0, :].rearrange("p (h f d) -> p h f d", h=PE_HEADS, f=2)
            for f, name in enumerate(("peer_k1_2", "peer_k2_2")):
                sp.dma_start(keys[:, :, f, :], a[name].rearrange("h n d -> n h d")).then_inc(s["k_in"], 16)

            u_rows = a["peer_u_2"].rearrange("(i j) d -> i j d", j=PE_KEYS)
            v_rows = a["peer_v_2"].rearrange("(i j) d -> i j d", j=PE_KEYS)

            def load_rows(kind, n, j):
                sp.dma_start(RAW[:, j, :], (u_rows if kind == "in" else v_rows)[n, :, :])\
                    .then_inc(s[f"row_full{j}"], 16)

            def wait_split(kind, tiles):
                sp.wait_ge(s["t_l" if kind == "in" else "v_l"], tiles * (4 if kind == "in" else 1))

            for seg, (kind, k) in enumerate(SEGMENTS):
                n0 = QR * k
                for j in range(4):
                    if seg == 0:
                        if j == 0:
                            sp.wait_ge(s["k_t"], 4)
                    else:
                        before, kb = SEGMENTS[seg - 1]
                        wait_split(before, QR * (kb + 1) - 3 + j)
                    load_rows(kind, n0 + j, j)
                with sp.Fori(1, QR // 4) as q:
                    for j in range(4):
                        wait_split(kind, 4 * q + (n0 + j - 3))
                        load_rows(kind, 4 * q + (n0 + j), j)

            for m in range(MT):
                sp.wait_ge(s["n_x"], 9 + m)
                sp.dma_start(out[0].rearrange("(m p) d -> p m d", p=P)[:, m, :],
                             BIG[:, 2 * m:2 * m + 2, :].rearrange("p a b -> p (a b)")).then_inc(s["out_done"], 16)
            sp.wait_ge(s["out_done"], 16 * MT)

        N_CONST = 9
        N_VEC = 12

        @block.gpsimd
        def _(pool):
            ch = Chain(pool, s["pool_chain"])
            link = ch.link
            pool.dma_start(XR[:, :, :], a["x"][0].rearrange("(m p) d -> p m d", p=P)).then_inc(s["x_in"], 16)
            vec, vecw = WORK[:, 0:P], WORK[:, P:2 * P]
            row = 0
            for name, n in (("ln_even", 16), ("ln_odd", 16), ("ln1_w_2", 16), ("ln2_w_2", 16),
                            ("ssd_norm_w_2", 8), ("conv_b_2", 12), ("lower_bounds", 8), ("g_norm_b", 1)):
                v = a[name]
                if name in ("ln_even", "ln_odd", "lower_bounds", "g_norm_b"):
                    v = v[0]
                pool.dma_start(vec[row:row + n, :], v.rearrange("(k p) -> k p", p=P)).then_inc(s["vec_in"], 16)
                row += n
            for tap in range(4):
                pool.dma_start(vecw[12 * tap:12 * tap + 12, :],
                               a["conv_w_2"][tap].rearrange("(k p) -> k p", p=P)).then_inc(s["vec_in"], 16)
            for name, at, n in (("q_norm_a", A_QN, 64), ("k_norm_a", A_KN, 64), ("sinks_a", A_SINK, 16),
                                ("dt_bias_2", S_DTB, 16), ("a_log_2", S_AL, 16), ("fox_f_bias_2", F_FB, 16),
                                ("d_skip_2", S_DSK, 16)):
                v = a[name][0] if name in ("q_norm_a", "k_norm_a", "sinks_a") else a[name]
                pool.dma_start(BC[:, at:at + n], v.partition_broadcast(P)).then_inc(s["const_in"], 16)
            for i, name in enumerate(("rope_cos", "rope_sin")):
                pool.dma_start(ROPE[:, i, :, :], a[name].rearrange("(m p) f -> p m f", p=P)).then_inc(s["const_in"], 16)

            def select(view, op, fill, base, pattern, cm):
                link(pool.affine_select(out=view, in_=view, compare_op=op, fill=fill, base=base,
                                        pattern=pattern, channel_multiplier=cm))

            for tile, v in ((ONES, 1.0), (ID, 1.0), (LE, 1.0), (GT, 1.0), (NTRI, -1.0), (NONES, -1.0),
                            (AMASK, 0.0), (FMASK, 0.0)):
                link(pool.memset(tile[:, :], v))
            select(ID[:, :], ALU.is_equal, 0.0, 0, [[-1, P]], 1)
            pool.sem_inc(s["masks"], 1)
            select(LE[:, :], ALU.is_ge, 0.0, 0, [[1, P]], -1)
            select(GT[:, :], ALU.is_gt, 0.0, 0, [[-1, P]], 1)
            select(NTRI[:, :], ALU.is_ge, 0.0, 0, [[-1, P]], 1)
            select(AMASK[:, 0:P], ALU.is_ge, NEG, 0, [[-1, P]], 1)
            select(AMASK[:, P:2 * P], ALU.is_gt, NEG, 0, [[1, P]], -1)
            select(AMASK[:, 2 * P:3 * P], ALU.is_ge, NEG, 0, [[-1, P]], 1)
            select(FMASK[:, 0:P], ALU.is_ge, NEG, 0, [[-1, P]], 1)
            select(FMASK[:, 2 * P:3 * P], ALU.is_ge, NEG, 0, [[-1, P]], 1)
            link(pool.memset(even_spare[:, 0:1920], 1.0))
            for l in range(LEVELS):
                h = 1 << l
                nb = P // (2 * h)
                ms = MS[:, l, :].rearrange("p (b s r) -> p b s r", b=nb, s=2)
                select(ms[:, :, 1, :], ALU.is_ge, 0.0, -h, [[-2 * h, nb], [0, h]], 1)
                select(ms[:, :, 1, :], ALU.is_ge, 0.0, h, [[2 * h, nb], [1, h]], -1)
                select(ms[:, :, 0, :], ALU.is_gt, 0.0, 0, [[-2 * h, nb], [-1, h]], 1)
                select(ms[:, :, 0, :], ALU.is_gt, 0.0, h, [[2 * h, nb], [0, h]], -1)
                mk = MK[:, l, :].rearrange("p (b s r) -> p b s r", b=nb, s=2)
                select(mk[:, :, 1, :], ALU.is_ge, 0.0, 0, [[-2 * h, nb], [0, h]], 1)
                select(mk[:, :, 1, :], ALU.is_gt, 0.0, h, [[2 * h, nb], [0, h]], -1)
                link(pool.memset(mk[:, :, 0, :], 0.0))
            select(MK[:, LEVELS, :], ALU.is_equal, 0.0, 0, [[-1, P]], 1)
            pool.wait_ge(s["const_in"], 16 * N_CONST)
            link(pool.tensor_copy(DSK[0:64, :], BC[0:64, S_DSK:S_DSK + 16:2]))
            link(pool.tensor_copy(DSK[64:128, :], BC[64:128, S_DSK + 1:S_DSK + 16:2]))
            pool.sem_inc(s["masks"], 1)

            def normalise(p, probs):
                for h in range(16):
                    pool.wait_ge(s[p + "rcp"], h + 1)
                    rc = SM[:, 24 + 2 * (h % 2):26 + 2 * (h % 2)]
                    pr = probs[:, h % 2, :]
                    pool.tensor_scalar(pr[:, 0:P], pr[:, 0:P], rc[:, 0:1], None, ALU.mult)
                    pool.tensor_scalar(pr[:, P:384], pr[:, P:384], rc[:, 1:2], None, ALU.mult)\
                        .then_inc(s[p + "pn"], 1)

            normalise("a_", A_PROBS)

            ke = WORK[:, 2048:3072].rearrange("p (l i) -> p l i", l=8)
            for u in range(2 * B_HEADS):
                h, m = u // 2, u % 2
                pool.wait_ge(s["b_ex"], u + 1)
                if u >= 1:
                    pool.wait_ge(s["b_att"], u)
                ex = WORK[:, 0:1024].rearrange("p (l i) -> p l i", l=8)
                k = chan(7, h)[:, m * P:(m + 1) * P]
                kk = k.unsqueeze(1).broadcast_to([P, 8, P])
                pool.tensor_tensor(ke, ex, kk, ALU.mult).then_inc(s["b_ke"], 1)
                if m == 0:
                    if h >= 1:
                        pool.wait_ge(s["b_cross"], h)
                    pool.tensor_tensor(KX, ex[:, 7, :], k, ALU.mult).then_inc(s["b_kx"], 1)

            pool.wait_ge(s["y_l"], 16)
            link(pool.memset(CM, 1.0))
            link(pool.memset(CN, 0.0))
            for d0 in (0, 256):
                select(CM[:, d0:d0 + P], ALU.is_gt, 0.0, 0, [[1, P]], -1)
                select(CN[:, d0:d0 + P], ALU.is_gt, NEG, 0, [[1, P]], -1)
            pool.sem_inc(s["c_mask"], 1)

            lg = WORK[:, 0:768].rearrange("p (b c) -> p b c", b=2)
            lf = SM[:, 96:128].rearrange("p (m h) -> p m h", m=2)
            pool.wait_ge(s["f_lf"], 1)
            probs = F_PROBS
            for i in range(F_HEADS + 2):
                if i < F_HEADS:
                    h = i
                    if h >= 2:
                        pool.wait_ge(s["f_score"], h - 1)
                    g = lg[:, h % 2, :]
                    pool.tensor_scalar(g[:, 0:P], GT[:, :], lf[:, 0, h:h + 1], None, ALU.mult)
                    pool.tensor_scalar(g[:, P:256], ONES[:, :], lf[:, 1, h:h + 1], None, ALU.mult)
                    pool.tensor_scalar(g[:, 256:384], GT[:, :], lf[:, 1, h:h + 1], None, ALU.mult)\
                        .then_inc(s["f_lg"], 1)
                if i >= 2:
                    h = i - 2
                    pool.wait_ge(s["f_rcp"], h + 1)
                    rc = SM[:, 24 + 2 * (h % 2):26 + 2 * (h % 2)]
                    pr = probs[:, h % 2, :]
                    pool.tensor_scalar(pr[:, 0:P], pr[:, 0:P], rc[:, 0:1], None, ALU.mult)
                    pool.tensor_scalar(pr[:, P:384], pr[:, P:384], rc[:, 1:2], None, ALU.mult)\
                        .then_inc(s["f_pn"], 1)

            ag = WORK[:, 0:768].rearrange("p (b c) -> p b c", b=2)
            pool.wait_ge(s["s_a"], 1)
            pool.wait_ge(s["f_score"], F_HEADS)
            acol = SM[:, 64:96].rearrange("p (m h) -> p m h", m=2)
            for h in range(S_HEADS):
                if h >= 2:
                    pool.wait_ge(s["s_seg"], h - 1)
                g = ag[:, h % 2, :]
                pool.tensor_scalar(g[:, 0:P], GT[:, :], acol[:, 0, h:h + 1], None, ALU.mult)
                pool.tensor_scalar(g[:, P:256], ONES[:, :], acol[:, 1, h:h + 1], None, ALU.mult)
                pool.tensor_scalar(g[:, 256:384], GT[:, :], acol[:, 1, h:h + 1], None, ALU.mult)\
                    .then_inc(s["s_ag"], 1)

            pool.wait_ge(s["y_l"], 48)
            iota_i = WORK[:, 3968:4096].bitcast(mybir.dt.int32)
            link(pool.iota(iota_i, [[1, P]], base=0, channel_multiplier=0))
            pool.tensor_copy(IOTA, iota_i).then_inc(s["tk_iota"], 1)
            pool.wait_ge(s["tk_parts"], 1)
            for k in range(QUARTERS):
                with pool.Fori(0, QR // 2) as q:
                    for b in range(2):
                        pool.wait_ge(s["oh1"], 2 * q + (QR * k + b + 1))
                        t0 = 2 * TG * q + TG * b
                        pool.tensor_tensor(OHG[:, b, :, :, :],
                                           OH1[:, b, :, :].unsqueeze(1).broadcast_to([P, 3, TG, QR]),
                                           G3[:, :, bass.ds(t0, TG)].unsqueeze(3).broadcast_to([P, 3, TG, QR]),
                                           ALU.mult).then_inc(s["ohg"], 1)

            pool.wait_ge(s["g_mm"], QR * QUARTERS)
            pool.dma_start(WORK[:, 0:2048], a["lnf_w_2"].partition_broadcast(P)).then_inc(s["lnf_in"], 16)

        @block.scalar
        def _(act):
            ch = Chain(act, s["act_chain"])
            link = ch.link
            pending = []

            def leave(r, i, parity, t):
                kind = r["kind"]
                act.wait_ge(s["ws_used"], 8 * (t + 1))
                if kind == "res":
                    return
                for b in range(2):
                    ps = bank[2 * parity + b]
                    if kind == "gate":
                        dst, src = DTF[:, r["dest"], b, :], ps[:, 0:16]
                    elif kind == "tok" or kind in ("chan", "silu", "scaled", "eighth"):
                        w = r["width"]
                        dst = BIG[:, bass.ds(r["dest"] + i, 1), b * 512:b * 512 + w].rearrange("p o n -> p (o n)")
                        src = ps[:, 0:w]
                    if kind == "silu":
                        ins = act.activation(dst, src, ACT.Silu)
                    elif kind == "scaled":
                        ins = act.activation(dst, src, ACT.Copy, scale=float(C_HD) ** -0.5)
                    elif kind == "eighth":
                        ins = act.activation(dst, src, ACT.Copy, scale=float(F_HD) ** -0.5)
                    else:
                        ins = act.activation(dst, src, ACT.Copy)
                ins.then_inc(s["tile_free"], 1)

            def split(r, i, parity, first):
                t = r["base"] + i
                w = r["width"]
                for sub in range(8):
                    beside(8 * t + sub)
                    if sub == 4:
                        if not first:
                            leave(r, i - 1, 1 - parity, t - 1)
                        elif pending:
                            leave(*pending.pop())
                    if sub % 2 == 0:
                        act.wait_ge(s[f"w_full{sub // 2}"], 16 * (t + 1))
                    if r["base"] > 0 or not first or sub >= 4:
                        act.wait_ge(s["ws_used"], 8 * t + (sub - 3))
                    raw = RAW[:, sub // 2, :].rearrange("p (k n) -> p k n", k=4)
                    k0 = 2 * (sub % 2)
                    sl = 2 * (sub % 4)
                    act.activation(WH[:, sl:sl + 2, 0:w], raw[:, k0:k0 + 2, 0:w], ACT.Copy)\
                        .then_inc(s["wh_done"], 1)
                if isinstance(i, int) and i == r["n"] - 1:
                    pending.append((r, i, parity, t))

            def phase(name):
                over_tiles(act, name, split)
                leave(*pending.pop())

            def rms(n, scratch):
                ss = SM[:, 16:18]
                for m in range(MT):
                    link(act.activation(scratch, XR[:, m, :], ACT.Square, accum_out=ss[:, m:m + 1]))
                link(act.activation(SM[:, 18:20], ss, ACT.Ln, bias=SM[:, 22:23], scale=1.0 / D))
                act.activation(SM[:, 20:22], SM[:, 18:20], ACT.Exp, scale=-0.5).then_inc(s["n_rstd"], 1)

            def norm_high(n):
                for g in range(8):
                    act.wait_ge(s["n_t"], 8 * n + g + 1)
                    for kk in range(2):
                        kt = 2 * g + kk
                        act.activation(HH[:, kt, :], bank[4 + g % 4][:, kk * T:(kk + 1) * T], ACT.Copy,
                                       scale=COLS[:, V_LN + 16 * n + kt:V_LN + 16 * n + kt + 1])\
                            .then_inc(s["n_h"], 1)

            def y_high(c, kt=None):
                act.wait_ge(s["y_ready"], c + 1)
                act.activation(HH[:, c % 16 if kt is None else kt, :], YB[:, c % 2, :], ACT.Copy).then_inc(s["y_h"], 1)

            def y_high_eight(c, kt, tiles):
                act.wait_ge(s["y_ready"], c + 8)
                act.activation(HH[:, kt:kt + 8, :], tiles.rearrange("p a (b t) -> p (a b) t", t=T), ACT.Copy)\
                    .then_inc(s["y_h"], 8)

            big_scratch = BIG[:, 4:6, :].rearrange("p a b -> p (a b)")

            qT = WORK[:, 0:2048].rearrange("p (k t) -> p k t", k=8)
            kT = WORK[:, 2048:2560].rearrange("p (k t) -> p k t", k=2)

            def a_copy(g):
                act.wait_ge(s["qk_t"], g + 1)
                dst = qT[:, 2 * g:2 * g + 2, :] if g < 4 else kT[:, :, :]
                act.activation(dst, bank[4 + g % 4][:, :].rearrange("p (k t) -> p k t", k=2), ACT.Copy)\
                    .then_inc(s["qk_c"], 1)

            def attend_step(p, i, S, probs, pt, sinks):
                if i < 16:
                    h = i
                    act.wait_ge(s[p + "soft"], h + 1)
                    if h >= 2:
                        act.wait_ge(s[p + "pt"], h - 1)
                    nm = SM[:, 32 + 2 * (h % 2):34 + 2 * (h % 2)]
                    den = SM[:, 36 + 2 * (h % 2):38 + 2 * (h % 2)]
                    act.activation(probs[:, h % 2, 0:P], S[:, h % 2, 0:P], ACT.Exp, bias=nm[:, 0:1],
                                   accum_out=den[:, 0:1])
                    if sinks is not None:
                        act.activation(SM[:, 40 + 2 * (h % 2):42 + 2 * (h % 2)], nm, ACT.Exp,
                                       bias=sinks[:, h:h + 1])
                    act.activation(probs[:, h % 2, P:384], S[:, h % 2, P:384], ACT.Exp, bias=nm[:, 1:2],
                                   accum_out=den[:, 1:2]).then_inc(s[p + "exp"], 1)
                if 2 <= i <= 17:
                    h = i - 2
                    act.wait_ge(s[p + "pt"], h + 1)
                    if h >= 2:
                        act.wait_ge(s[p + "pv"], h - 1)
                    act.activation(pt[:, h % 2, :], bank[6][:, 0:384], ACT.Copy).then_inc(s[p + "ptc"], 1)

            def stick_step(i):
                if 2 <= i <= C_HEADS + 1:
                    h = i - 2
                    act.wait_ge(s["c_min"], h + 1)
                    act.activation(C_W[:, h % 2, :], C_W[:, h % 2, :], ACT.Exp).then_inc(s["c_w"], 1)
                if i < C_HEADS:
                    h = i
                    act.wait_ge(s["c_z"], h + 1)
                    if h >= 2:
                        act.wait_ge(s["c_sp"], 2 * (h - 1))
                    t = C_T[:, h % 2, :]
                    link(act.activation(t, bank[4 + h % 2][:, 0:384], ACT.Abs))
                    link(act.activation(t, t, ACT.Exp, scale=-1.0))
                    act.activation(t, t, ACT.Ln, bias=SM[:, 23:24]).then_inc(s["c_exp"], 1)

            def softplus(v, tmp, sem_in, sem_out):
                act.wait_ge(sem_in, 1)
                link(act.activation(tmp, v, ACT.Abs))
                link(act.activation(tmp, tmp, ACT.Exp, scale=-1.0))
                act.activation(tmp, tmp, ACT.Ln, bias=SM[:, 23:24]).then_inc(sem_out, 1)

            XBC = BIG[:, 11:14, :].rearrange("p a b -> p (a b)")

            def beside(place):
                i = step_at(place, C_FIRST + C_ACT_LAG, 3, C_STEPS)
                if i is not None:
                    stick_step(i)
                if place == A_PREPARE + 4:
                    st = SM[:, 96:132]
                    act.wait_ge(s["aq_ready"], 1)
                    link(act.activation(st, st, ACT.Ln, bias=SM[:, 22:23], scale=1.0 / A_HD))
                    link(act.activation(st, st, ACT.Exp, scale=-0.5))
                    act.sem_inc(s["aq_ready"], 1)
                if place == A_TURN + ACT_LAG:
                    for g in range(4):
                        a_copy(g)
                if place == A_TURN + 1 + ACT_LAG:
                    a_copy(4)
                i = step_at(place, A_FIRST + ACT_LAG, 2, ATTEND_STEPS)
                if i is not None:
                    attend_step("a_", i, A_S, A_PROBS, A_PT, BC[:, A_SINK:A_SINK + 16])
                i = step_at(place, F_FIRST + ACT_LAG, 2, ATTEND_STEPS)
                if i is not None:
                    attend_step("f_", i, F_S, F_PROBS, F_PT, None)
                if place == F_GATE + 2:
                    softplus(SM[:, 96:128], F_TMP, s["f_v"], s["f_e"])
                if place == S_GATE + 2:
                    act.wait_ge(s["s_dt"], 1)
                    act.activation(S_AEX, BC[:, S_AL:S_AL + 16], ACT.Exp)
                    softplus(SM[:, 64:96], S_TMP, s["s_dt"], s["s_e"])
                g = step_at(place, S_CONV + 5, 4, 3)
                if g is not None:
                    act.wait_ge(s["s_conv"], 4 * (g + 1))
                    act.activation(XBC[:, g * 1024:(g + 1) * 1024], XBC[:, g * 1024:(g + 1) * 1024], ACT.Silu)\
                        .then_inc(s["s_xbc"], 1)

            act.wait_ge(s["vec_t"], 1)
            act.activation(COLS[:, 0:V_ROWS], bank[0][:, 0:V_ROWS], ACT.Copy)
            act.activation(COLS[:, V_CW:V_COLS], bank[0][:, V_ROWS:V_ROWS + 48], ACT.Copy).then_inc(s["cols_set"], 1)
            act.wait_ge(s["x_in"], 16)
            act.wait_ge(s["eps_set"], 1)
            act.wait_ge(s["cols_set"], 1)
            rms(0, big_scratch)
            norm_high(0)
            phase("even_in")

            y_high_eight(0, 0, BIG[:, 3:5, :])

            T1 = BIG[:, 0:2, :].rearrange("p a b -> p (a b)")
            T2 = BIG[:, 3:5, :].rearrange("p a b -> p (a b)")
            bfv = bf.rearrange("p a b -> p (a b)")
            lbz = SM[:, 44:52]
            act.wait_ge(s["b_vec"], 1)
            link(act.activation(SM[:, 52:60], lbz, ACT.Exp))
            act.sem_inc(s["b_vec"], 1)
            act.wait_ge(s["b_vec"], 3)
            link(act.activation(SM[:, 68:76], SM[:, 68:76], ACT.Ln, scale=2.0 ** 64))
            link(act.activation(SM[:, 76:84], SM[:, 60:68], ACT.Ln, scale=-1.0, bias=SM[:, 23:24]))
            act.sem_inc(s["b_vec"], 1)
            link(act.activation(T1, bfv, ACT.Abs))
            link(act.activation(T1, T1, ACT.Exp, scale=-1.0))
            act.activation(T1, T1, ACT.Ln, bias=SM[:, 23:24]).then_inc(s["b_e"], 1)
            act.wait_ge(s["b_lsg"], 2)
            act.wait_ge(s["b_vec"], 6)
            for h in range(B_HEADS):
                act.activation(bfv[:, h * T:(h + 1) * T], T2[:, h * T:(h + 1) * T], ACT.Exp,
                               bias=SM[:, 76 + h:77 + h]).then_inc(s["b_kin"], 1)
            act.wait_ge(s["b_ml"], B_HEADS)
            for h in range(B_HEADS):
                link(act.activation(T1[:, h * T:(h + 1) * T], T1[:, h * T:(h + 1) * T], ACT.Abs,
                                    bias=SM[:, 84 + h:85 + h]))
            link(act.activation(T1, T1, ACT.Exp, scale=-1.0))
            act.activation(T1, T1, ACT.Ln, bias=SM[:, 23:24]).then_inc(s["b_x"], 1)

            def decays(u):
                act.wait_ge(s["b_lt"], u + 1)
                if u >= 2:
                    act.wait_ge(s["b_es"], u - 1)
                act.activation(LFT[:, u % 2, :], bank[4][:, (u % 2) * P:(u % 2 + 1) * P], ACT.Copy)\
                    .then_inc(s["b_lf"], 1)
                act.wait_ge(s["b_es"], u + 1)
                if u >= 1:
                    act.wait_ge(s["b_qe"], u)
                    act.wait_ge(s["b_ke"], u)
                    act.wait_ge(s["b_kx"], (u + 1) // 2)
                for b in range(2):
                    ins = act.activation(WORK[:, 512 * b:512 * (b + 1)], bank[b][:, :], ACT.Exp)
                ins.then_inc(s["b_ex"], 1)

            def head_square(h):
                act.wait_ge(s["b_ov"], h + 1)
                if h >= 1:
                    act.wait_ge(s["b_ss"], h)
                act.activation(BSQ, bank[5 + 2 * (h % 2)][:, 0:T], ACT.Square).then_inc(s["b_sq"], 1)

            def head_rms(h):
                act.wait_ge(s["b_ss"], h + 1)
                if h >= 1:
                    act.wait_ge(s["y_ready"], 8 + h)
                link(act.activation(BRS, bank[5 + 2 * (h % 2)][:, T:2 * T], ACT.Ln, bias=SM[:, 22:23], scale=1.0 / B_HD))
                act.activation(BRS, BRS, ACT.Exp, scale=-0.5).then_inc(s["b_rs"], 1)

            for i in range(2 * B_HEADS + 5):
                if i < 2 * B_HEADS:
                    decays(i)
                if i >= 2 and i % 2 == 0 and i - 2 < 2 * B_HEADS:
                    h = (i - 2) // 2
                    act.wait_ge(s["b_cross"], h + 1)
                    if h >= 1:
                        act.wait_ge(s["b_ov"], h)
                    act.activation(CX, bank[6][:, 0:P], ACT.Copy).then_inc(s["b_cx"], 1)
                if i >= 6 and i % 2 == 0:
                    y_high(8 + (i - 6) // 2)
                if i >= 4 and i % 2 == 0 and i < 2 * B_HEADS + 4:
                    head_square((i - 4) // 2)
                if i >= 5 and i % 2 == 1:
                    head_rms((i - 5) // 2)
            phase("even_out")

            act.wait_ge(s["tile_free"], last_tile("even_out") + 1)
            rms(1, big_scratch)
            norm_high(1)
            phase("odd_in")
            for g in range(4):
                act.wait_ge(s["y_ready"], 16 + 4 * (g + 1))
                act.activation(HH[:, 4 * g:4 * g + 4, :], BIG[:, g, :].rearrange("p (b t) -> p b t", t=T), ACT.Copy)\
                    .then_inc(s["y_h"], 4)
            phase("odd_out")

            act.wait_ge(s["tile_free"], last_tile("odd_out") + 1)
            rms(2, big_scratch)
            norm_high(2)
            phase("two_in")
            y_high_eight(32, 8, BIG[:, 5:7, :])
            sE = WORK[:, 768:1536].rearrange("p (b c) -> p b c", b=2)
            for h in range(S_HEADS):
                act.wait_ge(s["s_seg"], h + 1)
                if h >= 2:
                    act.wait_ge(s["s_l"], h - 1)
                act.activation(sE[:, h % 2, :], bank[4 + h % 2][:, 0:384], ACT.Exp).then_inc(s["s_ex"], 1)
            ZS = BIG[:, 0:2, :].rearrange("p a b -> p (a b)")
            SQ = WORK[:, 768:1792]
            for g in range(2):
                act.wait_ge(s["s_yg"], 4 * (g + 1))
                act.wait_ge(s["s_l"], S_HEADS)
                if g == 1:
                    act.wait_ge(s["s_ss"], 1)
                act.activation(SQ, ZS[:, g * 1024:(g + 1) * 1024], ACT.Square).then_inc(s["s_sq"], 1)
                act.wait_ge(s["s_ss"], g + 1)
                if g == 1:
                    act.wait_ge(s["y_ready"], 44)
                link(act.activation(WORK[:, 3456:3712], bank[6][:, 0:T], ACT.Ln, bias=SM[:, 22:23],
                                    scale=1.0 / 512))
                act.activation(WORK[:, 3456:3712], WORK[:, 3456:3712], ACT.Exp, scale=-0.5)\
                    .then_inc(s["s_rs"], 1)
                for j in range(4):
                    y_high(40 + 4 * g + j, 4 * g + j)
            phase("two_out")

            act.wait_ge(s["tile_free"], last_tile("two_out") + 1)
            rms(3, big_scratch)
            norm_high(3)
            phase("peer_q")
            kTp = BIG[:, 4:6, :].rearrange("p a b -> p (a b)")
            for g in range(4):
                act.wait_ge(s["k_t"], g + 1)
                act.activation(kTp[:, g * 512:(g + 1) * 512], bank[4 + g][:, :], ACT.Copy).then_inc(s["k_c"], 1)
            SC = BIG[:, 8:12, :].rearrange("p a b -> p (a b)")
            for g in range(8):
                act.wait_ge(s["q_s"], g + 1)
                act.activation(SC[:, g * 512:(g + 1) * 512], bank[g % 4][:, :], ACT.Copy).then_inc(s["q_sc"], 1)

            def rows_high(n, j, g0=0):
                for g in range(4):
                    act.wait_ge(s["t_t"], 4 * n + g + 1)
                    if not (isinstance(n, int) and (n < 2 or (n >= 2 * QR and n % QR < 2))):
                        act.wait_ge(s["u_used"], 4 * n + (g - 7))
                    act.activation(WH[:, 4 * (j % 2) + g, :], bank[4 + g][:, :], ACT.Copy).then_inc(s["t_h"], 1)

            def gelu(n, j, k):
                act.wait_ge(s["u_used"], 4 * n + 4)
                act.activation(GB[k % 2][:, bass.ds(n - QR * k, 1), :].rearrange("p o t -> p (o t)"),
                               bank[j % 2][:, 0:T], ACT.Gelu).then_inc(s["a_gelu"], 1)

            def v_high(n, j, full):
                act.wait_ge(s[f"row_full{j}"], full)
                act.activation(WH[:, 4 * (j % 2):4 * (j % 2) + 4, :],
                               RAW[:, j, :].rearrange("p (g n) -> p g n", g=4), ACT.Copy).then_inc(s["v_h"], 1)

            def p_high(n, j, k):
                if not (isinstance(n, int) and n < 2):
                    act.wait_ge(s["o_mm"], n - 1)
                act.activation(PS[:, j % 2, 0, :], GB[k % 2][:, bass.ds(n - QR * k, 1), :].rearrange("p o t -> p (o t)"),
                               ACT.Copy).then_inc(s["p_h"], 1)

            for seg, (kind, k) in enumerate(SEGMENTS):
                n0 = QR * k
                full = (QR // 4) * seg
                after = SEGMENTS[seg + 1] if seg + 1 < len(SEGMENTS) else None
                if kind == "in":
                    for j in range(4):
                        if seg > 0 and SEGMENTS[seg - 1][0] == "out" and j < 2:
                            act.wait_ge(s["o_mm"], QR * (SEGMENTS[seg - 1][1] + 1) - 1 + j)
                        rows_high(n0 + j, j)
                        if j == 1 and k == 1:
                            act.wait_ge(s["tk_idx"], 2)
                        if j >= 1:
                            gelu(n0 + j - 1, j - 1, k)
                    with act.Fori(1, QR // 4) as q:
                        for j in range(4):
                            rows_high(4 * q + (n0 + j), j)
                            gelu(4 * q + (n0 + j - 1), (j + 3) % 4, k)
                    if after[0] == "out":
                        act.wait_ge(s["u_used"], 4 * (n0 + QR - 1))
                        v_high(QR * after[1], 0, 16 * (QR // 4 * (seg + 1) + 1))
                    gelu(n0 + QR - 1, 3, k)
                    if k == 0:
                        for m in range(MT):
                            g = WORK[:, 1024 + 128 * m:1152 + 128 * m]
                            act.wait_ge(s["tk_e"], m + 1)
                            act.activation(g, g, ACT.Exp).then_inc(s["tk_g"], 1)
                        for n in range(6):
                            act.wait_ge(s["tk_t"], n + 1)
                            act.activation(TKT[:, n % 3, (n // 3) * P:(n // 3 + 1) * P], bank[2 + n % 2][:, 0:P],
                                           ACT.Copy).then_inc(s["tk_tc"], 1)
                else:
                    if seg > 0 and SEGMENTS[seg - 1][0] == "out":
                        act.wait_ge(s["o_mm"], n0 - 1)
                        v_high(n0, 0, 16 * (full + 1))
                    act.wait_ge(s["g_mul"], n0 + QR)

                    def out_high(n, j, k, full, more=True):
                        p_high(n, j, k)
                        if more:
                            if j == 0 and isinstance(n, int) and n == QR * k:
                                act.wait_ge(s["u_used"], 4 * u_tiles)
                                if n > 0:
                                    act.wait_ge(s["o_mm"], n)
                            else:
                                act.wait_ge(s["o_mm"], n)
                            v_high(n + 1, (j + 1) % 4, full)

                    u_tiles = QR * (1 + max(kk for kd, kk in SEGMENTS[:seg] if kd == "in"))
                    for j in range(4):
                        out_high(n0 + j, j, k, 16 * (full + 1 + (j == 3)))
                    with act.Fori(1, QR // 4 - 1) as q:
                        for j in range(4):
                            out_high(4 * q + (n0 + j), j, k, 16 * q + 16 * (full + 1 + (j == 3)))
                    for j in range(4):
                        out_high(n0 + QR - 4 + j, j, k, 16 * (full + QR // 4), j < 3)

            act.wait_ge(s["o_add"], 8 * QUARTERS)
            rms(4, big_scratch)

        @block.vector
        def _(dve):
            ch = Chain(dve, s["dve_chain"])
            link = ch.link
            pending = []

            def leave(r, i, parity, t):
                if r["kind"] != "res":
                    return
                dve.wait_ge(s["ws_used"], 8 * (t + 1))
                for m in range(MT):
                    x = XR[:, m, bass.ds(r["c0"] + i * NW, NW)]
                    ins = dve.tensor_tensor(x, x, bank[2 * parity + m][:, :], ALU.add)
                ins.then_inc(s["tile_free"], 1)

            def split(r, i, parity, first):
                t = r["base"] + i
                w = r["width"]
                for sub in range(8):
                    beside(8 * t + sub)
                    if sub == 4:
                        if not first:
                            leave(r, i - 1, 1 - parity, t - 1)
                        elif pending:
                            leave(*pending.pop())
                    dve.wait_ge(s["wh_done"], 8 * t + sub + 1)
                    raw = RAW[:, sub // 2, :].rearrange("p (k n) -> p k n", k=4)
                    k0 = 2 * (sub % 2)
                    sl = 2 * (sub % 4)
                    dve.tensor_tensor(WL[:, sl:sl + 2, 0:w], raw[:, k0:k0 + 2, 0:w],
                                      WH[:, sl:sl + 2, 0:w].bitcast(F32), ALU.subtract).then_inc(s["wl_done"], 1)
                if isinstance(i, int) and i == r["n"] - 1:
                    pending.append((r, i, parity, t))

            def phase(name):
                over_tiles(dve, name, split)
                leave(*pending.pop())

            xn = BIG[:, 0:4, :].rearrange("p (m a) b -> p m (a b)", m=2)

            def norm_low(n):
                dve.wait_ge(s["n_rstd"], n + 1)
                for m in range(MT):
                    dve.tensor_scalar(xn[:, m, :], XR[:, m, :], SM[:, 20 + m:21 + m], None, ALU.mult)\
                        .then_inc(s["n_x"], 1)
                for g in range(8):
                    dve.wait_ge(s["n_h"], 16 * n + 2 * g + 2)
                    for kk in range(2):
                        kt = 2 * g + kk
                        dve.scalar_tensor_tensor(
                            HL[:, kt, :], bank[4 + g % 4][:, kk * T:(kk + 1) * T],
                            COLS[:, V_LN + 16 * n + kt:V_LN + 16 * n + kt + 1],
                            HH[:, kt, :].bitcast(F32), ALU.mult, ALU.subtract).then_inc(s["n_l"], 1)

            def y_wait(c):
                if c >= 2:
                    dve.wait_ge(s["y_l"], c - 1)

            def y_low(c, kt=None):
                kt = c % 16 if kt is None else kt
                dve.wait_ge(s["y_h"], c + 1)
                dve.tensor_tensor(HL[:, kt, :], YB[:, c % 2, :], HH[:, kt, :].bitcast(F32),
                                  ALU.subtract).then_inc(s["y_l"], 1)

            def y_low_eight(c, kt, tiles):
                dve.wait_ge(s["y_h"], c + 8)
                dve.tensor_tensor(HL[:, kt:kt + 8, :], tiles.rearrange("p a (b t) -> p (a b) t", t=T),
                                  HH[:, kt:kt + 8, :].bitcast(F32), ALU.subtract).then_inc(s["y_l"], 8)
                dve.wait_ge(s["y_l"], c + 8)

            q_t = BIG[:, 0:2, :].rearrange("p a b -> p (a b)")
            q3 = q_t.rearrange("p (h d) -> p h d", d=64)
            kv = BIG[:, 2, :].rearrange("p (m n) -> p m n", m=2)
            kcol = kv[:, :, 0:P]
            w1, w2 = WORK[:, 0:2048], WORK[:, 2048:4096]
            k2 = w2[:, 0:256].rearrange("p (m n) -> p m n", m=2)
            kc = w2[:, 1024:1280].rearrange("p (h d) -> p h d", d=64)
            kd = w2[:, 1536:2048].rearrange("p (m g c d) -> p m g c d", m=2, g=2, c=2)

            def a_prepare(step):
                st = SM[:, 96:132]
                if step == 0:
                    dve.wait_ge(s["const_in"], 16 * N_CONST)
                    dve.wait_ge(s["tile_free"], 3)
                    link(dve.tensor_tensor(w1, q_t, q_t, ALU.mult))
                    link(dve.tensor_reduce(st[:, 0:32], w1.rearrange("p (h d) -> p h d", d=64), AX.X, ALU.add))
                elif step == 1:
                    link(dve.tensor_tensor(k2, kcol, kcol, ALU.mult))
                    link(dve.tensor_reduce(st[:, 32:36], w2[:, 0:256].rearrange("p (h d) -> p h d", d=64), AX.X,
                                           ALU.add))
                    dve.sem_inc(s["aq_ready"], 1)
                elif step == 2:
                    dve.wait_ge(s["aq_ready"], 2)
                    link(dve.tensor_tensor(q3, q3, st[:, 0:32].unsqueeze(2).broadcast_to([P, 32, 64]), ALU.mult))
                elif step == 3:
                    link(dve.tensor_tensor(q3, q3, BC[:, A_QN:A_QN + 64].unsqueeze(1).broadcast_to([P, 32, 64]),
                                           ALU.mult))
                elif step == 4:
                    link(dve.tensor_tensor(
                        kc.rearrange("p (m g) d -> p m g d", m=2), kcol.rearrange("p m (g d) -> p m g d", g=2),
                        st[:, 32:36].rearrange("p (m g) -> p m g", m=2).unsqueeze(3).broadcast_to([P, 2, 2, 64]),
                        ALU.mult))
                    link(dve.tensor_tensor(kc, kc, BC[:, A_KN:A_KN + 64].unsqueeze(1).broadcast_to([P, 4, 64]),
                                           ALU.mult))
                elif step < 13:
                    tt, m, part = (step - 5) // 4, (step - 5) // 2 % 2, (step - 5) % 2
                    o = tt * 1024 + m * 512
                    if part == 0:
                        x = q_t[:, o:o + 512].rearrange("p (h d) -> p h d", h=16)
                        y1 = w1[:, 0:512].rearrange("p (h d) -> p h d", h=16)
                        y2 = w1[:, 512:1024].rearrange("p (h d) -> p h d", h=16)
                        link(dve.tensor_tensor(y1, x, ROPE[:, 0, m, :].unsqueeze(1).broadcast_to([P, 16, 32]), ALU.mult))
                        link(dve.tensor_tensor(y2, x, ROPE[:, 1, m, :].unsqueeze(1).broadcast_to([P, 16, 32]), ALU.mult))
                    else:
                        xh = q_t[:, o:o + 512].rearrange("p (h f d) -> p h f d", h=8, f=2)
                        y1h = w1[:, 0:512].rearrange("p (h f d) -> p h f d", h=8, f=2)
                        y2h = w1[:, 512:1024].rearrange("p (h f d) -> p h f d", h=8, f=2)
                        link(dve.tensor_tensor(xh[:, :, 0, :], y1h[:, :, 0, :], y2h[:, :, 1, :], ALU.subtract))
                        link(dve.tensor_tensor(xh[:, :, 1, :], y1h[:, :, 1, :], y2h[:, :, 0, :], ALU.add))
                else:
                    m = step - 13
                    x = kc[:, 2 * m:2 * m + 2, :].rearrange("p h (f d) -> p (h f) d", f=2)
                    y1 = w1[:, 0:128].rearrange("p (h d) -> p h d", h=4)
                    y2 = w1[:, 128:256].rearrange("p (h d) -> p h d", h=4)
                    link(dve.tensor_tensor(y1, x, ROPE[:, 0, m, :].unsqueeze(1).broadcast_to([P, 4, 32]), ALU.mult))
                    link(dve.tensor_tensor(y2, x, ROPE[:, 1, m, :].unsqueeze(1).broadcast_to([P, 4, 32]), ALU.mult))
                    y1h = w1[:, 0:128].rearrange("p (h f d) -> p h f d", h=2, f=2)
                    y2h = w1[:, 128:256].rearrange("p (h f d) -> p h f d", h=2, f=2)
                    for c2 in range(2):
                        link(dve.tensor_tensor(kd[:, m, :, c2, 0:32], y1h[:, :, 0, :], y2h[:, :, 1, :], ALU.subtract))
                        link(dve.tensor_tensor(kd[:, m, :, c2, 32:64], y1h[:, :, 1, :], y2h[:, :, 0, :], ALU.add))
                    if m == 1:
                        dve.sem_inc(s["aq_ready"], 1)

            def attend_step(p, i, S, mask, scale, sinks, leave_pair):
                if i < 16:
                    h = i
                    dve.wait_ge(s[p + "score"], h + 1)
                    if h >= 2:
                        dve.wait_ge(s[p + "exp"], h - 1)
                    z = S[:, h % 2, :]
                    link(dve.scalar_tensor_tensor(z, bank[4 + h % 2][:, 0:384], scale, mask, ALU.mult, ALU.add))
                    mx = SM[:, 28 + 2 * (h % 2):30 + 2 * (h % 2)]
                    nm = SM[:, 32 + 2 * (h % 2):34 + 2 * (h % 2)]
                    link(dve.tensor_reduce(mx[:, 0:1], z[:, 0:P], AX.X, ALU.max))
                    link(dve.tensor_reduce(mx[:, 1:2], z[:, P:384], AX.X, ALU.max))
                    if sinks is not None:
                        dve.tensor_scalar(nm, mx, sinks[:, h:h + 1], -1.0, ALU.max, ALU.mult)\
                            .then_inc(s[p + "soft"], 1)
                    else:
                        dve.tensor_scalar(nm, mx, -1.0, None, ALU.mult).then_inc(s[p + "soft"], 1)
                if 1 <= i <= 16:
                    h = i - 1
                    den = SM[:, 36 + 2 * (h % 2):38 + 2 * (h % 2)]
                    rc = SM[:, 24 + 2 * (h % 2):26 + 2 * (h % 2)]
                    dve.wait_ge(s[p + "exp"], h + 1)
                    if h >= 2:
                        dve.wait_ge(s[p + "pn"], h - 1)
                    if sinks is not None:
                        link(dve.tensor_tensor(den, den, SM[:, 40 + 2 * (h % 2):42 + 2 * (h % 2)], ALU.add))
                    dve.reciprocal(rc, den).then_inc(s[p + "rcp"], 1)
                if i >= 4 and i % 2 == 0:
                    j = (i - 4) // 2
                    dve.wait_ge(s[p + "pv"], 2 * j + 2)
                    leave_pair(j, bank[7][:, 0:T]).then_inc(s["y_ready"], 1)

            def a_leave(j, o):
                return dve.tensor_tensor(chan(3, j), o, chan(3, j), ALU.mult)

            def f_leave(j, o):
                return dve.tensor_copy(chan(5, j), o)

            def stick_step(i):
                if i < C_HEADS:
                    h = i
                    if h == 0:
                        dve.wait_ge(s["c_mask"], 1)
                    dve.wait_ge(s["c_exp"], h + 1)
                    if h >= 2:
                        dve.wait_ge(s["c_e"], h - 1)
                    sp_ = C_SP[:, h % 2, :]
                    dve.scalar_tensor_tensor(sp_, bank[4 + h % 2][:, 0:384], 0.0, C_T[:, h % 2, :], ALU.max,
                                             ALU.add).then_inc(s["c_sp"], 1)
                    dve.wait_ge(s["c_sp"], 2 * h + 1)
                    dve.tensor_tensor(sp_, sp_, CM, ALU.mult).then_inc(s["c_sp"], 1)
                if 1 <= i <= C_HEADS:
                    h = i - 1
                    dve.wait_ge(s["c_e"], h + 1)
                    if h >= 2:
                        dve.wait_ge(s["c_pv"], h - 1)
                    dve.tensor_tensor(C_W[:, h % 2, :], bank[4 + h % 2][:, 0:384], CN, ALU.min).then_inc(s["c_min"], 1)
                if i >= 3:
                    h = i - 3
                    dve.wait_ge(s["c_pv"], h + 1)
                    dve.tensor_copy(chan(0, h), bank[6 + h % 2][:, 0:T]).then_inc(s["c_out"], 1)

            two = "p (m h) -> p m h"
            s_dt, f_lf = SM[:, 64:96], SM[:, 96:128]

            def per_head(at):
                return BC[:, at:at + 16].unsqueeze(1).broadcast_to([P, 2, 16])

            XB = BIG[:, 2:5, :].rearrange("p a b -> p (a b)")
            XBC = BIG[:, 11:14, :].rearrange("p a b -> p (a b)")

            def convolve(k):
                x, y = XB[:, k * T:(k + 1) * T], XBC[:, k * T:(k + 1) * T]

                def tap(j):
                    return COLS[:, V_CW + 12 * j + k:V_CW + 12 * j + k + 1]

                link(dve.tensor_scalar(y, x, tap(3), COLS[:, V_CB + k:V_CB + k + 1], ALU.mult, ALU.add))
                for back in (1, 2, 3):
                    ins = dve.scalar_tensor_tensor(y[:, back:T], x[:, 0:T - back], tap(3 - back), y[:, back:T],
                                                   ALU.mult, ALU.add)
                    if back < 3:
                        link(ins)
                    else:
                        ins.then_inc(s["s_conv"], 1)

            def beside(place):
                i = step_at(place, C_FIRST + C_DVE_LAG, 3, C_STEPS)
                if i is not None:
                    stick_step(i)
                step = step_at(place, A_PREPARE, 2, A_PREPARE_STEPS)
                if step is not None:
                    a_prepare(step)
                i = step_at(place, A_FIRST + DVE_LAG, 2, ATTEND_STEPS)
                if i is not None:
                    attend_step("a_", i, A_S, AMASK[:, :], float(A_HD) ** -0.5, BC[:, A_SINK:A_SINK + 16], a_leave)
                i = step_at(place, F_FIRST + DVE_LAG, 2, ATTEND_STEPS)
                if i is not None:
                    attend_step("f_", i, F_S, FMASK[:, :], 1.0, None, f_leave)
                if place == F_GATE:
                    dve.wait_ge(s["tile_free"], TWO_TILE + 1)
                    link(dve.tensor_tensor(f_lf.rearrange(two, m=2), DTF[:, 1, :, :], per_head(F_FB), ALU.add))
                    dve.tensor_scalar(f_lf, f_lf, -1.0, None, ALU.mult).then_inc(s["f_v"], 1)
                if place == F_GATE + 4:
                    dve.wait_ge(s["f_e"], 1)
                    link(dve.scalar_tensor_tensor(f_lf, f_lf, 0.0, F_TMP, ALU.max, ALU.add))
                    dve.tensor_scalar(f_lf, f_lf, -1.0, None, ALU.mult).then_inc(s["f_lf"], 1)
                if place == S_GATE:
                    dve.wait_ge(s["tile_free"], TWO_TILE + 8)
                    dve.tensor_tensor(s_dt.rearrange(two, m=2), DTF[:, 0, :, :], per_head(S_DTB), ALU.add)\
                        .then_inc(s["s_dt"], 1)
                if place == S_GATE + 4:
                    dve.wait_ge(s["s_e"], 1)
                    link(dve.scalar_tensor_tensor(S_DT, s_dt, 0.0, S_TMP, ALU.max, ALU.add))
                    link(dve.tensor_scalar(S_AEX, S_AEX, -1.0, None, ALU.mult))
                    dve.tensor_tensor(s_dt.rearrange(two, m=2), S_DT.rearrange(two, m=2),
                                      S_AEX.unsqueeze(1).broadcast_to([P, 2, 16]), ALU.mult).then_inc(s["s_a"], 1)
                k = step_at(place, S_CONV, 1, 12)
                if k is not None:
                    dve.wait_ge(s["tile_free"], TWO_TILE + 9 + k // 4)
                    convolve(k)

            link(dve.memset(SM[:, 22:23], EPS))
            dve.memset(SM[:, 23:24], 1.0).then_inc(s["eps_set"], 1)
            norm_low(0)
            phase("even_in")

            y_low_eight(0, 0, BIG[:, 3:5, :])

            T1 = BIG[:, 0:2, :].rearrange("p a b -> p (a b)")
            T2 = BIG[:, 3:5, :].rearrange("p a b -> p (a b)")
            bfv = bf.rearrange("p a b -> p (a b)")
            link(dve.tensor_tensor(SM[:, 44:52], COLS[:, V_LB:V_LB + 8], COLS[:, V_LB:V_LB + 8], ALU.subtract))
            dve.sem_inc(s["b_vec"], 1)
            dve.wait_ge(s["b_vec"], 2)
            link(dve.reciprocal(SM[:, 60:68], SM[:, 52:60]))
            link(dve.tensor_tensor(SM[:, 52:60], SM[:, 52:60], SM[:, 60:68], ALU.mult))
            link(dve.tensor_tensor(SM[:, 60:68], SM[:, 52:60], SM[:, 52:60], ALU.subtract))
            link(dve.tensor_scalar(SM[:, 68:76], SM[:, 60:68], 1e-30, None, ALU.max))
            link(dve.tensor_tensor(SM[:, 92:100], SM[:, 60:68], SM[:, 68:76], ALU.subtract))
            dve.sem_inc(s["b_vec"], 1)
            dve.wait_ge(s["b_vec"], 4)
            link(dve.tensor_scalar(SM[:, 68:76], SM[:, 68:76], -64.0 * LN2, None, ALU.add))
            link(dve.tensor_tensor(SM[:, 84:92], SM[:, 76:84], SM[:, 68:76], ALU.subtract))
            dve.sem_inc(s["b_vec"], 2)
            dve.wait_ge(s["b_e"], 1)
            link(dve.scalar_tensor_tensor(T1, bfv, 0.0, T1, ALU.min, ALU.subtract))
            dve.sem_inc(s["b_lsg"], 1)
            dve.tensor_tensor(T2, T1, bfv, ALU.subtract).then_inc(s["b_lsg"], 1)
            for h in range(B_HEADS):
                dve.wait_ge(s["b_kin"], h + 1)
                c = slice(h * T, (h + 1) * T)
                link(dve.tensor_scalar(bfv[:, c], bfv[:, c], SM[:, 92 + h:93 + h], None, ALU.add))
                dve.tensor_scalar(T2[:, c], T1[:, c], SM[:, 76 + h:77 + h], SM[:, 68 + h:69 + h], ALU.add, ALU.max)\
                    .then_inc(s["b_ml"], 1)
            dve.wait_ge(s["b_x"], 1)
            link(dve.tensor_tensor(T1, T1, T2, ALU.add))
            dve.sem_inc(s["b_x"], 1)
            qe = WORK[:, 1024:2048].rearrange("p (l i) -> p l i", l=8)
            am = WORK[:, 3072:4096]
            ex = WORK[:, 0:1024].rearrange("p (l i) -> p l i", l=8)
            for i in range(1, 2 * B_HEADS + 4):
                if 0 <= i - 2 < 2 * B_HEADS:
                    u = i - 2
                    dve.wait_ge(s["b_att"], u + 1)
                    if u >= 1:
                        dve.wait_ge(s["b_lev"], u)
                    for b in range(2):
                        ins = dve.tensor_tensor(am[:, 512 * b:512 * (b + 1)], bank[2 + b][:, :],
                                                MK[:, 4 * b:4 * b + 4, :].rearrange("p l i -> p (l i)"), ALU.mult)
                    ins.then_inc(s["b_am"], 1)
                if i - 1 < 2 * B_HEADS:
                    u = i - 1
                    h, m = u // 2, u % 2
                    dve.wait_ge(s["b_ex"], u + 1)
                    if m == 0 and h >= 1:
                        dve.wait_ge(s["b_cross"], h)
                    qq = chan(5, h)[:, m * P:(m + 1) * P].unsqueeze(1).broadcast_to([P, 8, P])
                    dve.tensor_tensor(qe, ex, qq, ALU.mult).then_inc(s["b_qe"], 1)
                if i >= 5 and i % 2 == 1:
                    h = (i - 5) // 2
                    c = 8 + h
                    if h >= 1:
                        y_low(c - 1)
                    dve.wait_ge(s["b_rs"], h + 1)
                    y_wait(c)
                    y = YB[:, c % 2, :]
                    link(dve.scalar_tensor_tensor(y, bank[5 + 2 * (h % 2)][:, 0:T], COLS[:, V_GN:V_GN + 1], BRS,
                                                  ALU.mult, ALU.mult))
                    dve.tensor_tensor(y, y, chan(11, h), ALU.mult).then_inc(s["y_ready"], 1)
            y_low(15)
            phase("even_out")

            norm_low(1)
            phase("odd_in")
            dve.wait_ge(s["tile_free"], ODD_TILE + 16)
            dve.wait_ge(s["c_out"], C_HEADS)

            def c_low(g):
                dve.wait_ge(s["y_h"], 16 + 4 * (g + 1))
                dve.tensor_tensor(HL[:, 4 * g:4 * g + 4, :], BIG[:, g, :].rearrange("p (b t) -> p b t", t=T),
                                  HH[:, 4 * g:4 * g + 4, :].bitcast(F32), ALU.subtract).then_inc(s["y_l"], 4)

            for g in range(4):
                dve.tensor_tensor(BIG[:, g, :], BIG[:, g, :], BIG[:, 12 + g, :], ALU.mult).then_inc(s["y_ready"], 4)
                if g >= 1:
                    c_low(g - 1)
            c_low(3)
            phase("odd_out")

            norm_low(2)
            phase("two_in")
            dve.wait_ge(s["tile_free"], last_tile("two_in") + 1)
            y_low_eight(32, 8, BIG[:, 5:7, :])
            DT = S_DT
            XD = BIG[:, 14:16, :].rearrange("p a b -> p (a b)").rearrange("p (m h d) -> p m h d", m=2, h=16)
            for g in range(4):
                m, hh = g // 2, g % 2
                dve.wait_ge(s["s_xt"], g + 1)
                dve.tensor_tensor(XD[:, m, 8 * hh:8 * hh + 8, :],
                                  bank[g % 2][:, :].rearrange("p (h d) -> p h d", h=8),
                                  DT[:, 16 * m + 8 * hh:16 * m + 8 * hh + 8].unsqueeze(2).broadcast_to([P, 8, 64]),
                                  ALU.mult).then_inc(s["s_xd"], 1)
            CB = WORK[:, 2688:3456].rearrange("p (g c) -> p g c", g=2)
            for g in range(2):
                dve.wait_ge(s["s_cb"], g + 1)
                dve.tensor_tensor(CB[:, g, 0:P], bank[2 + g][:, 0:P], LE[:, :], ALU.mult)
                dve.tensor_copy(CB[:, g, P:256], bank[2 + g][:, P:256])
                dve.tensor_tensor(CB[:, g, 256:384], bank[2 + g][:, 256:384], LE[:, :], ALU.mult)\
                    .then_inc(s["s_cbm"], 1)
            dve.wait_ge(s["s_cbm"], 2)
            sE = WORK[:, 768:1536].rearrange("p (b c) -> p b c", b=2)
            sL = WORK[:, 1792:2560].rearrange("p (b c) -> p b c", b=2)
            ZS = BIG[:, 0:2, :].rearrange("p a b -> p (a b)")
            dve.wait_ge(s["masks"], 2)
            for i in range(S_HEADS + 2):
                if i < S_HEADS:
                    h = i
                    dve.wait_ge(s["s_ex"], h + 1)
                    if h >= 2:
                        dve.wait_ge(s["s_y"], h - 1)
                    dve.tensor_tensor(sL[:, h % 2, :], sE[:, h % 2, :], CB[:, h // 8, :], ALU.mult)\
                        .then_inc(s["s_l"], 1)
                if i >= 2 and i % 2 == 1:
                    j = (i - 2) // 2
                    dve.wait_ge(s["s_y"], 2 * j + 2)
                    xs = XBC[:, j * T:(j + 1) * T]
                    link(dve.scalar_tensor_tensor(xs, xs, DSK[:, j:j + 1], bank[j % 2][:, 0:T], ALU.mult, ALU.add))
                    z = ZS[:, j * T:(j + 1) * T]
                    dve.tensor_tensor(z, z, xs, ALU.mult).then_inc(s["s_yg"], 1)
            for g in range(2):
                dve.wait_ge(s["s_rs"], g + 1)
                for j in range(4 * g, 4 * g + 4):
                    c = 40 + j
                    y_wait(c)
                    dve.scalar_tensor_tensor(YB[:, c % 2, :], ZS[:, j * T:(j + 1) * T],
                                             COLS[:, V_SSDN + j:V_SSDN + j + 1], WORK[:, 3456:3712],
                                             ALU.mult, ALU.mult).then_inc(s["y_ready"], 1)
                    y_low(c, j)
            phase("two_out")

            norm_low(3)
            phase("peer_q")
            dve.wait_ge(s["q_sc"], 8)
            SC = BIG[:, 8:12, :].rearrange("p (m a) b -> p m (a b)", m=2)
            v16 = WORK[:, 0:256].rearrange("p (f k) -> p f k", k=16)
            v4 = WORK[:, 0:256].rearrange("p (h f k) -> p h f k", f=2, k=16)
            i16 = WORK[:, 256:512].bitcast(U32).rearrange("p (f k) -> p f k", k=16)
            if16 = WORK[:, 512:768].rearrange("p (h f k) -> p h f k", f=2, k=16)
            s16 = WORK[:, 768:896].rearrange("p (h k) -> p h k", k=16)
            p16 = WORK[:, 896:1024].bitcast(U32)
            gate = WORK[:, 1024:1280].rearrange("p (m n) -> p m n", m=2)
            pa_u = WORK[:, 1280:1408].bitcast(U32)
            pb_u = WORK[:, 1408:1536].bitcast(U32)
            pa_f, pb_f = WORK[:, 1536:1664], WORK[:, 1664:1792]
            gsum = SM[:, 96:104]
            cand = BIG[:, 12:14, :].rearrange("p a b -> p (a b)")
            oh = BIG[:, 14:16, :].rearrange("p a b -> p (a b)").rearrange("p (h k j) -> p h k j", h=8, k=16)
            dve.wait_ge(s["tk_iota"], 1)

            def top16(x, values, places):
                link(dve.max(values[:, 0:8], x))
                link(dve.max_index(places[:, 0:8], values[:, 0:8], x))
                link(dve.match_replace(x, values[:, 0:8], x, -3.0e38))
                link(dve.max(values[:, 8:16], x))
                link(dve.max_index(places[:, 8:16], values[:, 8:16], x))

            def top_keys(step):
                m, r = step // 16, step % 16
                if r < 8:
                    for f in (2 * r, 2 * r + 1):
                        top16(SC[:, m, f * P:(f + 1) * P], v16[:, f, :], i16[:, f, :])
                    return
                if r == 8:
                    link(dve.tensor_copy(WORK[:, 512:768], WORK[:, 256:512].bitcast(U32)))
                    link(dve.tensor_tensor(cand.rearrange("p (h a b) -> p h a b", h=8, a=16),
                                           v4[:, :, 0, :].unsqueeze(3).broadcast_to([P, 8, 16, 16]),
                                           v4[:, :, 1, :].unsqueeze(2).broadcast_to([P, 8, 16, 16]), ALU.add))
                if r < 12:
                    for h in (2 * (r - 8), 2 * (r - 8) + 1):
                        top16(cand[:, h * 256:(h + 1) * 256], s16[:, h, :], p16[:, h * 16:(h + 1) * 16])
                    return
                if r == 12:
                    dve.tensor_tensor(gate[:, m, :].rearrange("p (h k) -> p h k", k=16), s16,
                                      s16[:, :, 0:1].broadcast_to([P, 8, 16]), ALU.subtract).then_inc(s["tk_e"], 1)
                    link(dve.tensor_scalar(pa_u, p16, 4, None, ALU.logical_shift_right))
                    link(dve.tensor_scalar(pb_u, p16, 15, None, ALU.bitwise_and))
                    link(dve.tensor_copy(pa_f, pa_u))
                    link(dve.tensor_copy(pb_f, pb_u))
                f, part = (r - 12) // 2, (r - 12) % 2
                pf = (pa_f, pb_f)[f].rearrange("p (h k) -> p h k", k=16)
                if part == 0:
                    link(dve.tensor_tensor(oh, IOTA[:, 0:16].unsqueeze(1).unsqueeze(1).broadcast_to([P, 8, 16, 16]),
                                           pf.unsqueeze(3).broadcast_to([P, 8, 16, 16]), ALU.is_equal))
                else:
                    link(dve.tensor_tensor(oh, oh, if16[:, :, f, :].unsqueeze(2).broadcast_to([P, 8, 16, 16]), ALU.mult))
                    link(dve.tensor_reduce(SEL[:, m, f, :].rearrange("p (h k) -> p h k", k=16), oh, AX.X, ALU.add))

            def rows_low(n, j):
                for g in range(4):
                    dve.wait_ge(s["t_h"], 4 * n + g + 1)
                    sl = 4 * (j % 2) + g
                    dve.tensor_tensor(WL[:, sl, :], bank[4 + g][:, :], WH[:, sl, :].bitcast(F32), ALU.subtract)\
                        .then_inc(s["t_l"], 1)

            def one_hots(g, i, b, k):
                if not (isinstance(g, int) and g < 2):
                    dve.wait_ge(s["g_mm"], g - 1)
                t0 = TG * i
                dve.tensor_tensor(OH2[:, b, :, :], IOTA.unsqueeze(1).broadcast_to([P, TG, P]),
                                  TKT[:, 1, bass.ds(t0, TG)].unsqueeze(2).broadcast_to([P, TG, P]),
                                  ALU.is_equal).then_inc(s["oh2"], 1)
                dve.tensor_tensor(OH1[:, b, :, :], IOTA[:, QR * k:QR * (k + 1)].unsqueeze(1).broadcast_to([P, TG, QR]),
                                  TKT[:, 0, bass.ds(t0, TG)].unsqueeze(2).broadcast_to([P, TG, QR]),
                                  ALU.is_equal).then_inc(s["oh1"], 1)

            def gated(g, i, b, k):
                dve.wait_ge(s["g_mm"], g + 1)
                x = GB[k % 2][:, :, bass.ds(TG * i, TG)]
                dve.tensor_tensor(x, x, bank[2 + b][:, 0:TG * QR].rearrange("p (t i) -> p i t", t=TG), ALU.mult)\
                    .then_inc(s["g_mul"], 1)

            def p_low(n, j, k):
                dve.wait_ge(s["p_h"], n + 1)
                dve.tensor_tensor(PS[:, j % 2, 1, :], GB[k % 2][:, bass.ds(n - QR * k, 1), :].rearrange("p o t -> p (o t)"),
                                  PS[:, j % 2, 0, :].bitcast(F32), ALU.subtract).then_inc(s["p_l"], 1)

            def v_low(n, j):
                dve.wait_ge(s["v_h"], n + 1)
                sl = slice(4 * (j % 2), 4 * (j % 2) + 4)
                dve.tensor_tensor(WL[:, sl, :], RAW[:, j, :].rearrange("p (g n) -> p g n", g=4),
                                  WH[:, sl, :].bitcast(F32), ALU.subtract).then_inc(s["v_l"], 1)

            for seg, (kind, k) in enumerate(SEGMENTS):
                n0 = QR * k
                if kind == "in" and k == 0:
                    for n in range(QR):
                        rows_low(n, n % 4)
                        top_keys(n)
                    for m in range(MT):
                        dve.wait_ge(s["tk_g"], m + 1)
                        g3 = gate[:, m, :].rearrange("p (h k) -> p h k", k=16)
                        link(dve.tensor_reduce(gsum, g3, AX.X, ALU.add))
                        link(dve.reciprocal(gsum, gsum))
                        link(dve.tensor_tensor(g3, g3, gsum.unsqueeze(2).broadcast_to([P, 8, 16]), ALU.mult))
                        dve.sem_inc(s["tk_idx"], 1)
                    dve.wait_ge(s["tk_tc"], 6)
                    left = WORK[:, 512:768]
                    link(dve.tensor_copy(G3[:, 0, :], TKT[:, 2, :]))
                    link(dve.tensor_tensor(left, TKT[:, 2, :], G3[:, 0, :], ALU.subtract))
                    link(dve.tensor_copy(G3[:, 1, :], left))
                    link(dve.tensor_tensor(left, left, G3[:, 1, :], ALU.subtract))
                    link(dve.tensor_copy(G3[:, 2, :], left))
                    dve.sem_inc(s["tk_parts"], 1)
                    one_hots(0, 0, 0, 0)
                elif kind == "in":
                    g0 = QR * (k - 1)
                    dve.wait_ge(s["a_gelu"], g0 + QR)
                    for j in range(4):
                        rows_low(n0 + j, j)
                        if j >= 1:
                            gated(g0 + j - 1, j - 1, (j - 1) % 2, k - 1)
                        one_hots(g0 + j + 1, j + 1, (j + 1) % 2, k - 1)
                    with dve.Fori(1, QR // 4 - 1) as q:
                        for j in range(4):
                            rows_low(4 * q + (n0 + j), j)
                            gated(4 * q + (g0 + j - 1), 4 * q + (j - 1), (j + 1) % 2, k - 1)
                            one_hots(4 * q + (g0 + j + 1), 4 * q + (j + 1), (j + 1) % 2, k - 1)
                    for i in range(QR - 4, QR):
                        rows_low(n0 + i, i % 4)
                        gated(g0 + i - 1, i - 1, (i - 1) % 2, k - 1)
                        if i + 1 < QR:
                            one_hots(g0 + i + 1, i + 1, (i + 1) % 2, k - 1)
                        else:
                            one_hots(g0 + QR, 0, 0, k)
                    v_low(QR * SEGMENTS[seg + 1][1], 0)
                    gated(g0 + QR - 1, QR - 1, 1, k - 1)
                else:
                    if k == QUARTERS - 1:
                        dve.wait_ge(s["a_gelu"], n0 + QR)
                        one_hots(n0 + 1, 1, 1, k)
                        gated(n0, 0, 0, k)
                        with dve.Fori(0, QR // 2 - 1) as q:
                            for b in range(2):
                                one_hots(2 * q + (n0 + b + 2), 2 * q + (b + 2), b, k)
                                gated(2 * q + (n0 + b + 1), 2 * q + (b + 1), 1 - b, k)
                        gated(n0 + QR - 1, QR - 1, 1, k)
                        v_low(n0, 0)
                    with dve.Fori(0, QR // 4 - 1) as q:
                        for j in range(4):
                            p_low(4 * q + (n0 + j), j, k)
                            v_low(4 * q + (n0 + j + 1), (j + 1) % 4)
                    for j in range(4):
                        p_low(n0 + QR - 4 + j, j, k)
                        if j < 3:
                            v_low(n0 + QR - 3 + j, j + 1)
                    dve.wait_ge(s["o_mm"], n0 + QR)
                    for b in (4, 5, 6, 7, 0, 1, 2, 3):
                        x = XR[:, b // 4, (b % 4) * NW:(b % 4 + 1) * NW]
                        dve.tensor_tensor(x, x, bank[b][:, :], ALU.add).then_inc(s["o_add"], 1)

            dve.wait_ge(s["n_rstd"], 5)
            dve.wait_ge(s["lnf_in"], 16)
            for m in range(MT):
                dve.scalar_tensor_tensor(xn[:, m, :], XR[:, m, :], SM[:, 20 + m:21 + m],
                                         WORK[:, 0:2048], ALU.mult, ALU.mult)\
                    .then_inc(s["n_x"], 1)

        @block.tensor
        def _(pe):
            def mm(dst, lhsT, rhs, start, stop):
                return pe.matmul(dst, lhsT, rhs, start=start, stop=stop, skip_group_check=True)

            inputs = {"even_in": ("n_l", 0), "even_out": ("y_l", 0), "odd_in": ("n_l", 16), "odd_out": ("y_l", 16),
                      "two_in": ("n_l", 32), "two_out": ("y_l", 40), "peer_q": ("n_l", 48)}

            def tile(r, i, parity, first):
                t = r["base"] + i
                w = r["width"]
                toks = r["kind"] in ("tok", "res", "gate")
                for sub in range(8):
                    beside(8 * t + sub)
                    if sub == 0 and (r["base"] >= 2 or i >= 2):
                        pe.wait_ge(s["tile_free"], t - 1)
                    if first and (r["base"] == 0 or RUNS[[x["base"] for x in RUNS].index(r["base"]) - 1]["phase"] != r["phase"]):
                        name, before = inputs[r["phase"]]
                        pe.wait_ge(s[name], before + min(2 * sub + 2, 48 - before if name == "y_l" else 16))
                    pe.wait_ge(s["wl_done"], 8 * t + sub + 1)
                    for kk in range(2):
                        kt = 2 * sub + kk
                        sl = 2 * (sub % 4) + kk
                        last = kt == KT - 1
                        if toks:
                            for m in range(MT):
                                ms = slice(m * P, (m + 1) * P)
                                dst = bank[2 * parity + m][:, 0:w]
                                mm(dst, HH[:, kt, ms], WH[:, sl, 0:w], kt == 0, False)
                                mm(dst, HL[:, kt, ms], WH[:, sl, 0:w], False, False)
                                ins = mm(dst, HH[:, kt, ms], WL[:, sl, 0:w], False, last)
                        else:
                            for c in range(4):
                                cs = slice(c * P, (c + 1) * P)
                                dst = bank[2 * parity + c // 2][:, (c % 2) * T:(c % 2 + 1) * T]
                                mm(dst, WH[:, sl, cs], HH[:, kt, :], kt == 0 and c % 2 == 0, False)
                                mm(dst, WH[:, sl, cs], HL[:, kt, :], False, False)
                                ins = mm(dst, WL[:, sl, cs], HH[:, kt, :], False, last)
                    ins.then_inc(s["ws_used"], 1)

            xn = BIG[:, 0:4, :].rearrange("p (m a) b -> p m (a b)", m=2)

            def norm_t(n):
                pe.wait_ge(s["n_x"], 2 * n + 2)
                for g in range(8):
                    if g >= 4:
                        pe.wait_ge(s["n_l"], 16 * n + 2 * (g - 3))
                    for kk in range(2):
                        for m in range(MT):
                            c0 = (2 * g + kk) * P
                            ins = pe.transpose(bank[4 + g % 4][:, kk * T + m * P:kk * T + (m + 1) * P],
                                               xn[:, m, c0:c0 + P], ID[:, :])
                    ins.then_inc(s["n_t"], 1)

            def phase(name):
                over_tiles(pe, name, tile)
                pe.wait_ge(s["tile_free"], last_tile(name) + 1)

            q_t = BIG[:, 0:2, :].rearrange("p a b -> p (a b)")
            kd = WORK[:, 3584:4096].rearrange("p (m g c) -> p m g c", m=2, g=2)
            qT = WORK[:, 0:2048].rearrange("p (k t) -> p k t", k=8)
            kT = WORK[:, 2048:2560].rearrange("p (k t) -> p k t", k=2)
            lg = WORK[:, 0:768].rearrange("p (b c) -> p b c", b=2)

            def a_turn(g):
                if g == 4:
                    pe.wait_ge(s["qk_c"], 1)
                for kk in range(2):
                    for m in range(MT):
                        if g < 4:
                            pair = 2 * g + kk
                            o = (pair // 4) * 1024 + m * 512 + (pair % 4) * P
                            src = q_t[:, o:o + P]
                        else:
                            src = kd[:, m, kk, :]
                        ins = pe.transpose(bank[4 + g % 4][:, kk * T + m * P:kk * T + (m + 1) * P], src, ID[:, :])
                ins.then_inc(s["qk_t"], 1)

            def attend_step(p, i, score, probs, pt, value, c0):
                if i < 16:
                    h = i
                    if h >= 2:
                        pe.wait_ge(s[p + "soft"], h - 1)
                    score(h, bank[4 + h % 2]).then_inc(s[p + "score"], 1)
                if 2 <= i <= 17:
                    h = i - 2
                    pe.wait_ge(s[p + "pn"], h + 1)
                    if h >= 1:
                        pe.wait_ge(s[p + "ptc"], h)
                    for b in range(3):
                        ins = pe.transpose(bank[6][:, b * P:(b + 1) * P], probs[:, h % 2, b * P:(b + 1) * P],
                                           ID[:, :])
                    ins.then_inc(s[p + "pt"], 1)
                if i >= 3:
                    h = i - 3
                    j = h // 2
                    pe.wait_ge(s[p + "ptc"], h + 1)
                    if h % 2 == 0 and j >= 1:
                        pe.wait_ge(s["y_ready"], c0 + j)
                    o = bank[7][64 * (h % 2):64 * (h % 2) + 64, :]
                    mm(o[:, 0:T], value(h, 0), pt[:, h % 2, 0:T], True, False)
                    mm(o[:, P:T], value(h, 1), pt[:, h % 2, T:384], False, True).then_inc(s[p + "pv"], 1)

            def a_score(h, ps):
                r = slice(64 * (h % 2), 64 * (h % 2) + 64)
                q, k = qT[r, h // 2, :], kT[r, h // 8, :]
                if h == 0:
                    pe.wait_ge(s["qk_c"], 5)
                mm(ps[:, 0:P], q[:, 0:P], k[:, 0:P], True, True)
                return mm(ps[:, P:384], q[:, P:T], k[:, 0:T], True, True)

            def a_value(h, m):
                o = m * 512 + P + 64 * (h // 8)
                return BIG[:, 2, o:o + 64]

            def f_score(h, ps):
                r = slice(64 * (h % 2), 64 * (h % 2) + 64)
                q, k = chan(5, h // 2)[r, :], chan(7, h // 2)[r, :]
                g = lg[:, h % 2, :]
                if h == 0:
                    pe.wait_ge(s["tile_free"], TWO_TILE + 5)
                pe.wait_ge(s["f_lg"], h + 1)
                mm(ps[:, 0:P], q[:, 0:P], k[:, 0:P], True, False)
                mm(ps[:, P:384], q[:, P:T], k, False, False)
                mm(ps[:, 0:P], LE[:, :], g[:, 0:P], False, False)
                mm(ps[:, P:T], ONES[:, :], g[:, 0:P], False, False)
                return mm(ps[:, P:384], LE[:, :], g[:, P:384], False, True)

            def f_value(h, m):
                if h % 8 == 0 and m == 0:
                    pe.wait_ge(s["tile_free"], TWO_TILE + 6 + h // 8)
                o = m * 512 + (h % 8) * 64
                return BIG[:, 9 + h // 8, o:o + 64]

            def c_value(h, m):
                return BIG[:, 8 + h // 4, m * 512 + (h % 4) * P:m * 512 + (h % 4 + 1) * P]

            def stick_step(i):
                if i < C_HEADS:
                    h = i
                    ps = bank[4 + h % 2]
                    q, k = chan(0, h), chan(4, h)
                    if h == 0:
                        pe.wait_ge(s["tile_free"], ODD_TILE + 8)
                    if h >= 2:
                        pe.wait_ge(s["c_min"], h - 1)
                    mm(ps[:, 0:T], k[:, 0:P], q, True, True)
                    mm(ps[:, T:384], k[:, P:T], q[:, P:T], False, True).then_inc(s["c_z"], 1)
                if 1 <= i <= C_HEADS:
                    h = i - 1
                    ps = bank[4 + h % 2]
                    sp_ = C_SP[:, h % 2, :]
                    pe.wait_ge(s["c_sp"], 2 * (h + 1))
                    mm(ps[:, 0:384], NTRI[:, :], sp_, False, True)
                    mm(ps[:, P:T], NONES[:, :], sp_[:, T:384], False, True).then_inc(s["c_e"], 1)
                if i >= 3:
                    h = i - 3
                    pe.wait_ge(s["c_w"], h + 1)
                    if h % 4 == 0:
                        pe.wait_ge(s["tile_free"], ODD_TILE + 9 + h // 4)
                    if h >= 2:
                        pe.wait_ge(s["c_out"], h - 1)
                    o = bank[6 + h % 2]
                    w = C_W[:, h % 2, :]
                    mm(o[:, 0:T], c_value(h, 0), w[:, 0:T], True, False)
                    mm(o[:, P:T], c_value(h, 1), w[:, T:384], False, True).then_inc(s["c_pv"], 1)

            def beside(place):
                i = step_at(place, C_FIRST, 3, C_STEPS)
                if i is not None:
                    stick_step(i)
                if place == A_TURN:
                    pe.wait_ge(s["masks"], 2)
                    pe.wait_ge(s["aq_ready"], 3)
                    for g in range(4):
                        a_turn(g)
                if place == A_TURN + 1:
                    a_turn(4)
                i = step_at(place, A_FIRST, 2, ATTEND_STEPS)
                if i is not None:
                    attend_step("a_", i, a_score, A_PROBS, A_PT, a_value, 0)
                i = step_at(place, F_FIRST, 2, ATTEND_STEPS)
                if i is not None:
                    attend_step("f_", i, f_score, F_PROBS, F_PT, f_value, 32)

            pe.wait_ge(s["masks"], 1)
            pe.wait_ge(s["vec_in"], 16 * N_VEC)
            pe.transpose(bank[0][:, 0:V_ROWS], WORK[0:V_ROWS, 0:P], ID[0:V_ROWS, 0:V_ROWS])
            pe.transpose(bank[0][:, V_ROWS:V_ROWS + 48], WORK[0:48, P:2 * P], ID[0:48, 0:48]).then_inc(s["vec_t"], 1)
            pe.wait_ge(s["cols_set"], 1)
            norm_t(0)
            phase("even_in")

            lgf = BIG[:, 0:2, :].rearrange("p a b -> p (a b)")
            msf = MS.rearrange("p l i -> p (l i)")
            qe = WORK[:, 1024:2048].rearrange("p (l i) -> p l i", l=8)
            ke = WORK[:, 2048:3072].rearrange("p (l i) -> p l i", l=8)
            am = WORK[:, 3072:4096].rearrange("p (l i) -> p l i", l=8)
            pe.wait_ge(s["b_x"], 2)
            pe.wait_ge(s["y_ready"], 8)

            def level_sums(u):
                h, m = u // 2, u % 2
                if u >= 1:
                    pe.wait_ge(s["b_lf"], u)
                pe.transpose(bank[4][:, m * P:(m + 1) * P], lgf[:, h * T + m * P:h * T + (m + 1) * P], ID[:, :])\
                    .then_inc(s["b_lt"], 1)
                pe.wait_ge(s["b_lf"], u + 1)
                if u >= 1:
                    pe.wait_ge(s["b_ex"], u)
                mm(bank[0][:, :], LFT[:, m, :], msf[:, 0:512], True, True)
                mm(bank[1][:, 0:384], LFT[:, m, :], msf[:, 512:896], True, True)
                mm(bank[1][:, 384:512], LFT[:, m, :], (GT if m == 0 else LE)[:, :], True, True)\
                    .then_inc(s["b_es"], 1)

            def values(u):
                h, m = u // 2, u % 2
                ts = slice(m * P, (m + 1) * P)
                o = bank[5 + 2 * (h % 2)]
                pe.wait_ge(s["b_am"], u + 1)
                if m == 0 and h >= 2:
                    pe.wait_ge(s["y_ready"], 8 + h - 1)
                v = BIG[:, 9 + h // 4, m * 512 + (h % 4) * P:m * 512 + (h % 4 + 1) * P]
                for l in range(8):
                    ins = mm(o[:, ts], v, am[:, l, :], l == 0, l == 7 and m == 0)
                ins.then_inc(s["b_lev"], 1)
                if m == 1:
                    pe.wait_ge(s["b_cx"], h + 1)
                    v0 = BIG[:, 9 + h // 4, (h % 4) * P:(h % 4 + 1) * P]
                    mm(o[:, ts], v0, CX, False, True).then_inc(s["b_ov"], 1)

            def products(u):
                h, m = u // 2, u % 2
                ts = slice(m * P, (m + 1) * P)
                pe.wait_ge(s["b_qe"], u + 1)
                pe.wait_ge(s["b_ke"], u + 1)
                if u >= 1:
                    pe.wait_ge(s["b_am"], u)
                for l in range(8):
                    dst = bank[2 + l // 4][:, (l % 4) * P:(l % 4 + 1) * P]
                    if l < LEVELS:
                        ins = mm(dst, ke[:, l, :], qe[:, l, :], True, True)
                    else:
                        ins = mm(dst, chan(7, h)[:, ts], chan(5, h)[:, ts], True, True)
                ins.then_inc(s["b_att"], 1)
                if m == 1:
                    pe.wait_ge(s["b_kx"], h + 1)
                    if h >= 1:
                        pe.wait_ge(s["b_cx"], h)
                    mm(bank[6][:, 0:P], KX, qe[:, 7, :], True, True).then_inc(s["b_cross"], 1)

            def square_sums(h):
                pe.wait_ge(s["b_sq"], h + 1)
                if h >= 1:
                    pe.wait_ge(s["b_rs"], h)
                mm(bank[5 + 2 * (h % 2)][:, T:2 * T], ONES[:, :], BSQ, True, True).then_inc(s["b_ss"], 1)

            for i in range(2 * B_HEADS + 4):
                if i < 2 * B_HEADS:
                    level_sums(i)
                if 0 <= i - 2 < 2 * B_HEADS:
                    values(i - 2)
                if 0 <= i - 1 < 2 * B_HEADS:
                    products(i - 1)
                if i >= 4 and i % 2 == 0:
                    square_sums((i - 4) // 2)
            phase("even_out")

            norm_t(1)
            phase("odd_in")
            phase("odd_out")

            norm_t(2)
            phase("two_in")
            XBC = BIG[:, 11:14, :].rearrange("p a b -> p (a b)")
            pe.wait_ge(s["s_xbc"], 3)
            for g in range(4):
                m, hh = g // 2, g % 2
                if g >= 2:
                    pe.wait_ge(s["s_xd"], g - 1)
                for j in range(4):
                    k = 4 * hh + j
                    ins = pe.transpose(bank[g % 2][:, j * P:(j + 1) * P],
                                       XBC[:, k * T + m * P:k * T + (m + 1) * P], ID[:, :])
                ins.then_inc(s["s_xt"], 1)
            for g in range(2):
                B, C = XBC[:, (8 + g) * T:(9 + g) * T], XBC[:, (10 + g) * T:(11 + g) * T]
                mm(bank[2 + g][:, 0:T], B[:, 0:P], C, True, True)
                mm(bank[2 + g][:, T:384], B[:, P:T], C[:, P:T], False, True).then_inc(s["s_cb"], 1)
            XD = BIG[:, 14:16, :].rearrange("p a b -> p (a b)").rearrange("p (m h d) -> p m h d", m=2, h=16)
            ag = WORK[:, 0:768].rearrange("p (b c) -> p b c", b=2)
            sL = WORK[:, 1792:2560].rearrange("p (b c) -> p b c", b=2)
            pe.wait_ge(s["s_xd"], 4)
            for i in range(S_HEADS + 1):
                if i < S_HEADS:
                    h = i
                    g = ag[:, h % 2, :]
                    ps = bank[4 + h % 2]
                    pe.wait_ge(s["s_ag"], h + 1)
                    if h >= 2:
                        pe.wait_ge(s["s_ex"], h - 1)
                    mm(ps[:, 0:P], g[:, 0:P], LE[:, :], True, False)
                    mm(ps[:, P:T], g[:, 0:P], ONES[:, :], False, False)
                    mm(ps[:, P:T], g[:, P:T], LE[:, :], False, False)
                    mm(ps[:, T:384], g[:, T:384], LE[:, :], False, True).then_inc(s["s_seg"], 1)
                if i >= 1:
                    h = i - 1
                    j = h // 2
                    pe.wait_ge(s["s_l"], h + 1)
                    if j >= 2:
                        pe.wait_ge(s["s_yg"], j - 1)
                    o = bank[j % 2][64 * (h % 2):64 * (h % 2) + 64, :]
                    mm(o[:, 0:T], XD[:, 0, h, :], sL[:, h % 2, 0:T], True, False)
                    mm(o[:, P:T], XD[:, 1, h, :], sL[:, h % 2, T:384], False, True).then_inc(s["s_y"], 1)
            SQ = WORK[:, 768:1792].rearrange("p (j t) -> p j t", j=4)
            for g in range(2):
                pe.wait_ge(s["s_sq"], g + 1)
                if g == 1:
                    pe.wait_ge(s["s_rs"], 1)
                for j in range(4):
                    ins = mm(bank[6][:, 0:T], ONES[:, :], SQ[:, j, :], j == 0, j == 3)
                ins.then_inc(s["s_ss"], 1)

            phase("two_out")

            norm_t(3)
            phase("peer_q")
            keys = RAW[:, 0, :].rearrange("p (f d) -> p f d", f=16)
            kTp = BIG[:, 4:6, :].rearrange("p a b -> p (a b)").rearrange("p (f d) -> p f d", f=16)
            pe.wait_ge(s["k_in"], 32)
            for g in range(4):
                for j in range(4):
                    ins = pe.transpose(bank[4 + g][:, j * P:(j + 1) * P], keys[:, 4 * g + j, :], ID[:, :])
                ins.then_inc(s["k_t"], 1)
            pe.wait_ge(s["k_c"], 4)
            for g in range(8):
                m = g // 4
                if g >= 4:
                    pe.wait_ge(s["q_sc"], g - 3)
                for j in range(4):
                    f = 4 * (g % 4) + j
                    ins = mm(bank[g % 4][:, j * P:(j + 1) * P], chan(0, f)[:, m * P:(m + 1) * P], kTp[:, f, :],
                             True, True)
                ins.then_inc(s["q_s"], 1)
            gate = WORK[:, 1024:1280].rearrange("p (m n) -> p m n", m=2)

            def turn(n, j, g, full, fresh):
                if g == 0:
                    pe.wait_ge(s[f"row_full{j}"], full)
                if not fresh:
                    pe.wait_ge(s["t_l"], 4 * n + (g - 3))
                for b in range(4):
                    c0 = (4 * g + b) * P
                    ins = pe.transpose(bank[4 + g][:, b * P:(b + 1) * P], RAW[:, j, c0:c0 + P], ID[:, :])
                ins.then_inc(s["t_t"], 1)

            def products(n, j, g, fresh):
                if g == 0 and not fresh:
                    pe.wait_ge(s["a_gelu"], n - 1)
                pe.wait_ge(s["t_l"], 4 * n + g + 1)
                for b in range(4):
                    kt = 4 * g + b
                    sl, cs = 4 * (j % 2) + g, slice(b * P, (b + 1) * P)
                    dst = bank[j % 2][:, 0:T]
                    mm(dst, WH[:, sl, cs], HH[:, kt, :], kt == 0, False)
                    mm(dst, WH[:, sl, cs], HL[:, kt, :], False, False)
                    ins = mm(dst, WL[:, sl, cs], HH[:, kt, :], False, kt == KT - 1)
                ins.then_inc(s["u_used"], 1)

            def spread(g, b, fresh):
                pe.wait_ge(s["oh2"], g + 1)
                pe.wait_ge(s["ohg"], g + 1)
                if not fresh:
                    pe.wait_ge(s["g_mul"], g - 1)
                for t in range(TG):
                    for c in range(3):
                        ins = mm(bank[2 + b][:, t * QR:(t + 1) * QR], OH2[:, b, t, :], OHG[:, b, c, t, :],
                                 c == 0, c == 2)
                ins.then_inc(s["g_mm"], 1)

            def outputs(n, j, start):
                pe.wait_ge(s["p_l"], n + 1)
                pe.wait_ge(s["v_l"], n + 1)
                for m in range(MT):
                    ms = slice(m * P, (m + 1) * P)
                    for nn in range(4):
                        sl = 4 * (j % 2) + nn
                        dst = bank[4 * m + nn][:, :]
                        mm(dst, PS[:, j % 2, 0, ms], WH[:, sl, :], start, False)
                        mm(dst, PS[:, j % 2, 1, ms], WH[:, sl, :], False, False)
                        ins = mm(dst, PS[:, j % 2, 0, ms], WL[:, sl, :], False, False)
                ins.then_inc(s["o_mm"], 1)

            for seg, (kind, k) in enumerate(SEGMENTS):
                n0 = QR * k
                full = (QR // 4) * seg
                g0 = QR * (k - 1)
                after_out = seg > 0 and SEGMENTS[seg - 1][0] == "out"
                added = 8 * (SEGMENTS[seg - 1][1]) if after_out else 0
                if kind == "in":
                    if k == 1:
                        for m in range(MT):
                            pe.wait_ge(s["tk_idx"], m + 1)
                            for f in range(3):
                                n = 3 * m + f
                                if n >= 2:
                                    pe.wait_ge(s["tk_tc"], n - 1)
                                src = SEL[:, m, f, :] if f < 2 else gate[:, m, :]
                                pe.transpose(bank[2 + n % 2][:, 0:P], src, ID[:, :]).then_inc(s["tk_t"], 1)
                        pe.wait_ge(s["tk_tc"], 6)
                    for j in range(4):
                        for g in range(4):
                            if after_out and j == 0:
                                pe.wait_ge(s["o_add"], added + g + 1)
                            turn(n0 + j, j, g, 16 * (full + 1), seg == 0 and j == 0)
                            if j >= 1:
                                if after_out and g == 0 and j <= 2:
                                    pe.wait_ge(s["o_add"], added + 4 + j)
                                products(n0 + j - 1, j - 1, g, seg == 0 and j <= 2)
                        if k >= 1:
                            if after_out and j < 2:
                                pe.wait_ge(s["o_add"], added + 7 + j)
                            spread(g0 + j, j % 2, k == 1 and j < 2)
                    with pe.Fori(1, QR // 4) as q:
                        for j in range(4):
                            for g in range(4):
                                turn(4 * q + (n0 + j), j, g, 16 * q + 16 * (full + 1), False)
                                products(4 * q + (n0 + j - 1), (j + 3) % 4, g, False)
                            if k >= 1:
                                spread(4 * q + (g0 + j), j % 2, False)
                    for g in range(4):
                        products(n0 + QR - 1, 3, g, False)
                else:
                    if k == QUARTERS - 1:
                        pe.wait_ge(s["o_add"], 8 * k)
                        for b in range(2):
                            spread(n0 + b, b, False)
                        with pe.Fori(1, QR // 2) as q:
                            for b in range(2):
                                spread(2 * q + (n0 + b), b, False)
                    u_tiles = QR * (1 + max(kk for kd, kk in SEGMENTS[:seg] if kd == "in"))
                    pe.wait_ge(s["a_gelu"], u_tiles)
                    pe.wait_ge(s["g_mul"], n0 + QR)
                    for j in range(4):
                        outputs(n0 + j, j, j == 0)
                    with pe.Fori(1, QR // 4) as q:
                        for j in range(4):
                            outputs(4 * q + (n0 + j), j, False)


_INS = ["x", "ln_even", "w_in_even", "q_norm_a", "k_norm_a", "sinks_a", "lower_bounds", "g_norm_b",
        "w_out_even", "ln_odd", "w_in_odd", "w_out_odd", "ln1_w_2", "w_in_2", "conv_w_2", "conv_b_2",
        "dt_bias_2", "a_log_2", "d_skip_2", "ssd_norm_w_2", "fox_f_bias_2", "w_out_2", "ln2_w_2",
        "peer_wq_2", "peer_k1_2", "peer_k2_2", "peer_u_2", "peer_v_2", "lnf_w_2"]
_LAYERED = ("w_in_even", "w_out_even", "w_in_odd", "w_out_odd")


def rope_tables():
    half = A_HD // 2
    inv = (1.0 / (np.float32(10000.0) ** (np.arange(half, dtype=np.float32) / np.float32(half)))).astype(np.float32)
    ang = np.arange(T, dtype=np.float32)[:, None] * inv[None, :]
    return np.cos(ang), np.sin(ang)


def kernel(**inputs):
    import concourse.bacc as _bacc
    from concourse.bass_utils import run_bass_kernel_spmd as _run

    nc = _bacc.Bacc("TRN2", target_bir_lowering=False, num_devices=1)
    arrays, args = {}, {}
    cos, sin = rope_tables()
    for name in _INS + ["rope_cos", "rope_sin"]:
        v = cos if name == "rope_cos" else sin if name == "rope_sin" else np.ascontiguousarray(inputs[name])
        arrays[f"in_{name}_dram"] = v
        ap = nc.dram_tensor(f"in_{name}_dram", v.shape, mybir.dt.from_np(v.dtype), kind="ExternalInput").ap()
        args[name] = ap[0] if name in _LAYERED else ap
    out = nc.dram_tensor("out_0_dram", (1, T, D), F32, kind="ExternalOutput").ap()
    two_blocks(nc, args, out)
    r = _run(nc, [arrays], core_ids=[0])
    return r.results[0]["out_0_dram"]
```
